# Optimizing a Trainium2 kernel written in Bass

```python
import jax, jax.numpy as jnp
from jax import lax
import numpy as np
import math

D_MODEL = 1024
BATCH = 1
SEQ = 512
DEPTH = 1

CTX_LEN = 256
GRID_W = 64
NORM_EPS = 1e-6
SGU_WIDTH = 1024
SGU_GROUPS = 8
SGU_GROUP_DIM = SGU_WIDTH // SGU_GROUPS
CHUNK = 128
TINY_DIM = 64
ATTN_BLOCK = 128
ROPE_BASE = 10000.0
NA_HEADS = 16
NA_HEAD_DIM = 32
NA_WIDTH = NA_HEADS * NA_HEAD_DIM
NA_ROWS = 8
NA_COLS = 16
N_EXPERTS = 64
TOP_K = 8
EXPERT_FF = 256
SHARED_FF = 256
ROUTE_SCALE = 2.5
EXPERT_BLOCK = 128
COL_U = 0
COL_V = COL_U + SGU_WIDTH
COL_TQ = COL_V + SGU_WIDTH
COL_TK = COL_TQ + TINY_DIM
COL_TV = COL_TK + TINY_DIM
COL_NQ = COL_TV + TINY_DIM
COL_NK = COL_NQ + NA_WIDTH
COL_NV = COL_NK + NA_WIDTH
COL_GA = COL_NV + NA_WIDTH
COL_GB = COL_GA + D_MODEL
IN_WIDTH = COL_GB + D_MODEL


def rms_norm(x, g):
    xf = x.astype(jnp.float32)
    y = xf * lax.rsqrt(jnp.mean(xf * xf, -1, keepdims=True) + NORM_EPS)
    return (y * g.astype(jnp.float32)).astype(x.dtype)

def layer_norm(x, g, b):
    xf = x.astype(jnp.float32)
    mu = jnp.mean(xf, -1, keepdims=True)
    var = jnp.mean(jnp.square(xf - mu), -1, keepdims=True)
    y = (xf - mu) * lax.rsqrt(var + NORM_EPS) * g.astype(jnp.float32) + b.astype(jnp.float32)
    return y.astype(x.dtype)

def modulate(h, shift, scale):
    return h * (1 + scale) + shift

def swiglu(x, wg, wu, wd):
    return (jax.nn.silu(x @ wg) * (x @ wu)) @ wd

def axial_rope(x, n_tokens):
    dh = x.shape[-1]
    quarter = dh // 4
    t = jnp.arange(n_tokens)
    pos = jnp.stack([t // GRID_W, t % GRID_W], -1).astype(jnp.float32)
    inv_freq = ROPE_BASE ** (-jnp.arange(quarter, dtype=jnp.float32) / quarter)
    ang = pos[:, :, None] * inv_freq
    cos, sin = jnp.cos(ang), jnp.sin(ang)
    xf = x.astype(jnp.float32).reshape(x.shape[:-1] + (2, 2, quarter))
    x1, x2 = xf[..., 0, :], xf[..., 1, :]
    out = jnp.stack([x1 * cos - x2 * sin, x2 * cos + x1 * sin], -2)
    return out.reshape(x.shape).astype(x.dtype)

def tiny_attention(q, k_lat, v_lat, k_ctx, v_ctx):
    b, s, t = q.shape
    k_all = jnp.concatenate([k_lat, k_ctx], 1)
    v_all = jnp.concatenate([v_lat, v_ctx], 1)
    q_blocks = q.reshape(b, s // ATTN_BLOCK, ATTN_BLOCK, t).transpose(1, 0, 2, 3)
    scale = t ** -0.5

    def one_block(qb):
        sc = jnp.einsum("bqt,bkt->bqk", qb, k_all, preferred_element_type=jnp.float32) * scale
        p = jax.nn.softmax(sc, -1).astype(v_all.dtype)
        return jnp.einsum("bqk,bkt->bqt", p, v_all)

    out = lax.map(one_block, q_blocks)
    return out.transpose(1, 0, 2, 3).reshape(b, s, t)

def spatial_gating(u, v, tiny, ln_g, ln_b, w_s, b_s):
    b, s, _ = v.shape
    vn = layer_norm(v, ln_g, ln_b).reshape(b, s // CHUNK, CHUNK, SGU_GROUPS, SGU_GROUP_DIM)
    mixed = jnp.einsum("gpq,bnqgc->bnpgc", w_s, vn) + b_s.T[:, :, None]
    return u * (mixed.reshape(b, s, SGU_WIDTH) + tiny)

def neighbourhood_attention(q, k, v, k_ctx, v_ctx, rpb, rows):
    b, s, h, dh = q.shape
    kh = min(NA_ROWS, rows)
    qg = q.reshape(b, rows, GRID_W, h, dh)
    kg = k.reshape(b, rows, GRID_W, h, dh)
    vg = v.reshape(b, rows, GRID_W, h, dh)
    cq = np.arange(GRID_W)
    c_start = np.clip(cq - NA_COLS // 2, 0, GRID_W - NA_COLS)
    col_mask = (cq[None, :] >= c_start[:, None]) & (cq[None, :] < c_start[:, None] + NA_COLS)
    band_mask = np.broadcast_to(col_mask[:, None, :], (GRID_W, kh, GRID_W)).reshape(GRID_W, kh * GRID_W)
    dc_idx = np.clip(cq[None, :] - cq[:, None], -(NA_COLS - 1), NA_COLS - 1) + NA_COLS - 1
    col_bias = rpb[:, :, dc_idx]
    scale = dh ** -0.5

    def one_row(r):
        r_start = jnp.clip(r - kh // 2, 0, rows - kh)
        qb = lax.dynamic_index_in_dim(qg, r, axis=1, keepdims=False)
        kb = lax.dynamic_slice_in_dim(kg, r_start, kh, axis=1).reshape(b, kh * GRID_W, h, dh)
        vb = lax.dynamic_slice_in_dim(vg, r_start, kh, axis=1).reshape(b, kh * GRID_W, h, dh)
        dr = r_start + jnp.arange(kh) - r + NA_ROWS - 1
        bias = jnp.take(col_bias, dr, axis=1).transpose(0, 2, 1, 3).reshape(h, GRID_W, kh * GRID_W)
        s_lat = jnp.einsum("bqhd,bkhd->bhqk", qb, kb, preferred_element_type=jnp.float32) * scale + bias
        s_lat = jnp.where(band_mask, s_lat, -jnp.inf)
        s_ctx = jnp.einsum("bqhd,bkhd->bhqk", qb, k_ctx, preferred_element_type=jnp.float32) * scale
        p = jax.nn.softmax(jnp.concatenate([s_lat, s_ctx], -1), -1).astype(v.dtype)
        n_lat = kh * GRID_W
        return (jnp.einsum("bhqk,bkhd->bqhd", p[..., :n_lat], vb)
                + jnp.einsum("bhqk,bkhd->bqhd", p[..., n_lat:], v_ctx))

    out = lax.map(one_row, jnp.arange(rows))
    return out.transpose(1, 0, 2, 3, 4).reshape(b, s, h * dh)

def moe_ffn(h, w_router, b_router, w_e_gate, w_e_up, w_e_down, w_sh_gate, w_sh_up, w_sh_down):
    n, d = h.shape
    scores = jax.nn.sigmoid(jnp.matmul(h, w_router, preferred_element_type=jnp.float32))
    _, idx = lax.top_k(scores + b_router.astype(jnp.float32), TOP_K)
    wts = jnp.take_along_axis(scores, idx, axis=-1)
    wts = (wts / jnp.sum(wts, -1, keepdims=True) * ROUTE_SCALE).astype(h.dtype)
    n_assign = n * TOP_K
    flat_e = idx.reshape(-1)
    flat_tok = jnp.repeat(jnp.arange(n, dtype=jnp.int32), TOP_K)
    flat_w = wts.reshape(-1)
    order = jnp.argsort(flat_e)
    se, st, sw = flat_e[order], flat_tok[order], flat_w[order]
    counts = jnp.bincount(flat_e, length=N_EXPERTS)
    starts = jnp.cumsum(counts) - counts
    pad_counts = (counts + EXPERT_BLOCK - 1) // EXPERT_BLOCK * EXPERT_BLOCK
    pad_ends = jnp.cumsum(pad_counts)
    pad_starts = pad_ends - pad_counts
    dest = pad_starts[se] + jnp.arange(n_assign) - starts[se]
    n_blocks = -(-n_assign // EXPERT_BLOCK) + N_EXPERTS
    n_rows = n_blocks * EXPERT_BLOCK
    row_tok = jnp.full((n_rows,), n, jnp.int32).at[dest].set(st)
    row_w = jnp.zeros((n_rows,), h.dtype).at[dest].set(sw)
    block_e = jnp.minimum(jnp.searchsorted(pad_ends, jnp.arange(n_blocks) * EXPERT_BLOCK, side="right"),
                          N_EXPERTS - 1)
    h_pad = jnp.concatenate([h, jnp.zeros((1, d), h.dtype)], 0)

    def expert_block(acc, blk):
        tok, wt, e = blk
        yb = swiglu(h_pad[tok], w_e_gate[e], w_e_up[e], w_e_down[e]) * wt[:, None]
        return acc.at[tok].add(yb), None

    routed, _ = lax.scan(expert_block, jnp.zeros((n + 1, d), h.dtype),
                         (row_tok.reshape(n_blocks, EXPERT_BLOCK), row_w.reshape(n_blocks, EXPERT_BLOCK), block_e))
    return swiglu(h, w_sh_gate, w_sh_up, w_sh_down) + routed[:n]

def hybrid_layer(x, c, ctx, c_ctx, w_ada, b_ada, norm_mix_g, norm_ffn_g, w_in, b_in,
                 sgu_ln_g, sgu_ln_b, sgu_w_s, sgu_b_s, tiny_w_o, na_rpb, w_up_a, w_up_b, w_out,
                 w_router, b_router, w_e_gate, w_e_up, w_e_down, w_sh_gate, w_sh_up, w_sh_down):
    b, s, d = x.shape
    rows = s // GRID_W
    ctx_len = ctx.shape[1]
    mod = (jax.nn.silu(c) @ w_ada + b_ada)[:, None, :]
    sh_mix, sc_mix, g_mix, sh_ffn, sc_ffn, g_ffn = jnp.split(mod, 6, -1)
    mod_ctx = jax.nn.silu(c_ctx) @ w_ada[:, :2 * d] + b_ada[:2 * d]

    h = modulate(rms_norm(x, norm_mix_g), sh_mix, sc_mix)
    p_in = h @ w_in + b_in
    u = jax.nn.gelu(p_in[..., COL_U:COL_V], approximate=False)
    v = jax.nn.gelu(p_in[..., COL_V:COL_TQ], approximate=False)
    tq = axial_rope(p_in[..., COL_TQ:COL_TK], s)
    tk = axial_rope(p_in[..., COL_TK:COL_TV], s)
    tv = p_in[..., COL_TV:COL_NQ]
    nq = p_in[..., COL_NQ:COL_NK].reshape(b, s, NA_HEADS, NA_HEAD_DIM)
    nk = p_in[..., COL_NK:COL_NV].reshape(b, s, NA_HEADS, NA_HEAD_DIM)
    nv = p_in[..., COL_NV:COL_GA].reshape(b, s, NA_HEADS, NA_HEAD_DIM)
    gate_a = jax.nn.sigmoid(p_in[..., COL_GA:COL_GB])
    gate_b = jax.nn.sigmoid(p_in[..., COL_GB:IN_WIDTH])

    hc = modulate(rms_norm(ctx, norm_mix_g), mod_ctx[:d], mod_ctx[d:])
    c_tiny = hc @ w_in[:, COL_TK:COL_NQ] + b_in[COL_TK:COL_NQ]
    tk_c, tv_c = c_tiny[..., :TINY_DIM], c_tiny[..., TINY_DIM:]
    c_na = hc @ w_in[:, COL_NK:COL_GA] + b_in[COL_NK:COL_GA]
    nk_c = c_na[..., :NA_WIDTH].reshape(b, ctx_len, NA_HEADS, NA_HEAD_DIM)
    nv_c = c_na[..., NA_WIDTH:].reshape(b, ctx_len, NA_HEADS, NA_HEAD_DIM)

    tiny = tiny_attention(tq, tk, tv, tk_c, tv_c) @ tiny_w_o
    o_a = spatial_gating(u, v, tiny, sgu_ln_g, sgu_ln_b, sgu_w_s, sgu_b_s)
    o_b = neighbourhood_attention(nq, nk, nv, nk_c, nv_c, na_rpb, rows)

    merged = gate_a * (o_a @ w_up_a) + gate_b * (o_b @ w_up_b)
    x = x + g_mix * (merged @ w_out)

    h2 = modulate(rms_norm(x, norm_ffn_g), sh_ffn, sc_ffn).reshape(b * s, d)
    y = moe_ffn(h2, w_router, b_router, w_e_gate, w_e_up, w_e_down, w_sh_gate, w_sh_up, w_sh_down)
    return x + g_ffn * y.reshape(b, s, d)

def first_inputs(seed: int = 0) -> dict:
    key = jax.random.key(seed)
    ks = jax.random.split(key, 32)
    f32 = jnp.float32
    L, D = DEPTH, D_MODEL

    def nrm(k, shape, scale):
        return jax.random.normal(k, shape, f32) * scale

    return {
        "x": nrm(ks[0], (BATCH, SEQ, D), 1.0),
        "c": nrm(ks[1], (BATCH, D), 1.0),
        "ctx": nrm(ks[2], (BATCH, CTX_LEN, D), 1.0),
        "c_ctx": nrm(ks[3], (D,), 1.0),
        "w_ada": nrm(ks[4], (L, D, 6 * D), 0.5 * D ** -0.5),
        "b_ada": nrm(ks[5], (L, 6 * D), 0.01),
        "norm_mix_g": 1.0 + nrm(ks[6], (L, D), 0.1),
        "norm_ffn_g": 1.0 + nrm(ks[7], (L, D), 0.1),
        "w_in": nrm(ks[8], (L, D, IN_WIDTH), D ** -0.5),
        "b_in": nrm(ks[9], (L, IN_WIDTH), 0.01),
        "sgu_ln_g": 1.0 + nrm(ks[10], (L, SGU_WIDTH), 0.1),
        "sgu_ln_b": nrm(ks[11], (L, SGU_WIDTH), 0.01),
        "sgu_w_s": nrm(ks[12], (L, SGU_GROUPS, CHUNK, CHUNK), CHUNK ** -0.5),
        "sgu_b_s": 1.0 + nrm(ks[13], (L, SGU_GROUPS, CHUNK), 0.1),
        "tiny_w_o": nrm(ks[14], (L, TINY_DIM, SGU_WIDTH), TINY_DIM ** -0.5),
        "na_rpb": nrm(ks[15], (L, NA_HEADS, 2 * NA_ROWS - 1, 2 * NA_COLS - 1), 0.1),
        "w_up_a": nrm(ks[16], (L, SGU_WIDTH, D), SGU_WIDTH ** -0.5),
        "w_up_b": nrm(ks[17], (L, NA_WIDTH, D), NA_WIDTH ** -0.5),
        "w_out": nrm(ks[18], (L, D, D), D ** -0.5),
        "w_router": nrm(ks[19], (L, D, N_EXPERTS), D ** -0.5),
        "b_router": nrm(ks[20], (L, N_EXPERTS), 0.01),
        "w_e_gate": nrm(ks[21], (L, N_EXPERTS, D, EXPERT_FF), D ** -0.5),
        "w_e_up": nrm(ks[22], (L, N_EXPERTS, D, EXPERT_FF), D ** -0.5),
        "w_e_down": nrm(ks[23], (L, N_EXPERTS, EXPERT_FF, D), EXPERT_FF ** -0.5),
        "w_sh_gate": nrm(ks[24], (L, D, SHARED_FF), D ** -0.5),
        "w_sh_up": nrm(ks[25], (L, D, SHARED_FF), D ** -0.5),
        "w_sh_down": nrm(ks[26], (L, SHARED_FF, D), SHARED_FF ** -0.5),
        "final_norm_g": 1.0 + nrm(ks[27], (D,), 0.1),
    }

def first_block(x, c, ctx, c_ctx, w_ada, b_ada, norm_mix_g, norm_ffn_g, w_in, b_in,
              sgu_ln_g, sgu_ln_b, sgu_w_s, sgu_b_s, tiny_w_o, na_rpb, w_up_a, w_up_b, w_out,
              w_router, b_router, w_e_gate, w_e_up, w_e_down, w_sh_gate, w_sh_up, w_sh_down,
              final_norm_g):
    for i in range(DEPTH):
        x = hybrid_layer(x, c, ctx, c_ctx, w_ada[i], b_ada[i], norm_mix_g[i], norm_ffn_g[i], w_in[i], b_in[i],
                         sgu_ln_g[i], sgu_ln_b[i], sgu_w_s[i], sgu_b_s[i], tiny_w_o[i], na_rpb[i],
                         w_up_a[i], w_up_b[i], w_out[i], w_router[i], b_router[i],
                         w_e_gate[i], w_e_up[i], w_e_down[i], w_sh_gate[i], w_sh_up[i], w_sh_down[i])
    return rms_norm(x, final_norm_g)


N_META = 16
EPS = 1e-6
MLA_HEADS = 8
MLA_Q_LORA = 384
MLA_KV_LORA = 256
MLA_NOPE = 64
MLA_ROPE = 32
MLA_V = 64
MLA_QK = MLA_NOPE + MLA_ROPE
RET_HEADS = 8
RET_DK = 64
RET_DV = 128
PEER_HEADS = 8
PEER_NKEYS = 128
PEER_EXPERTS = PEER_NKEYS * PEER_NKEYS
PEER_DQ = 128
PEER_TOPK = 16
PEER_BLOCK = 256
IN_SIZES = (MLA_Q_LORA, MLA_KV_LORA, MLA_ROPE, RET_HEADS * RET_DK, RET_HEADS * RET_DK,
            RET_HEADS * RET_DV, RET_HEADS * RET_DV, D_MODEL, D_MODEL)
IN_WIDTH_2 = sum(IN_SIZES)


def rmsnorm(x, g):
    xf = x.astype(jnp.float32)
    y = xf * lax.rsqrt(jnp.mean(xf * xf, axis=-1, keepdims=True) + EPS)
    return (y * g.astype(jnp.float32)).astype(x.dtype)

def rope(x, pos):
    half = x.shape[-1] // 2
    inv = ROPE_BASE ** (-jnp.arange(half, dtype=jnp.float32) / half)
    ang = pos.astype(jnp.float32)[:, None] * inv[None, :]
    cos, sin = jnp.cos(ang), jnp.sin(ang)
    xf = x.astype(jnp.float32)
    x1, x2 = xf[..., :half], xf[..., half:]
    return jnp.concatenate([x1 * cos - x2 * sin, x1 * sin + x2 * cos], -1).astype(x.dtype)

def causal_block_attention(q, k, v):
    B, H, L, dqk = q.shape
    dv = v.shape[-1]
    nblk = -(-L // CHUNK)
    Lp = nblk * CHUNK
    qp = jnp.pad(q, ((0, 0), (0, 0), (0, Lp - L), (0, 0)))
    kpos = jnp.arange(L)
    scale = 1.0 / math.sqrt(dqk)

    def one_block(i):
        qb = lax.dynamic_slice_in_dim(qp, i * CHUNK, CHUNK, axis=2)
        s = jnp.einsum('bhqd,bhkd->bhqk', qb, k).astype(jnp.float32) * scale
        qpos = i * CHUNK + jnp.arange(CHUNK)
        s = jnp.where(kpos[None, :] <= qpos[:, None], s, -jnp.inf)
        p = jax.nn.softmax(s, axis=-1)
        return jnp.einsum('bhqk,bhkd->bhqd', p.astype(v.dtype), v)

    out = lax.map(one_block, jnp.arange(nblk))
    out = out.transpose(1, 2, 0, 3, 4).reshape(B, H, Lp, dv)
    return out[:, :, :L]

def mla_branch(c_q, c_kv, k_pe, pos, g_q_lora, w_uq, g_kv_lora, w_ukv, g_qk_q, g_qk_k):
    B, L, _ = c_q.shape
    q = (rmsnorm(c_q, g_q_lora) @ w_uq).reshape(B, L, MLA_HEADS, MLA_QK)
    kv = (rmsnorm(c_kv, g_kv_lora) @ w_ukv).reshape(B, L, MLA_HEADS, MLA_NOPE + MLA_V)
    k_nope, v = kv[..., :MLA_NOPE], kv[..., MLA_NOPE:]
    k = jnp.concatenate([k_nope, jnp.broadcast_to(k_pe[:, :, None, :], (B, L, MLA_HEADS, MLA_ROPE))], -1)
    q = rmsnorm(q, g_qk_q).transpose(0, 2, 1, 3)
    k = rmsnorm(k, g_qk_k).transpose(0, 2, 1, 3)
    q = jnp.concatenate([q[..., :MLA_NOPE], rope(q[..., MLA_NOPE:], pos)], -1)
    k = jnp.concatenate([k[..., :MLA_NOPE], rope(k[..., MLA_NOPE:], pos)], -1)
    o = causal_block_attention(q, k, v.transpose(0, 2, 1, 3))
    return o.transpose(0, 2, 1, 3).reshape(B, L, MLA_HEADS * MLA_V)

def retention_branch(q, k, v, gate, pos, g_gn):
    B, L, _ = q.shape
    H, C = RET_HEADS, CHUNK
    q = rope(q.reshape(B, L, H, RET_DK).transpose(0, 2, 1, 3), pos)
    k = rope(k.reshape(B, L, H, RET_DK).transpose(0, 2, 1, 3), pos) * (RET_DK ** -0.5)
    v = v.reshape(B, L, H, RET_DV).transpose(0, 2, 1, 3)
    P = (-N_META) % C
    Lp = L + P
    NC = Lp // C
    padf = lambda t: jnp.pad(t, ((0, 0), (0, 0), (P, 0), (0, 0))).reshape(B, H, NC, C, t.shape[-1])
    qc, kc, vc = padf(q), padf(k), padf(v)

    log_gamma = jnp.log(1.0 - 2.0 ** (-5.0 - jnp.arange(H, dtype=jnp.float32)))
    idx = jnp.arange(C, dtype=jnp.float32)
    diff = idx[:, None] - idx[None, :]
    decay = jnp.where(diff[None] >= 0, jnp.exp(jnp.maximum(diff, 0.0)[None] * log_gamma[:, None, None]), 0.0)
    zeta = jnp.exp((C - 1 - idx)[None, :] * log_gamma[:, None])
    xi = jnp.exp((idx + 1)[None, :] * log_gamma[:, None])
    gamma_c = jnp.exp(C * log_gamma)

    scores = jnp.einsum('bhncd,bhnmd->bhncm', qc, kc) * decay[None, :, None]
    inner = jnp.einsum('bhncm,bhnme->bhnce', scores, vc)
    chunk_kv = jnp.einsum('bhnmd,bhnme->bhnde', kc * zeta[None, :, None, :, None], vc)

    def step(state, kv_n):
        return gamma_c[None, :, None, None] * state + kv_n, state

    init = jnp.zeros((B, H, RET_DK, RET_DV), chunk_kv.dtype)
    _, prev_states = lax.scan(step, init, jnp.moveaxis(chunk_kv, 2, 0))
    prev_states = jnp.moveaxis(prev_states, 0, 2)
    cross = jnp.einsum('bhncd,bhnde->bhnce', qc, prev_states) * xi[None, :, None, :, None]
    y = (inner + cross).reshape(B, H, Lp, RET_DV)[:, :, P:]

    yf = y.astype(jnp.float32)
    mu = jnp.mean(yf, -1, keepdims=True)
    var = jnp.mean((yf - mu) ** 2, -1, keepdims=True)
    yn = ((yf - mu) * lax.rsqrt(var + EPS)).transpose(0, 2, 1, 3).reshape(B, L, H * RET_DV)
    yn = (yn * g_gn.astype(jnp.float32)).astype(gate.dtype)
    return jax.nn.silu(gate) * yn

def mixer_sublayer(h, pos, g_mix, w_in, g_q_lora, w_uq, g_kv_lora, w_ukv, g_qk_q, g_qk_k,
                   w_mla_out, g_ret_gn, w_ret_out, w_mix_out):
    hn = rmsnorm(h, g_mix)
    z = hn @ w_in
    c_q, c_kv, k_pe, r_q, r_k, r_v, r_g, za, zr = jnp.split(z, np.cumsum(IN_SIZES)[:-1].tolist(), axis=-1)
    y_a = mla_branch(c_q, c_kv, k_pe, pos, g_q_lora, w_uq, g_kv_lora, w_ukv, g_qk_q, g_qk_k) @ w_mla_out
    y_r = retention_branch(r_q, r_k, r_v, r_g, pos, g_ret_gn) @ w_ret_out
    merged = jax.nn.sigmoid(za) * y_a + jax.nn.sigmoid(zr) * y_r
    return merged @ w_mix_out

def peer_sublayer(h, g_ffn, w_peer_q, keys_1, keys_2, peer_u, peer_v):
    shape = h.shape
    x = rmsnorm(h, g_ffn).reshape(-1, shape[-1])
    T = x.shape[0]
    q = (x @ w_peer_q).reshape(T, PEER_HEADS, PEER_DQ)
    half = PEER_DQ // 2
    s1 = jnp.einsum('thd,kd->thk', q[..., :half], keys_1).astype(jnp.float32)
    s2 = jnp.einsum('thd,kd->thk', q[..., half:], keys_2).astype(jnp.float32)
    v1, i1 = lax.top_k(s1, PEER_TOPK)
    v2, i2 = lax.top_k(s2, PEER_TOPK)
    cand = (v1[..., :, None] + v2[..., None, :]).reshape(T, PEER_HEADS, PEER_TOPK * PEER_TOPK)
    sc, ci = lax.top_k(cand, PEER_TOPK)
    e1 = jnp.take_along_axis(i1, ci // PEER_TOPK, axis=-1)
    e2 = jnp.take_along_axis(i2, ci % PEER_TOPK, axis=-1)
    eidx = (e1 * PEER_NKEYS + e2).reshape(T, PEER_HEADS * PEER_TOPK)
    gates = jax.nn.softmax(sc, axis=-1).reshape(T, PEER_HEADS * PEER_TOPK).astype(x.dtype)

    pad = (-T) % PEER_BLOCK
    nb = (T + pad) // PEER_BLOCK
    xb = jnp.pad(x, ((0, pad), (0, 0))).reshape(nb, PEER_BLOCK, -1)
    ib = jnp.pad(eidx, ((0, pad), (0, 0))).reshape(nb, PEER_BLOCK, -1)
    gb = jnp.pad(gates, ((0, pad), (0, 0))).reshape(nb, PEER_BLOCK, -1)

    def block(args):
        xt, it, gt = args
        act = jax.nn.gelu(jnp.einsum('td,tkd->tk', xt, peer_u[it]), approximate=False)
        return jnp.einsum('tk,tkd->td', gt * act, peer_v[it])

    y = lax.map(block, (xb, ib, gb)).reshape(nb * PEER_BLOCK, -1)[:T]
    return y.reshape(shape)

def second_inputs(seed: int = 0) -> dict:
    key = jax.random.key(seed)
    ks = jax.random.split(key, 20)
    f32 = jnp.float32
    nrm = lambda k, s, sc: jax.random.normal(k, s, f32) * sc
    gain = lambda k, s: 1.0 + 0.02 * jax.random.normal(k, s, f32)
    return {
        "x": nrm(ks[0], (BATCH, SEQ, D_MODEL), 1.0),
        "meta_tokens": nrm(ks[1], (N_META, D_MODEL), 1.0),
        "g_mix": gain(ks[2], (DEPTH, D_MODEL)),
        "w_in": nrm(ks[3], (DEPTH, D_MODEL, IN_WIDTH_2), D_MODEL ** -0.5),
        "g_q_lora": gain(ks[4], (DEPTH, MLA_Q_LORA)),
        "w_uq": nrm(ks[5], (DEPTH, MLA_Q_LORA, MLA_HEADS * MLA_QK), MLA_Q_LORA ** -0.5),
        "g_kv_lora": gain(ks[6], (DEPTH, MLA_KV_LORA)),
        "w_ukv": nrm(ks[7], (DEPTH, MLA_KV_LORA, MLA_HEADS * (MLA_NOPE + MLA_V)), MLA_KV_LORA ** -0.5),
        "g_qk_q": gain(ks[8], (DEPTH, MLA_QK)),
        "g_qk_k": gain(ks[9], (DEPTH, MLA_QK)),
        "w_mla_out": nrm(ks[10], (DEPTH, MLA_HEADS * MLA_V, D_MODEL), (MLA_HEADS * MLA_V) ** -0.5),
        "g_ret_gn": gain(ks[11], (DEPTH, RET_HEADS * RET_DV)),
        "w_ret_out": nrm(ks[12], (DEPTH, RET_HEADS * RET_DV, D_MODEL), (RET_HEADS * RET_DV) ** -0.5),
        "w_mix_out": nrm(ks[13], (DEPTH, D_MODEL, D_MODEL), D_MODEL ** -0.5),
        "g_ffn": gain(ks[14], (DEPTH, D_MODEL)),
        "w_peer_q": nrm(ks[15], (DEPTH, D_MODEL, PEER_HEADS * PEER_DQ), D_MODEL ** -0.5),
        "peer_keys_1": nrm(ks[16], (DEPTH, PEER_NKEYS, PEER_DQ // 2), (PEER_DQ // 2) ** -0.5),
        "peer_keys_2": nrm(ks[17], (DEPTH, PEER_NKEYS, PEER_DQ // 2), (PEER_DQ // 2) ** -0.5),
        "peer_u": nrm(ks[18], (DEPTH, PEER_EXPERTS, D_MODEL), D_MODEL ** -0.5),
        "peer_v": nrm(ks[19], (DEPTH, PEER_EXPERTS, D_MODEL), PEER_HEADS ** -0.5),
    }

def second_block(x, meta_tokens, g_mix, w_in, g_q_lora, w_uq, g_kv_lora, w_ukv, g_qk_q, g_qk_k,
              w_mla_out, g_ret_gn, w_ret_out, w_mix_out, g_ffn, w_peer_q, peer_keys_1,
              peer_keys_2, peer_u, peer_v):
    B = x.shape[0]
    meta = jnp.broadcast_to(meta_tokens.astype(x.dtype)[None], (B, N_META, x.shape[-1]))
    h = jnp.concatenate([meta, x], axis=1)
    pos = jnp.arange(h.shape[1])
    for layer in range(DEPTH):
        h = h + mixer_sublayer(h, pos, g_mix[layer], w_in[layer], g_q_lora[layer], w_uq[layer],
                               g_kv_lora[layer], w_ukv[layer], g_qk_q[layer], g_qk_k[layer],
                               w_mla_out[layer], g_ret_gn[layer], w_ret_out[layer], w_mix_out[layer])
        if layer == DEPTH - 1:
            h = h[:, N_META:]
        h = h + peer_sublayer(h, g_ffn[layer], w_peer_q[layer], peer_keys_1[layer], peer_keys_2[layer],
                              peer_u[layer], peer_v[layer])
    return h


def setup_inputs(seed=0):
    out = dict(first_inputs(seed))
    for name, value in second_inputs(seed + 1).items():
        if name != "x":
            out[name + "_2"] = value
    return out


def reference(
    x, c, ctx, c_ctx, w_ada, b_ada, norm_mix_g, norm_ffn_g, w_in, b_in, sgu_ln_g, sgu_ln_b,
    sgu_w_s, sgu_b_s, tiny_w_o, na_rpb, w_up_a, w_up_b, w_out, w_router, b_router, w_e_gate,
    w_e_up, w_e_down, w_sh_gate, w_sh_up, w_sh_down, final_norm_g, meta_tokens_2, g_mix_2,
    w_in_2, g_q_lora_2, w_uq_2, g_kv_lora_2, w_ukv_2, g_qk_q_2, g_qk_k_2, w_mla_out_2,
    g_ret_gn_2, w_ret_out_2, w_mix_out_2, g_ffn_2, w_peer_q_2, peer_keys_1_2, peer_keys_2_2,
    peer_u_2, peer_v_2,
):
    x = first_block(
        x, c, ctx, c_ctx, w_ada, b_ada, norm_mix_g, norm_ffn_g, w_in, b_in, sgu_ln_g, sgu_ln_b,
        sgu_w_s, sgu_b_s, tiny_w_o, na_rpb, w_up_a, w_up_b, w_out, w_router, b_router, w_e_gate,
        w_e_up, w_e_down, w_sh_gate, w_sh_up, w_sh_down, final_norm_g,
    )
    return second_block(
        x, meta_tokens_2, g_mix_2, w_in_2, g_q_lora_2, w_uq_2, g_kv_lora_2, w_ukv_2, g_qk_q_2,
        g_qk_k_2, w_mla_out_2, g_ret_gn_2, w_ret_out_2, w_mix_out_2, g_ffn_2, w_peer_q_2,
        peer_keys_1_2, peer_keys_2_2, peer_u_2, peer_v_2,
    )


_drawn_inputs = setup_inputs


def setup_inputs(seed=0):
    import zlib

    import numpy as np

    out = dict(_drawn_inputs(seed))
    spreads = {}
    factors = {'b_in': 3.289,
     'sgu_ln_b': 3.394,
     'na_rpb': 4.235,
     'g_q_lora_2': 7.46,
     'g_kv_lora_2': 6.015,
     'g_qk_q_2': 7.764,
     'g_qk_k_2': 7.53,
     'g_ret_gn_2': 23.98,
     'g_ffn_2': 7.199}
    for name, (base, spread) in spreads.items():
        noise = np.random.default_rng([zlib.crc32(name.encode()), seed]).standard_normal(out[name].shape)
        drawn = base * np.exp(spread * noise) if base else spread * noise
        out[name] = __import__('jax').numpy.asarray(drawn.astype(out[name].dtype))
    for name, factor in factors.items():
        out[name] = (out[name] * factor).astype(out[name].dtype)
    return out
```

```python
from contextlib import ExitStack

import concourse.bass as bass
from concourse import mybir

ALU = mybir.AluOpType
ACT = mybir.ActivationFunctionType
F32 = mybir.dt.float32
F32R = mybir.dt.float32r
U32 = mybir.dt.uint32
AX = mybir.AxisListType.X

P = 128
S, D = 512, 1024
T = S // P
KD = D // P
CTX, META = 256, 16
EPS = 1e-6
TINY, NAH, NAD = 64, 16, 32
GRID, ROWS = 64, 8
SGU_G = 8
E, FF, TOPK = 64, 256, 8
MH, MNOPE, MROPE, MV = 8, 64, 32, 64
MQK = MNOPE + MROPE
QL, KVL = 384, 256
RH, RDK, RDV = 8, 64, 128
PH, PK, PNK = 8, 16, 128
NEG = -1e30
DR = 2 * ROWS - 2
W_BLOCK = 512

COLS = {}


def _place_cols():
    at = 0
    for name, n in (("c", 8), ("c_ctx", 8), ("b_ada", 48), ("g_mix", 8), ("g_ffn", 8), ("b_u", 8), ("b_nq", 4),
                    ("b_nk", 4), ("b_ga", 8), ("b_gb", 8), ("g_mix_2", 8), ("g_ffn_2", 8), ("g_q_lora", 3),
                    ("g_kv_lora", 2)):
        COLS[name] = (at, n)
        at += n
    return at


N_COLS = _place_cols()


class Signal:

    def __init__(self, sem):
        self.sem, self.base = sem, 0

    def at(self, n):
        return self.base + n


class Core:

    def __init__(self, nc, stack):
        self.nc, self.stack = nc, stack
        self.held = []
        self.top = nc.sbuf_usable_end
        self.low = (nc.sbuf_base + 63) // 64 * 64
        self.signals = {}
        self.uid = 0
        self.spans = {}

    def sb(self, name, shape, dt=F32, at=None):
        size = 1
        for n in shape[1:]:
            size *= n
        size = (size * 4 + 63) // 64 * 64
        if at is None:
            at = self.low
            for a, b in sorted(self.held):
                if a - at >= size:
                    break
                at = max(at, b)
            assert at + size <= self.top, (name, at, size)
        self.uid += 1
        t = self.nc.alloc_sbuf_tensor_at(f"{name}_{self.uid}", shape, dt, offset=at)
        self.held.append((at, at + size))
        self.spans[t.name] = (at, at + size)
        return t

    def alias(self, t, name, shape, dt):
        self.uid += 1
        return self.nc.alloc_sbuf_tensor_at(f"{name}_{self.uid}", shape, dt, offset=self.at(t))

    def psum(self, name, shape, dt):
        self.uid += 1
        return self.nc.psum_tensor(f"{name}_{self.uid}", shape, dt)

    def at(self, t):
        return self.spans[t.name][0]

    def drop(self, *tensors):
        for t in tensors:
            self.held.remove(self.spans[t.name])

    def sig(self, name):
        if name not in self.signals:
            self.signals[name] = Signal(self.stack.enter_context(self.nc.semaphore(name)))
        return self.signals[name]


def linked(eng, signal):
    def link(ins):
        signal.base += 1
        ins.then_inc(signal.sem, 1)
        eng.wait_ge(signal.sem, signal.base)
    return link


def dram_rows(ap, lo, hi):
    return ap[:, lo:hi].rearrange("(k p) n -> p k n", p=P)



def load_constants(core, a, keep):
    nc = core.nc
    loads = [(keep["ident"][:], a["k_ident"]), (keep["ones"][:], a["k_ones"]), (keep["cols"][:], a["cols"]),
             (keep["x"][:], a["x"].rearrange("(t p) d -> p t d", p=P))]
    done = core.sig("constants_in")
    with nc.Block() as block:
        @block.sync
        def _(sp):
            for dst, src in loads:
                sp.dma_start(dst, src).then_inc(done.sem, 16)
            sp.wait_ge(done.sem, 16 * len(loads))


def modulation(core, a, keep):
    nc = core.nc
    NB, W = 6 * D // W_BLOCK, W_BLOCK
    MB = W // P
    w = core.sb("w_ada", [P, 2, KD, W])
    silu_c = core.sb("silu_c", [P, KD, 2])
    mod = core.sb("mod", [P, 6 * KD, 2])
    diag = core.sb("diag", [P, 2, P])
    w_in = [core.sig("ada_w_even"), core.sig("ada_w_odd")]
    c_ready, mm, mod_ready = core.sig("silu_c_ready"), core.sig("ada_mm"), core.sig("mod_ready")
    diag_ready, row_mm, chain = core.sig("diag_ready"), core.sig("gain_row_mm"), core.sig("dve_chain")
    row_out = core.sig("gain_row_out")
    c0 = COLS["c"][0]
    col = keep["cols"]
    with (core.psum("ps_mod", [P, 6 * KD, 2], F32) as ps_mod,
          core.psum("ps_row", [P, 2, 2 * W], F32) as ps_row, nc.Block() as block):
        @block.sync
        def _(sp):
            for s in range(2):
                sp.dma_start(w[:, s], dram_rows(a["w_ada"], s * W, (s + 1) * W)).then_inc(w_in[s].sem, 16)
            with sp.Fori(1, NB // 2) as i:
                for s in range(2):
                    sp.wait_ge(mm.sem, 2 * i + (s - 1))
                    sp.dma_start(w[:, s], a["w_ada"].rearrange("(k p) (b n) -> b p k n", p=P, n=W)
                                 [bass.ds(2 * i + s, 1)].rearrange("b p k n -> (b p) k n")).then_inc(w_in[s].sem, 16)

        @block.scalar
        def _(act):
            for j in range(2):
                nc.scalar.activation(silu_c[:, :, j], col[:, c0 + j * KD:c0 + (j + 1) * KD], ACT.Silu) \
                    .then_inc(c_ready.sem, 1)

        @block.tensor
        def _(pe):
            pe.wait_ge(c_ready.sem, 2)
            with pe.Fori(0, NB // 2) as i:
                for s in range(2):
                    pe.wait_ge(w_in[s].sem, 16 * i + 16)
                    for m in range(MB):
                        for k in range(KD):
                            last = nc.tensor.matmul(
                                ps_mod[:, bass.ds((2 * i + s) * MB + m, 1), :].rearrange("p a b -> p (a b)"),
                                w[:, s, k, m * P:(m + 1) * P], silu_c[:, k, :], start=k == 0, stop=k == KD - 1)
                    last.then_inc(mm.sem, 1)
            for g in range(2):
                for k in range(KD):
                    n = g * KD + k
                    pe.wait_ge(diag_ready.sem, n + 1)
                    nc.tensor.matmul(ps_row[:, g, k * P:(k + 1) * P], keep["ones"][:], diag[:, n % 2, :],
                                     start=True, stop=True).then_inc(row_mm.sem, 1)

        @block.vector
        def _(dve):
            link = linked(dve, chain)
            dve.wait_ge(mm.sem, NB)
            b0 = COLS["b_ada"][0]
            for j in range(2):
                link(nc.vector.tensor_tensor(mod[:, :, j], ps_mod[:, :, j], col[:, b0:b0 + 6 * KD], ALU.add))
            for j in range(2):
                g0 = COLS["g_mix"][0]
                link(nc.vector.scalar_tensor_tensor(keep["gain_mix"][:, j, :], mod[:, KD:2 * KD, j], 1.0,
                                                    col[:, g0:g0 + KD], ALU.add, ALU.mult))
                link(nc.vector.tensor_copy(keep["shift_mix"][:, j, :], mod[:, 0:KD, j]))
            g0 = COLS["g_ffn"][0]
            link(nc.vector.scalar_tensor_tensor(keep["gain_ffn"][:], mod[:, 4 * KD:5 * KD, 0], 1.0,
                                                col[:, g0:g0 + KD], ALU.add, ALU.mult))
            link(nc.vector.tensor_copy(keep["shift_ffn"][:], mod[:, 3 * KD:4 * KD, 0]))
            for g, at in enumerate((2 * KD, 5 * KD)):
                for k in range(KD):
                    n = g * KD + k
                    if n >= 2:
                        dve.wait_ge(row_mm.sem, n - 1)
                    nc.vector.tensor_scalar(diag[:, n % 2, :], keep["ident"][:], mod[:, at + k, 0:1], None,
                                            ALU.mult).then_inc(diag_ready.sem, 1)
            dve.wait_ge(row_mm.sem, 2 * KD)
            for g, name in enumerate(("gate_mix_row", "gate_ffn_row")):
                for h in range(2):
                    nc.vector.tensor_copy(keep[name][:, h * W:(h + 1) * W], ps_row[:, g, h * W:(h + 1) * W]) \
                        .then_inc(row_out.sem, 1)
    core.drop(w, silu_c, mod, diag)



def normalise(core, sources, width, out):
    nc = core.nc
    n = len(sources)
    stat = core.sb("stat", [P, 3, n])
    junk = core.sb("junk", [P, width])
    squares, root, chain, done = core.sig("squares"), core.sig("root"), core.sig("dve_chain"), core.sig("normalised")
    act_chain = core.sig("act_chain")
    b_sq, b_root, b_done = squares.base, root.base, done.base
    with nc.Block() as block:
        @block.scalar
        def _(act):
            link = linked(act, act_chain)
            act.wait_ge(squares.sem, b_sq + 1)
            for i, (rows, src) in enumerate(sources):
                link(nc.scalar.activation(junk[0:rows, :], src, ACT.Square, accum_out=stat[0:rows, 0, i:i + 1]))
            nc.scalar.activation(junk[0:1, 0:1], junk[0:1, 0:1], ACT.Copy).then_inc(root.sem, 1)
            act.wait_ge(squares.sem, b_sq + 2)
            nc.scalar.activation(stat[:, 2, :], stat[:, 1, :], ACT.Sqrt).then_inc(root.sem, 1)

        @block.vector
        def _(dve):
            link = linked(dve, chain)
            nc.vector.memset(stat[:], 1.0).then_inc(squares.sem, 1)
            dve.wait_ge(root.sem, b_root + 1)
            nc.vector.tensor_scalar(stat[:, 1, :], stat[:, 0, :], 1.0 / width, EPS, ALU.mult, ALU.add) \
                .then_inc(squares.sem, 1)
            dve.wait_ge(root.sem, b_root + 2)
            link(nc.vector.reciprocal(stat[:, 0, :], stat[:, 2, :]))
            for i, (rows, src) in enumerate(sources):
                nc.vector.tensor_scalar(out[i], src, stat[0:rows, 0, i:i + 1], None, ALU.mult) \
                    .then_inc(done.sem, 1)
    squares.base += 2
    root.base += 2
    done.base += n
    core.drop(stat, junk)


def turn(core, jobs):
    nc = core.nc
    turned, out = core.sig("turned"), [core.sig("turn_out_dve"), core.sig("turn_out_act")]
    ident = core.ident
    b_t, b_o = turned.base, [o.base for o in out]
    with core.psum("ps_turn", [P, 4, W_BLOCK], F32) as ps, nc.Block() as block:
        @block.tensor
        def _(pe):
            for n, (pieces, _) in enumerate(jobs):
                if n >= 4:
                    pe.wait_ge(out[n % 2].sem, b_o[n % 2] + (n - 4) // 2 + 1)
                for src, c0 in pieces:
                    rows, cols = src.shape[0], src.shape[-1]
                    last = nc.tensor.transpose(ps[0:cols, n % 4, c0:c0 + rows], src, ident[0:rows, 0:rows])
                last.then_inc(turned.sem, 1)

        @block.vector
        def _(dve):
            for n in range(0, len(jobs), 2):
                dve.wait_ge(turned.sem, b_t + n + 1)
                jobs[n][1](nc.vector, ps[:, n % 4, :]).then_inc(out[0].sem, 1)

        @block.scalar
        def _(act):
            for n in range(1, len(jobs), 2):
                act.wait_ge(turned.sem, b_t + n + 1)
                jobs[n][1](nc.scalar, ps[:, n % 4, :]).then_inc(out[1].sem, 1)
    turned.base += len(jobs)
    out[0].base += (len(jobs) + 1) // 2
    out[1].base += len(jobs) // 2


def copied(nc, dst, rows, cols):
    def evacuate(eng, bank):
        if eng is nc.scalar:
            return nc.scalar.activation(dst, bank[0:rows, 0:cols], ACT.Copy)
        return nc.vector.tensor_copy(dst, bank[0:rows, 0:cols])
    return evacuate


def scaled(nc, dst, rows, cols, gain, shift=None):
    def evacuate(eng, bank):
        src = bank[0:rows, 0:cols]
        if eng is nc.scalar:
            if shift is None:
                return nc.scalar.activation(dst, src, ACT.Copy, scale=gain)
            return nc.scalar.activation(dst, src, ACT.Identity, scale=gain, bias=shift)
        if shift is None:
            return nc.vector.tensor_scalar(dst, src, gain, None, ALU.mult)
        return nc.vector.tensor_scalar(dst, src, gain, shift, ALU.mult, ALU.add)
    return evacuate


def norm_turned(core, sources, width, dst, spans):
    nc = core.nc
    xn = core.sb("xn", [P, len(sources), width])
    normalise(core, sources, width, [xn[0:r, i, :] for i, (r, _) in enumerate(sources)])
    jobs = []
    for k in range(width // P):
        for first, count, c0, gain, shift in spans:
            rows = [sources[first + i][0] for i in range(count)]
            pieces = [(xn[0:rows[i], first + i, k * P:(k + 1) * P], i * P) for i in range(count)]
            total = sum(rows)
            jobs.append((pieces, scaled(nc, dst[:, k, c0:c0 + total], P, total, gain(k), shift(k) if shift else None)))
    turn(core, jobs)
    core.drop(xn)


def project(core, blocks):
    nc = core.nc
    NW, NP = 3, 4
    kmax = max(b[0].shape[1] for b in blocks)
    w = core.sb("w", [P, NW, kmax, W_BLOCK])
    w_in = [core.sig(f"w_in_{i}") for i in range(NW)]
    mm = core.sig("unit_mm")
    out = {"act": core.sig("unit_out_act"), "dve": core.sig("unit_out_dve")}
    chain = {"act": core.sig("act_chain"), "dve": core.sig("dve_chain")}
    b_w, b_mm = [s.base for s in w_in], mm.base
    b_out = {e: s.base for e, s in out.items()}
    units = [(b, u) for b, (_, us) in enumerate(blocks) for u in us]
    slot = [w[:, b % NW, 0:src.shape[1], 0:src.shape[2]] for b, (src, _) in enumerate(blocks)]

    def outs_before(n, e):
        return sum(1 for _, u in units[:n] if u[3] == e)

    with core.psum("ps_unit", [P, NP, W_BLOCK], F32) as ps, nc.Block() as block:
        @block.sync
        def _(sp):
            for b, (src, _) in enumerate(blocks):
                if b >= NW:
                    sp.wait_ge(mm.sem, b_mm + sum(len(us) for _, us in blocks[:b - NW + 1]))
                sp.dma_start(slot[b], src).then_inc(w_in[b % NW].sem, 16)

        @block.tensor
        def _(pe):
            for n, (b, (pairs, rows, cols, _, _)) in enumerate(units):
                first = n == 0 or units[n - 1][0] != b
                if first:
                    pe.wait_ge(w_in[b % NW].sem, b_w[b % NW] + 16 * (b // NW + 1))
                if n >= NP:
                    e = units[n - NP][1][3]
                    pe.wait_ge(out[e].sem, b_out[e] + outs_before(n - NP + 1, e))
                both = pairs(slot[b])
                for i, (lhs, rhs) in enumerate(both):
                    last = nc.tensor.matmul(ps[0:rows, n % NP, 0:cols], lhs, rhs, start=i == 0, stop=i == len(both) - 1)
                last.then_inc(mm.sem, 1)

        def write_out(eng, name):
            link = linked(eng, chain[name])
            for n, (_, (_, rows, cols, e, evacuate)) in enumerate(units):
                if e == name:
                    eng.wait_ge(mm.sem, b_mm + n + 1)
                    evacuate(ps[0:rows, n % NP, 0:cols], link).then_inc(out[name].sem, 1)

        @block.scalar
        def _(act):
            write_out(act, "act")

        @block.vector
        def _(dve):
            write_out(dve, "dve")
    for b in range(len(blocks)):
        w_in[b % NW].base += 16
    mm.base += len(units)
    for e in out:
        out[e].base += outs_before(len(units), e)
    core.drop(w)


def features_unit(x, k_chunks, m, n, engine, evacuate):
    return (lambda w: [(w[:, k, m * P:(m + 1) * P], x[:, k, n]) for k in range(k_chunks)],
            P, n.stop - n.start, engine, evacuate)


def tokens_unit(x, k_chunks, tok, cols, engine, evacuate, c0=0):
    return (lambda w: [(x[:, k, tok], w[:, k, c0:c0 + cols]) for k in range(k_chunks)],
            tok.stop - tok.start, cols, engine, evacuate)


def rope(nc, link, x1, x2, cos, sin, o1, o2, t1, t2):
    link(nc.vector.tensor_tensor(t1, x1, cos, ALU.mult))
    link(nc.vector.tensor_tensor(t2, x2, sin, ALU.mult))
    link(nc.vector.tensor_tensor(o1, t1, t2, ALU.subtract))
    link(nc.vector.tensor_tensor(t1, x2, cos, ALU.mult))
    link(nc.vector.tensor_tensor(t2, x1, sin, ALU.mult))
    link(nc.vector.tensor_tensor(o2, t1, t2, ALU.add))


def attend(core, tiles, dv, outs):
    nc = core.nc
    units = [(j, h, u) for j, heads in enumerate(tiles) for h, u in enumerate(heads)]
    U, H = len(units), len(tiles[0])
    FAR = max(u[4] for _, _, u in units)
    s = core.sb("scores", [P, 2, S])
    pr = core.sb("probs", [P, 2, S + FAR])
    prT = core.sb("probsT", [P, 2, S + 2 * P])
    mx = core.sb("maxima", [P, 3, 2])
    sums = core.sb("sums", [P, 3, U])
    scored, maxed, exped = core.sig("scored"), core.sig("maxed"), core.sig("exped")
    turned, near_out, far_out = core.sig("probs_turned"), core.sig("near_out"), core.sig("far_out")
    near_taken, valued, tile_out = core.sig("near_taken"), core.sig("valued"), core.sig("tile_out")
    chain = core.sig("dve_chain")
    sigs = (scored, maxed, exped, turned, near_out, far_out, near_taken, valued, tile_out)
    bs, bm, be, bt, bn, bf, bk, bv, bo = (x.base for x in sigs)
    ident = core.ident
    with (core.psum("ps_near", [P, 2, S], F32) as ps_near, core.psum("ps_far", [P, 2, S], F32) as ps_far,
          core.psum("ps_pt", [P, 2, S], F32) as ps_pt, core.psum("ps_o", [P, 2, S], F32) as ps_o,
          nc.Block() as block):
        @block.tensor
        def _(pe):
            def score(n):
                j, h, (q, kn, near, kf, far, _, _, _) = units[n]
                b = n % 2
                if n >= 2:
                    pe.wait_ge(near_taken.sem, bk + n - 1)
                    pe.wait_ge(exped.sem, be + n - 1)
                nc.tensor.matmul(ps_near[:, b, 0:near], q, kn, start=True, stop=True)
                nc.tensor.matmul(ps_far[:, b, 0:far], q, kf, start=True, stop=True).then_inc(scored.sem, 1)

            score(0)
            for n in range(U):
                if n + 1 < U:
                    score(n + 1)
                j, h, (_, _, near, _, far, _, vn, vf) = units[n]
                b = n % 2
                pe.wait_ge(exped.sem, be + n + 1)
                if n >= 1:
                    pe.wait_ge(near_out.sem, bn + n)
                    pe.wait_ge(far_out.sem, bf + n)
                for i in range(near // P):
                    nc.tensor.transpose(ps_pt[:, 0, i * P:(i + 1) * P], pr[:, b, i * P:(i + 1) * P], ident[:])
                for i, v in enumerate(vf):
                    rows = v.shape[0]
                    last = nc.tensor.transpose(ps_pt[0:rows, 1, i * P:(i + 1) * P],
                                               pr[:, b, S + i * P:S + i * P + rows], ident[:])
                last.then_inc(turned.sem, 1)
                pe.wait_ge(near_out.sem, bn + n + 1)
                pe.wait_ge(far_out.sem, bf + n + 1)
                if h == 0 and j >= 2:
                    pe.wait_ge(tile_out.sem, bo + j - 1)
                total = len(vn) + len(vf)
                for i, v in enumerate(vn + vf):
                    rows = v.shape[0]
                    at = i * P if i < len(vn) else S + (i - len(vn)) * P
                    last = nc.tensor.matmul(ps_o[:, j % 2, h * dv:(h + 1) * dv], prT[0:rows, b, at:at + P], v,
                                            start=i == 0, stop=i == total - 1)
                last.then_inc(valued.sem, 1)

        @block.vector
        def _(dve):
            link = linked(dve, chain)

            def maxima(n):
                _, _, (_, _, near, _, far, bias, _, _) = units[n]
                b = n % 2
                dve.wait_ge(scored.sem, bs + n + 1)
                if n >= 2:
                    dve.wait_ge(exped.sem, be + n - 1)
                nc.vector.tensor_tensor_reduce(s[:, b, 0:near], ps_near[:, b, 0:near], bias, 1.0, NEG, ALU.add,
                                               ALU.max, mx[:, 0, b:b + 1]).then_inc(near_taken.sem, 1)
                link(nc.vector.tensor_reduce(mx[:, 1, b:b + 1], ps_far[:, b, 0:far], AX, ALU.max))
                dve.wait_ge(near_taken.sem, bk + n + 1)
                nc.vector.tensor_scalar(mx[:, 2, b:b + 1], mx[:, 0, b:b + 1], mx[:, 1, b:b + 1], -1.0, ALU.max,
                                        ALU.mult).then_inc(maxed.sem, 1)

            maxima(0)
            for n in range(U):
                if n + 1 < U:
                    maxima(n + 1)
                j, h, (_, _, near, _, _, _, _, _) = units[n]
                dve.wait_ge(turned.sem, bt + n + 1)
                if n >= 2:
                    dve.wait_ge(valued.sem, bv + n - 1)
                nc.vector.tensor_copy(prT[:, n % 2, 0:near], ps_pt[:, 0, 0:near]).then_inc(near_out.sem, 1)
                if h == H - 1:
                    cols = slice(n - H + 1, n + 1)
                    link(nc.vector.tensor_tensor(sums[:, 2, cols], sums[:, 0, cols], sums[:, 1, cols], ALU.add))
                    link(nc.vector.reciprocal(sums[:, 0, cols], sums[:, 2, cols]))
                    dve.wait_ge(valued.sem, bv + n + 1)
                    nc.vector.tensor_tensor(outs[j], ps_o[:, j % 2, 0:H * dv].rearrange("p (h d) -> p h d", h=H),
                                            sums[:, 0, cols].unsqueeze(2).to_broadcast([P, H, dv]), ALU.mult) \
                        .then_inc(tile_out.sem, 1)

        @block.scalar
        def _(act):
            def exponentials(n):
                _, _, (_, _, near, _, far, _, _, _) = units[n]
                b = n % 2
                act.wait_ge(maxed.sem, bm + n + 1)
                if n >= 2:
                    act.wait_ge(turned.sem, bt + n - 1)
                nc.scalar.activation(pr[:, b, 0:near], s[:, b, 0:near], ACT.Exp, bias=mx[:, 2, b:b + 1],
                                     accum_out=sums[:, 0, n:n + 1])
                nc.scalar.activation(pr[:, b, S:S + far], ps_far[:, b, 0:far], ACT.Exp, bias=mx[:, 2, b:b + 1],
                                     accum_out=sums[:, 1, n:n + 1]).then_inc(exped.sem, 1)

            exponentials(0)
            for n in range(U):
                if n + 1 < U:
                    exponentials(n + 1)
                _, _, (_, _, _, _, _, _, _, vf) = units[n]
                rows = vf[0].shape[0]
                act.wait_ge(turned.sem, bt + n + 1)
                if n >= 2:
                    act.wait_ge(valued.sem, bv + n - 1)
                nc.scalar.activation(prT[0:rows, n % 2, S:S + len(vf) * P], ps_pt[0:rows, 1, 0:len(vf) * P],
                                     ACT.Copy).then_inc(far_out.sem, 1)
    for x in sigs[:8]:
        x.base += U
    tile_out.base += len(tiles)
    core.drop(s, pr, prT, mx, sums)



def first_mixer(core, a, keep):
    nc = core.nc
    x, cols = keep["x"], keep["cols"]
    TC = T + CTX // P

    def col(name, i):
        at = COLS[name][0]
        return cols[:, at + i:at + i + 1]

    hT = core.sb("hT", [P, KD, S + CTX])
    ctx = core.sb("ctx", [P, CTX // P, D])
    load(core, [(ctx[:], a["ctx"].rearrange("(t p) d -> p t d", p=P))])
    norm_turned(core, [(P, x[:, t, :]) for t in range(T)] + [(P, ctx[:, t, :]) for t in range(CTX // P)], D, hT,
                [(0, T, 0, lambda k: keep["gain_mix"][:, 0, k:k + 1], lambda k: keep["shift_mix"][:, 0, k:k + 1]),
                 (T, CTX // P, S, lambda k: keep["gain_mix"][:, 1, k:k + 1],
                  lambda k: keep["shift_mix"][:, 1, k:k + 1])])
    core.drop(ctx)

    u = core.sb("u", [P, KD, S])
    v = core.sb("v", [P, T, D])
    tiny = core.sb("tiny_qkv", [P, TC, 3 * TINY])
    nq = core.sb("nq", [P, 4, S])
    nk = core.sb("nk", [P, 4, S + CTX])
    nv = core.sb("nv", [P, TC, NAH * NAD])
    brow = core.sb("b_rows", [P, D + 3 * TINY + 512])
    load(core, [(brow[:], a["b_rows"].partition_broadcast(P))])
    all_tok = slice(0, S)
    blocks = []

    def toks(t):
        return slice(t * P, (t + 1) * P)

    def plus_row(dst, at, n):
        return lambda ps, link: nc.vector.tensor_tensor(dst, ps, brow[:, at:at + n], ALU.add)

    def through(func, dst, bias):
        return lambda ps, link: nc.scalar.activation(dst, ps, func, bias=bias)

    for b in range(2):
        blocks.append((dram_rows(a["w_in"], b * 512, (b + 1) * 512),
                       [features_unit(hT, KD, m, all_tok, "act", through(ACT.Gelu, u[:, 4 * b + m, :], col("b_u", 4 * b + m)))
                        for m in range(4)]))
    for b in range(2):
        at = 1024 + b * 512
        blocks.append((dram_rows(a["w_in"], at, at + 512),
                       [tokens_unit(hT, KD, toks(t), 512, "dve", plus_row(v[:, t, b * 512:(b + 1) * 512], b * 512, 512))
                        for t in range(T)]))
    blocks.append((dram_rows(a["w_in"], 2048, 2240),
                   [tokens_unit(hT, KD, toks(t), 192, "dve", plus_row(tiny[:, t, :], D, 192)) for t in range(TC)]))
    scale = NAD ** -0.5
    blocks.append((dram_rows(a["w_in"], 2240, 2752),
                   [features_unit(hT, KD, m, all_tok, "dve",
                                  lambda ps, link, m=m: nc.vector.tensor_scalar(nq[:, m, :], ps, col("b_nq", m), scale,
                                                                                ALU.add, ALU.mult))
                    for m in range(4)]))
    blocks.append((dram_rows(a["w_in"], 2752, 3264),
                   [features_unit(hT, KD, m, sl, "act", through(ACT.Identity, nk[:, m, sl], col("b_nk", m)))
                    for m in range(4) for sl in (all_tok, slice(S, S + CTX))]))
    blocks.append((dram_rows(a["w_in"], 3264, 3776),
                   [tokens_unit(hT, KD, toks(t), 512, "dve", plus_row(nv[:, t, :], D + 192, 512)) for t in range(TC)]))
    project(core, blocks)
    core.drop(brow)

    rows = core.sb("ln_rows", [P, 2, D])
    tab = core.sb("rope_tab", [P, 2, T, 2, 16])
    tq = core.sb("tq", [P, T, TINY])
    tk = core.sb("tk", [P, TC, TINY])
    t1, t2 = core.sb("t1", [P, T, 2, 16]), core.sb("t2", [P, T, 2, 16])
    zero = core.sb("zero", [P, S])
    near_bias = core.sb("near_bias", [P, NAH, DR, GRID])
    raw = core.sb("raw_bias", [P, 2, DR, GRID])
    mask = core.sb("near_mask", [P, GRID])
    stats = core.sb("ln_stats", [P, T, 16])
    in_, gelu, chain = core.sig("prepare_in"), core.sig("v_gelu"), core.sig("dve_chain")
    raw_in = [core.sig("raw_bias_even"), core.sig("raw_bias_odd")]
    pool_done, root, var_done, ln_done = (core.sig("near_bias_done"), core.sig("root"), core.sig("ln_var"),
                                          core.sig("ln_done"))
    b_root = root.base
    with nc.Block() as block:
        @block.sync
        def _(sp):
            sp.dma_start(rows[:], a["ln_rows"].partition_broadcast(P)).then_inc(in_.sem, 16)
            sp.dma_start(tab[:], a["k_rope_tiny"]).then_inc(in_.sem, 16)
            sp.dma_start(mask[:], a["k_near_mask"]).then_inc(in_.sem, 16)
            rpb = a["rpb"]
            for h in range(NAH):
                if h >= 2:
                    sp.wait_ge(pool_done.sem, h - 1)
                for half in range(2):
                    src = bass.AP(tensor=rpb.tensor, offset=(h * 15 + 1 - half) * 127,
                                  ap=[[1, GRID], [127, DR], [1, GRID]])
                    sp.dma_start(raw[half * GRID:(half + 1) * GRID, h % 2, :, :], src).then_inc(raw_in[h % 2].sem, 16)

        @block.gpsimd
        def _(pool):
            pool.wait_ge(in_.sem, 48)
            for h in range(NAH):
                pool.wait_ge(raw_in[h % 2].sem, 32 * (h // 2 + 1))
                r = raw[:, h % 2, :, :]
                back = bass.AP(tensor=r.tensor, offset=r.offset + GRID - 1,
                               ap=[list(r.ap[0]), [GRID, DR], [-1, GRID]])
                nc.gpsimd.tensor_tensor(near_bias[:, h], back, mask[:].unsqueeze(1).to_broadcast([P, DR, GRID]),
                                        ALU.add).then_inc(pool_done.sem, 1)

        @block.scalar
        def _(act):
            for t in range(T):
                nc.scalar.activation(v[:, t, :], v[:, t, :], ACT.Gelu).then_inc(gelu.sem, 1)
            act.wait_ge(var_done.sem, 1)
            nc.scalar.activation(stats[:, :, 14:15], stats[:, :, 13:14], ACT.Sqrt, bias=0.0).then_inc(root.sem, 1)

        @block.vector
        def _(dve):
            link = linked(dve, chain)
            link(nc.vector.memset(zero[:], 0.0))
            dve.wait_ge(in_.sem, 48)
            for dst, at in ((tq, 0), (tk, TINY)):
                src = tiny[:, 0:T, at:at + TINY].rearrange("p t (a h d) -> p t a h d", a=2, h=2)
                o = dst[:, 0:T, :].rearrange("p t (a h d) -> p t a h d", a=2, h=2)
                for t in range(T):
                    rope(nc, link, src[:, t, :, 0, :], src[:, t, :, 1, :], tab[:, 0, t], tab[:, 1, t],
                         o[:, t, :, 0, :], o[:, t, :, 1, :], t1[:, t], t2[:, t])
            link(nc.vector.tensor_copy(tk[:, T:TC, :], tiny[:, T:TC, TINY:2 * TINY]))
            link(nc.vector.tensor_scalar(tq[:], tq[:], TINY ** -0.5, None, ALU.mult))
            for t in range(T):
                dve.wait_ge(gelu.sem, t + 1)
                for h in range(2):
                    link(nc.vector.bn_stats(stats[:, t, 6 * h:6 * h + 6], v[:, t, h * 512:(h + 1) * 512]))
                link(nc.vector.bn_aggr(stats[:, t, 12:14], stats[:, t, 0:12]))
            nc.vector.tensor_scalar(stats[:, :, 13:14], stats[:, :, 13:14], EPS, None, ALU.add) \
                .then_inc(var_done.sem, 1)
            dve.wait_ge(root.sem, b_root + 1)
            link(nc.vector.reciprocal(stats[:, :, 13:14], stats[:, :, 14:15]))
            for t in range(T):
                link(nc.vector.tensor_scalar(v[:, t, :], v[:, t, :], stats[:, t, 12:13], stats[:, t, 13:14],
                                             ALU.subtract, ALU.mult))
                link(nc.vector.tensor_tensor(v[:, t, :], v[:, t, :], rows[:, 0, :], ALU.mult))
                link(nc.vector.tensor_tensor(v[:, t, :], v[:, t, :], rows[:, 1, :], ALU.add))
    root.base += 1
    core.drop(rows, tab, t1, t2, raw, mask, stats)

    tqT = core.sb("tqT", [TINY, S])
    tkT = core.sb("tkT", [TINY, S + CTX])
    turn(core, [([(tq[:, t, :], t * P) for t in range(T)], copied(nc, tqT[:], TINY, S)),
                ([(tk[:, t, :], t * P) for t in range(T)], copied(nc, tkT[:, 0:S], TINY, S)),
                ([(tk[:, T + t, :], t * P) for t in range(2)], copied(nc, tkT[:, S:S + CTX], TINY, CTX))])
    core.drop(tq, tk)
    ot = core.sb("tiny_out", [P, T, TINY])
    vt = [tiny[:, t, 2 * TINY:3 * TINY] for t in range(TC)]
    attend(core, [[(tqT[:, toks(j)], tkT[:, 0:S], S, tkT[:, S:S + CTX], CTX, zero[:], vt[:T], vt[T:])]
                  for j in range(T)], TINY, [ot[:, j:j + 1, :] for j in range(T)])
    core.drop(tiny, tqT, tkT, zero)

    on = core.sb("near_out", [P, T, NAH * NAD])
    tiles = []
    for j in range(T):
        heads = []
        for h in range(NAH):
            p0, c = (h % 4) * NAD, h // 4
            pp = slice(p0, p0 + NAD)
            vh = [nv[:, t, h * NAD:(h + 1) * NAD] for t in range(TC)]
            bias = near_bias[:, h, 6 - 2 * j:14 - 2 * j, :].rearrange("p a b -> p (a b)")
            heads.append((nq[pp, c, toks(j)], nk[pp, c, 0:S], S, nk[pp, c, S:S + CTX], CTX, bias, vh[:T], vh[T:]))
        tiles.append(heads)
    attend(core, tiles, NAD, [on[:, j, :].rearrange("p (h d) -> p h d", h=NAH) for j in range(T)])
    core.drop(nq, nk, nv, near_bias)
    ga = core.sb("gate_a", [P, KD, S])
    gb = core.sb("gate_b", [P, KD, S])
    blocks = []
    for name, dst, at in (("b_ga", ga, 3776), ("b_gb", gb, 4800)):
        for b in range(2):
            blocks.append((dram_rows(a["w_in"], at + b * 512, at + (b + 1) * 512),
                           [features_unit(hT, KD, m, all_tok, "act",
                                          through(ACT.Sigmoid, dst[:, 4 * b + m, :], col(name, 4 * b + m)))
                            for m in range(4)]))
    project(core, blocks)
    core.drop(hT)
    otT = core.sb("tiny_outT", [TINY, S])
    onT = core.sb("near_outT", [P, 4, S])
    turn(core, [([(ot[:, t, :], t * P) for t in range(T)], copied(nc, otT[:], TINY, S))]
         + [([(on[:, t, c * P:(c + 1) * P], t * P) for t in range(T)], copied(nc, onT[:, c, :], P, S))
            for c in range(4)])
    core.drop(ot, on)

    ws = core.sb("sgu_w", [P, SGU_G, P])
    wo = core.sb("tiny_w_o", [TINY, D])
    bs = core.sb("sgu_b", [P, SGU_G, P])
    in_, mixed, out, link_sig = core.sig("sgu_in"), core.sig("sgu_mm"), core.sig("sgu_out"), core.sig("dve_chain")
    with core.psum("ps_sgu", [P, 2, S], F32) as ps, nc.Block() as block:
        @block.sync
        def _(sp):
            sp.dma_start(ws[:], a["sgu_w"]).then_inc(in_.sem, 16)
            sp.dma_start(wo[:], a["tiny_w_o"]).then_inc(in_.sem, 16)
            sp.dma_start(bs[:], a["sgu_b"].partition_broadcast(P)).then_inc(in_.sem, 16)

        @block.tensor
        def _(pe):
            pe.wait_ge(in_.sem, 48)
            for g in range(SGU_G):
                if g >= 2:
                    pe.wait_ge(out.sem, g - 1)
                for n in range(T):
                    nc.tensor.matmul(ps[:, g % 2, n * P:(n + 1) * P], v[:, n, g * P:(g + 1) * P], ws[:, g, :],
                                     start=n == 0, stop=False, skip_group_check=True)
                last = nc.tensor.matmul(ps[:, g % 2, :], wo[:, g * P:(g + 1) * P], otT[:], start=False, stop=True,
                                        skip_group_check=True)
                last.then_inc(mixed.sem, 1)

        @block.vector
        def _(dve):
            link = linked(dve, link_sig)
            dve.wait_ge(in_.sem, 48)
            for g in range(SGU_G):
                dve.wait_ge(mixed.sem, g + 1)
                p3 = ps[:, g % 2, :].rearrange("p (n q) -> p n q", n=T)
                link(nc.vector.tensor_tensor(p3, p3, bs[:, g, :].unsqueeze(1).to_broadcast([P, T, P]), ALU.add))
                nc.vector.tensor_tensor(u[:, g, :], ps[:, g % 2, :], u[:, g, :], ALU.mult).then_inc(out.sem, 1)
    core.drop(ws, wo, bs, otT, v)

    merge(core, ga, gb, (u, KD, a["w_up_a"]), (onT, 4, a["w_up_b"]))
    core.drop(u, onT, gb)

    def residual(t, sl):
        def evacuate(ps, link):
            link(nc.vector.tensor_tensor(ps, ps, keep["gate_mix_row"][:, sl], ALU.mult))
            return nc.vector.tensor_tensor(x[:, t, sl], x[:, t, sl], ps, ALU.add)
        return evacuate

    project(core, [(dram_rows(a["w_out"], b * 512, (b + 1) * 512),
                    [tokens_unit(ga, KD, toks(t), 512, "dve", residual(t, slice(b * 512, (b + 1) * 512)))
                     for t in range(T)]) for b in range(2)])
    core.drop(ga)


def load(core, pairs):
    done = core.sig("loaded")
    base = done.base
    with core.nc.Block() as block:
        @block.sync
        def _(sp):
            for dst, src in pairs:
                sp.dma_start(dst, src).then_inc(done.sem, 16)
            sp.wait_ge(done.sem, base + 16 * len(pairs))
    done.base += 16 * len(pairs)



def split(core, src, name, hi=None):
    nc = core.nc
    shape = [P, src.shape[1], src.shape[2]]
    hi = core.sb(name + "_hi", shape, F32R) if hi is None else hi
    lo = core.alias(src, name + "_lo", shape, F32R)
    hi_done, lo_done = core.sig("split_hi"), core.sig("split_lo")
    base = hi_done.base
    with nc.Block() as block:
        @block.scalar
        def _(act):
            for k in range(shape[1]):
                nc.scalar.activation(hi[:, k, :], src[:, k, :], ACT.Copy).then_inc(hi_done.sem, 1)

        @block.vector
        def _(dve):
            for k in range(shape[1]):
                dve.wait_ge(hi_done.sem, base + k + 1)
                nc.vector.tensor_tensor(lo[:, k, :], src[:, k, :], hi[:, k, :].bitcast(F32), ALU.subtract) \
                    .then_inc(lo_done.sem, 1)
    hi_done.base += shape[1]
    lo_done.base += shape[1]
    return hi, lo


def three_pass(nc, out, w_hi, w_lo, x_hi, x_lo, first, last):
    nc.tensor.matmul(out, w_hi, x_hi, start=first, stop=False)
    nc.tensor.matmul(out, w_hi, x_lo, start=False, stop=False)
    return nc.tensor.matmul(out, w_lo, x_hi, start=False, stop=last)


def experts(core, a, keep):
    nc = core.nc
    x = keep["x"]
    N = E + 1
    h2 = core.sb("h2T", [P, KD, S])
    norm_turned(core, [(P, x[:, t, :]) for t in range(T)], D, h2,
                [(0, T, 0, lambda k: keep["gain_ffn"][:, k:k + 1], lambda k: keep["shift_ffn"][:, k:k + 1])])

    sc = core.sb("router_scores", [P, T, E])
    sel = core.sb("router_sel", [P, 2, T, E])
    best = core.sb("router_best", [P, T, 8])
    total = core.sb("router_total", [P, 2, T])
    wt = core.sb("expert_weights", [P, T, N])
    brow = core.sb("router_bias", [P, E])
    load(core, [(brow[:], a["b_router"].partition_broadcast(P))])
    project(core, [(dram_rows(a["w_router"], 0, E),
                    [tokens_unit(h2, KD, slice(t * P, (t + 1) * P), E, "act",
                                 lambda ps, link, t=t: nc.scalar.activation(sc[:, t, :], ps, ACT.Sigmoid))
                     for t in range(T)])])
    with nc.Block() as block:
        @block.vector
        def _(dve):
            link = linked(dve, core.sig("dve_chain"))
            link(nc.vector.memset(wt[:], 1.0))
            link(nc.vector.tensor_tensor(sel[:, 0], sc[:], brow[:].unsqueeze(1).to_broadcast([P, T, E]), ALU.add))
            for t in range(T):
                link(nc.vector.max(best[:, t, :], sel[:, 0, t, :]))
                link(nc.vector.match_replace(sel[:, 1, t, :], best[:, t, :], sel[:, 0, t, :], NEG))
            link(nc.vector.tensor_tensor(sel[:, 0], sel[:, 0], sel[:, 1], ALU.not_equal))
            link(nc.vector.tensor_tensor(sc[:], sc[:], sel[:, 0], ALU.mult))
            link(nc.vector.tensor_reduce(total[:, 0, :], sc[:], AX, ALU.add))
            link(nc.vector.reciprocal(total[:, 1, :], total[:, 0, :]))
            for t in range(T):
                link(nc.vector.tensor_scalar(wt[:, t, 1:N], sc[:, t, :], total[:, 1, t:t + 1], 2.5, ALU.mult, ALU.mult))
    core.drop(sc, sel, best, total, brow)
    x_hi, x_lo = split(core, h2, "h2T")

    y = core.sb("y", [P, T, D])
    GU, DN = 2 * KD * FF, 2 * D
    gu = core.sb("gu", [P, 2, GU])
    gu_hi, gu_lo = core.sb("gu_hi", [P, 2, GU], F32R), core.alias(gu, "gu_lo", [P, 2, GU], F32R)
    dn = core.sb("dn", [P, 2, DN])
    dn_hi, dn_lo = core.sb("dn_hi", [P, 2, DN], F32R), core.alias(dn, "dn_lo", [P, 2, DN], F32R)
    sg, hg = core.sb("silu_gate", [P, 2, S]), core.sb("hidden", [P, 2, S])
    hg_hi, hg_lo = core.sb("hidden_hi", [P, 2, 2, S], F32R), core.sb("hidden_lo", [P, 2, 2, S], F32R)
    gu_in = [core.sig("gu_in_even"), core.sig("gu_in_odd")]
    dn_in = [core.sig("dn_in_even"), core.sig("dn_in_odd")]
    (gu_hi_done, gu_lo_done, dn_hi_done, dn_lo_done, gu_mm, dn_mm, silu_done, hidden_done, hidden_hi_done,
     hidden_lo_done, y_added) = (core.sig(n) for n in (
         "gu_hi_done", "gu_lo_done", "dn_hi_done", "dn_lo_done", "gu_mm", "dn_mm", "silu_done", "hidden_done",
         "hidden_hi_done", "hidden_lo_done", "y_added"))

    def weight(side, s, which, k, m):
        at = (which * KD + k) * FF + m * P
        return side[:, s, at:at + P]

    with (core.psum("ps_gate", [P, 2, S], F32) as ps_g, core.psum("ps_up", [P, 2, S], F32) as ps_u,
          core.psum("ps_down", [P, 4, S], F32) as ps_d, nc.Block() as block):
        def pairs(eng, lo, hi, step):
            n = lo
            with eng.Fori(0, (hi - lo) // 2) as i:
                for j in range(2):
                    step(2 * i + (n + j), (n + j) % 2)
            if (hi - lo) % 2:
                step(hi - 1, (hi - 1) % 2)

        @block.sync
        def _(sp):
            def load_gu(n, s, first=False):
                if not first:
                    sp.wait_ge(gu_mm.sem, 2 * n - 2)
                sp.dma_start(gu[:, s, :], a["e_gu"][bass.ds(n, 1)].rearrange("e p n -> (e p) n")) \
                    .then_inc(gu_in[s].sem, 16)

            def load_dn(n, s, first=False):
                if not first:
                    sp.wait_ge(dn_mm.sem, 8 * n - 8)
                sp.dma_start(dn[:, s, :], a["e_dn"][bass.ds(n, 1)].rearrange("e p n -> (e p) n")) \
                    .then_inc(dn_in[s].sem, 16)

            for n in range(2):
                load_gu(n, n, True)
                load_dn(n, n, True)

            def both(n, s):
                load_gu(n, s)
                load_dn(n, s)

            pairs(sp, 2, N, both)

        @block.scalar
        def _(act):
            def gu_high(n, s, half):
                act.wait_ge(gu_in[s].sem, half)
                nc.scalar.activation(gu_hi[:, s, :], gu[:, s, :], ACT.Copy).then_inc(gu_hi_done.sem, 1)

            def dn_high(n, s, half):
                act.wait_ge(dn_in[s].sem, half)
                nc.scalar.activation(dn_hi[:, s, :], dn[:, s, :], ACT.Copy).then_inc(dn_hi_done.sem, 1)

            def hidden(n, s, free):
                for m in range(2):
                    act.wait_ge(gu_mm.sem, 2 * n + (m + 1))
                    nc.scalar.activation(sg[:, m, :], ps_g[:, m, :], ACT.Silu).then_inc(silu_done.sem, 1)
                for m in range(2):
                    act.wait_ge(hidden_done.sem, 2 * n + (m + 1))
                    if free:
                        act.wait_ge(dn_mm.sem, 8 * n - 8)
                    nc.scalar.activation(hg_hi[:, s, m, :], hg[:, m, :], ACT.Copy).then_inc(hidden_hi_done.sem, 1)

            gu_high(0, 0, 16)
            gu_high(1, 1, 16)
            dn_high(0, 0, 16)
            hidden(0, 0, False)
            gu_high(2, 0, 32)
            dn_high(1, 1, 16)
            hidden(1, 1, False)
            gu_high(3, 1, 32)
            dn_high(2, 0, 32)
            with act.Fori(1, 31) as i:
                for s in range(2):
                    n = 2 * i + s
                    hidden(n, s, True)
                    gu_high(n, s, 16 * i + 32)
                    dn_high(n, 1 - s, 16 * i + 16 * (s + 1))
            hidden(62, 0, True)
            gu_high(64, 0, 16 * 33)
            dn_high(63, 1, 16 * 32)
            hidden(63, 1, True)
            dn_high(64, 0, 16 * 33)
            hidden(64, 0, True)

        @block.vector
        def _(dve):
            def gu_low(n, s):
                dve.wait_ge(gu_hi_done.sem, n + 1)
                nc.vector.tensor_tensor(gu_lo[:, s, :], gu[:, s, :], gu_hi[:, s, :].bitcast(F32), ALU.subtract) \
                    .then_inc(gu_lo_done.sem, 1)

            def dn_low(n, s):
                dve.wait_ge(dn_hi_done.sem, n + 1)
                nc.vector.tensor_tensor(dn_lo[:, s, :], dn[:, s, :], dn_hi[:, s, :].bitcast(F32), ALU.subtract) \
                    .then_inc(dn_lo_done.sem, 1)

            def hidden(n, s, before):
                for m in range(2):
                    dve.wait_ge(silu_done.sem, 2 * n + (m + 1))
                    if before:
                        dve.wait_ge(hidden_lo_done.sem, 2 * n + (m - 1))
                    nc.vector.tensor_tensor(hg[:, m, :], sg[:, m, :], ps_u[:, m, :], ALU.mult) \
                        .then_inc(hidden_done.sem, 1)
                for m in range(2):
                    dve.wait_ge(hidden_hi_done.sem, 2 * n + (m + 1))
                    nc.vector.tensor_tensor(hg_lo[:, s, m, :], hg[:, m, :], hg_hi[:, s, m, :].bitcast(F32),
                                            ALU.subtract).then_inc(hidden_lo_done.sem, 1)

            def add(n, first=False):
                for i in range(2 * T):
                    t, sl = i // 2, slice(i % 2 * S, (i % 2 + 1) * S)
                    dve.wait_ge(dn_mm.sem, 8 * n + (i + 1))
                    if first:
                        nc.vector.tensor_scalar(y[:, t, sl], ps_d[:, i % 4, :], wt[:, t, 0:1], None, ALU.mult) \
                            .then_inc(y_added.sem, 1)
                        continue
                    dve.wait_ge(y_added.sem, 8 * n + (i - 7))
                    nc.vector.scalar_tensor_tensor(y[:, t, sl], ps_d[:, i % 4, :], wt[:, t, bass.ds(n, 1)], y[:, t, sl],
                                                   ALU.mult, ALU.add).then_inc(y_added.sem, 1)

            gu_low(0, 0)
            gu_low(1, 1)
            dn_low(0, 0)
            hidden(0, 0, False)
            gu_low(2, 0)
            dn_low(1, 1)
            add(0, True)
            with dve.Fori(0, 31) as i:
                for j in range(1, 3):
                    n, s = 2 * i + j, j % 2
                    hidden(n, s, True)
                    gu_low(n + 2, s)
                    dn_low(n + 1, 1 - s)
                    add(n)
            hidden(63, 1, True)
            dn_low(64, 0)
            add(63)
            hidden(64, 0, True)
            add(64)

        @block.tensor
        def _(pe):
            def gate_up(n, s, before=True):
                pe.wait_ge(gu_lo_done.sem, n + 1)
                for m in range(2):
                    if before:
                        pe.wait_ge(hidden_done.sem, 2 * n + (m - 1))
                    for which, ps in ((0, ps_g), (1, ps_u)):
                        for k in range(KD):
                            last = three_pass(nc, ps[:, m, :], weight(gu_hi, s, which, k, m),
                                              weight(gu_lo, s, which, k, m), x_hi[:, k, :], x_lo[:, k, :],
                                              k == 0, k == KD - 1)
                    last.then_inc(gu_mm.sem, 1)

            def down(n, s, before=True):
                pe.wait_ge(hidden_lo_done.sem, 2 * n + 2)
                pe.wait_ge(dn_lo_done.sem, n + 1)
                for i in range(2 * T):
                    t, h = i // 2, i % 2
                    if before or i >= 4:
                        pe.wait_ge(y_added.sem, 8 * n + (i - 3))
                    for k in range(2):
                        at = k * D + h * S
                        last = three_pass(nc, ps_d[:, i % 4, :], hg_hi[:, s, k, t * P:(t + 1) * P],
                                          hg_lo[:, s, k, t * P:(t + 1) * P], dn_hi[:, s, at:at + S],
                                          dn_lo[:, s, at:at + S], k == 0, k == 1)
                    last.then_inc(dn_mm.sem, 1)

            gate_up(0, 0, False)
            gate_up(1, 1)
            down(0, 0, False)

            def both(n, s):
                gate_up(n + 1, 1 - s)
                down(n, s)

            pairs(pe, 1, N - 1, both)
            down(N - 1, (N - 1) % 2)
    core.drop(h2, x_hi, gu, gu_hi, dn, dn_hi, sg, hg, hg_hi, hg_lo, wt)

    row = core.sb("final_g", [P, D])
    load(core, [(row[:], a["final_norm_g"].partition_broadcast(P))])
    with nc.Block() as block:
        @block.vector
        def _(dve):
            link = linked(dve, core.sig("dve_chain"))
            for t in range(T):
                link(nc.vector.tensor_tensor(y[:, t, :], y[:, t, :], keep["gate_ffn_row"][:], ALU.mult))
                link(nc.vector.tensor_tensor(x[:, t, :], x[:, t, :], y[:, t, :], ALU.add))
    core.drop(y)
    normalise(core, [(P, x[:, t, :]) for t in range(T)], D, [x[:, t, :] for t in range(T)])
    with nc.Block() as block:
        @block.vector
        def _(dve):
            for t in range(T):
                nc.vector.tensor_tensor(x[:, t, :], x[:, t, :], row[:], ALU.mult)
    core.drop(row)



def second_mixer(core, a, keep):
    nc = core.nc
    x, cols = keep["x"], keep["cols"]
    TM = T + 1
    L = S + META
    rows = [P] * T + [META]
    toks = [slice(t * P, (t + 1) * P) for t in range(T)] + [slice(S, L)]
    all_tok = slice(0, S)

    def gains(name):
        at = COLS[name][0]
        return lambda k: cols[:, at + k:at + k + 1]

    meta = core.sb("meta", [META, D])
    load(core, [(meta[:], a["meta"])])
    hT = core.sb("hT_2", [P, KD, L])
    norm_turned(core, [(P, x[:, t, :]) for t in range(T)] + [(META, meta[:])], D, hT,
                [(0, T, 0, gains("g_mix_2"), None), (T, 1, S, gains("g_mix_2"), None)])
    core.drop(meta)

    def plain(dst, engine):
        if engine == "act":
            return lambda ps, link: nc.scalar.activation(dst, ps, ACT.Copy)
        return lambda ps, link: nc.vector.tensor_copy(dst, ps)

    def token_block(w, at, n, dst, d0, n_tiles, engine="dve", k_chunks=KD, src=None):
        src = hT if src is None else src
        return (dram_rows(w, at, at + n),
                [tokens_unit(src, k_chunks, toks[t], n, engine, plain(dst[0:rows[t], t, d0:d0 + n], engine))
                 for t in range(n_tiles)])

    cq, ckv = core.sb("c_q", [P, T, QL]), core.sb("c_kv", [P, TM, KVL + MROPE])
    w = a["w_in_2"]
    project(core, [token_block(w, 0, QL, cq, 0, T), token_block(w, QL, KVL + MROPE, ckv, 0, TM, "act")])
    cqT, ckvT = core.sb("c_qT", [P, QL // P, S]), core.sb("c_kvT", [P, KVL // P, L])
    norm_turned(core, [(P, cq[:, t, :]) for t in range(T)], QL, cqT, [(0, T, 0, gains("g_q_lora"), None)])
    norm_turned(core, [(rows[t], ckv[0:rows[t], t, 0:KVL]) for t in range(TM)], KVL, ckvT,
                [(0, T, 0, gains("g_kv_lora"), None), (T, 1, S, gains("g_kv_lora"), None)])
    q, kv = core.sb("mla_q", [P, T, MH, MQK]), core.sb("mla_kv", [P, TM, MH, P])
    kv_flat, q_flat = kv[:].rearrange("p t h d -> p t (h d)"), q[:].rearrange("p t h d -> p t (h d)")
    project(core, [token_block(a["w_uq"], b * QL, QL, q_flat, b * QL, T, k_chunks=3, src=cqT) for b in range(2)]
            + [token_block(a["w_ukv"], b * 512, 512, kv_flat, b * 512, TM, "act", k_chunks=2, src=ckvT)
               for b in range(2)])
    core.drop(cq, cqT, ckvT)

    kk = core.sb("mla_k", [P, TM, MH, MQK])
    g_rows = core.sb("g_qk", [P, 2, MQK])
    tab = core.sb("mla_rope", [P, 2, TM, MROPE // 2])
    sq = core.sb("mla_sq", [P, MH, MQK])
    t1, t2 = core.sb("t1", [P, MH, 16]), core.sb("t2", [P, MH, 16])
    rot = core.sb("rot", [P, MH, MROPE])
    st = core.sb("mla_stat", [P, 3, 2 * TM, MH])
    load(core, [(g_rows[:], a["g_qk"].partition_broadcast(P)), (tab[:], a["k_rope_mla"])])
    items = [(q, t, 0, t) for t in range(T)] + [(kk, t, 1, TM + t) for t in range(TM)]
    chain, var_done, root = core.sig("dve_chain"), core.sig("mla_var"), core.sig("root")
    b_root = root.base
    with nc.Block() as block:
        @block.vector
        def _(dve):
            link = linked(dve, chain)
            link(nc.vector.memset(st[:], 1.0))
            link(nc.vector.tensor_scalar(g_rows[:, 0, :], g_rows[:, 0, :], MQK ** -0.5, None, ALU.mult))
            for t in range(TM):
                r = slice(0, rows[t])
                link(nc.vector.tensor_copy(kk[r, t, :, 0:MNOPE], kv[r, t, :, 0:MNOPE]))
                link(nc.vector.tensor_copy(kk[r, t, :, MNOPE:MQK],
                                           ckv[r, t, KVL:].unsqueeze(1).to_broadcast([rows[t], MH, MROPE])))
            for src, t, _, i in items:
                r = slice(0, rows[t])
                link(nc.vector.tensor_tensor(sq[r], src[r, t], src[r, t], ALU.mult))
                link(nc.vector.tensor_reduce(st[r, 0, i, :], sq[r], AX, ALU.add))
            nc.vector.tensor_scalar(st[:, 1], st[:, 0], 1.0 / MQK, EPS, ALU.mult, ALU.add).then_inc(var_done.sem, 1)
            dve.wait_ge(root.sem, b_root + 1)
            link(nc.vector.reciprocal(st[:, 1], st[:, 2]))
            for src, t, which, i in items:
                r, n = slice(0, rows[t]), rows[t]
                link(nc.vector.tensor_tensor(src[r, t], src[r, t], st[r, 1, i, :].unsqueeze(2).to_broadcast([n, MH, MQK]),
                                             ALU.mult))
                link(nc.vector.tensor_tensor(src[r, t], src[r, t],
                                             g_rows[r, which, :].unsqueeze(1).to_broadcast([n, MH, MQK]), ALU.mult))
                cos, sin = (tab[r, j, t, :].unsqueeze(1).to_broadcast([n, MH, 16]) for j in range(2))
                rope(nc, link, src[r, t, :, MNOPE:MNOPE + 16], src[r, t, :, MNOPE + 16:MQK], cos, sin,
                     rot[r, :, 0:16], rot[r, :, 16:32], t1[r], t2[r])
                link(nc.vector.tensor_copy(src[r, t, :, MNOPE:MQK], rot[r]))

        @block.scalar
        def _(act):
            act.wait_ge(var_done.sem, 1)
            nc.scalar.activation(st[:, 2], st[:, 1], ACT.Sqrt).then_inc(root.sem, 1)
    root.base += 1
    core.drop(g_rows, tab, sq, t1, t2, rot, st, ckv)

    qT, kT, kmT = core.sb("mla_qT", [MQK, MH, S]), core.sb("mla_kT", [MQK, MH, S]), core.sb("mla_kmT", [MQK, MH, META])
    jobs = []
    for h in range(MH):
        jobs.append(([(q[:, t, h, :], t * P) for t in range(T)], copied(nc, qT[:, h, :], MQK, S)))
        jobs.append(([(kk[:, t, h, :], t * P) for t in range(T)], copied(nc, kT[:, h, :], MQK, S)))
    jobs.append(([(kk[0:META, T, h, :], h * META) for h in range(MH)],
                 copied(nc, kmT[:].rearrange("p h m -> p (h m)"), MQK, MH * META)))
    turn(core, jobs)
    core.drop(q, kk)
    causal = core.sb("causal", [P, S])
    load(core, [(causal[:], a["k_causal"])])
    om = core.sb("mla_out", [P, T, MH * MV])
    tiles = []
    for j in range(T):
        near = (j + 1) * P
        tiles.append([(qT[:, h, toks[j]], kT[:, h, 0:near], near, kmT[:, h, :], META, causal[:, S - near:S],
                       [kv[:, t, h, MNOPE:P] for t in range(j + 1)], [kv[0:META, T, h, MNOPE:P]]) for h in range(MH)])
    attend(core, tiles, MV, [om[:, j, :].rearrange("p (h d) -> p h d", h=MH) for j in range(T)])
    core.drop(qT, kT, kmT, kv, causal)
    omT = core.sb("mla_outT", [P, 4, S])
    turn(core, [([(om[:, t, c * P:(c + 1) * P], t * P) for t in range(T)], copied(nc, omT[:, c, :], P, S))
                for c in range(4)])
    core.drop(om)

    at = QL + KVL + MROPE
    RW = RH * RDK
    rq, rk = core.sb("ret_q", [P, T, RH, RDK]), core.sb("ret_k", [P, TM, RH, RDK])
    rv = core.sb("ret_v", [P, TM, RH * RDV])
    rq_flat, rk_flat = (r[:].rearrange("p t h d -> p t (h d)") for r in (rq, rk))
    project(core, [token_block(w, at, RW, rq_flat, 0, T), token_block(w, at + RW, RW, rk_flat, 0, TM, "act")]
            + [token_block(w, at + 2 * RW + b * 512, 512, rv, b * 512, TM, ("dve", "act")[b]) for b in range(2)])
    rqr, rkr = core.sb("ret_q_rope", [P, T, RH, RDK]), core.sb("ret_k_rope", [P, TM, RH, RDK])
    kz = core.sb("ret_kz", [P, TM, RH, RDK])
    tab = core.sb("ret_rope", [P, 2, TM, 32])
    zeta = core.sb("zeta", [P, 2, RH])
    t1, t2 = core.sb("t1", [P, RH, 32]), core.sb("t2", [P, RH, 32])
    load(core, [(tab[:], a["k_rope_ret"]), (zeta[:], a["k_zeta"])])
    with nc.Block() as block:
        @block.vector
        def _(dve):
            link = linked(dve, chain)
            for src, dst, n_tiles in ((rq, rqr, T), (rk, rkr, TM)):
                for t in range(n_tiles):
                    r, n = slice(0, rows[t]), rows[t]
                    cos, sin = (tab[r, j, t, :].unsqueeze(1).to_broadcast([n, RH, 32]) for j in range(2))
                    rope(nc, link, src[r, t, :, 0:32], src[r, t, :, 32:64], cos, sin, dst[r, t, :, 0:32],
                         dst[r, t, :, 32:64], t1[r], t2[r])
            for t in range(TM):
                r, n = slice(0, rows[t]), rows[t]
                link(nc.vector.tensor_scalar(rkr[r, t], rkr[r, t], RDK ** -0.5, None, ALU.mult))
                link(nc.vector.tensor_tensor(kz[r, t], rkr[r, t],
                                             zeta[r, t // T, :].unsqueeze(2).to_broadcast([n, RH, RDK]), ALU.mult))
    core.drop(rq, rk, tab, zeta, t1, t2)
    rqT, rkT = core.sb("ret_qT", [P, 4, S]), core.sb("ret_kT", [P, 4, S])
    jobs = []
    for c in range(4):
        for src, dst in ((rqr, rqT), (rkr, rkT)):
            jobs.append(([(src[:, t, 2 * c:2 * c + 2, :].rearrange("p h d -> p (h d)"), t * P) for t in range(T)],
                         copied(nc, dst[:, c, :], P, S)))
    turn(core, jobs)
    core.drop(rqr, rkr)
    qx = core.sb("ret_qx", [P, 4, S])
    decay = core.sb("decay", [P, 2, 4, P])
    xi = core.sb("xi", [P, 4, P])
    gamma = core.sb("gamma", [P, 4])
    state = core.sb("state", [P, 4, 2, P])
    prod = core.sb("state_decayed", [P, 4, P])
    sd = core.sb("ret_scores", [P, 2, 4, P])
    ry = core.sb("ret_y", [P, T, RH * RDV])
    load(core, [(decay[:], a["k_decay"]), (xi[:], a["k_xi"]), (gamma[:], a["k_gamma"])])
    scored, kv_mm, y_mm, decayed, state_done, y_out = (core.sig(n) for n in (
        "ret_scored", "ret_kv_mm", "ret_y_mm", "ret_decayed", "ret_state", "ret_y_out"))
    with (core.psum("ps_rs", [P, 2, 4, P], F32) as ps_s, core.psum("ps_kv", [P, 4, P], F32) as ps_kv,
          core.psum("ps_ry", [P, 2, 512], F32) as ps_y, nc.Block() as block):
        @block.tensor
        def _(pe):
            pe.wait_ge(decayed.sem, 1)
            for n in range(T):
                src, r = (T, slice(0, META)) if n == 0 else (n - 1, slice(0, P))
                if n >= 1:
                    pe.wait_ge(state_done.sem, n)
                    pe.wait_ge(decayed.sem, n + 1)
                for h in range(RH):
                    c, p0 = h // 2, h % 2 * RDK
                    last = nc.tensor.matmul(ps_kv[p0:p0 + RDK, c, :], kz[r, src, h, :],
                                            rv[r, src, h * RDV:(h + 1) * RDV], start=True, stop=True)
                last.then_inc(kv_mm.sem, 1)
                for h in range(RH):
                    c, p0 = h // 2, h % 2 * RDK
                    last = nc.tensor.matmul(ps_s[:, h % 2, c, :], rkT[p0:p0 + RDK, c, toks[n]],
                                            rqT[p0:p0 + RDK, c, toks[n]], start=True, stop=True)
                last.then_inc(scored.sem, 1)
                pe.wait_ge(state_done.sem, n + 1)
                pe.wait_ge(decayed.sem, n + 2)
                if n >= 1:
                    pe.wait_ge(y_out.sem, n)
                for h in range(RH):
                    c, hv = h // 2, slice(h % 4 * RDV, (h % 4 + 1) * RDV)
                    nc.tensor.matmul(ps_y[:, h // 4, hv], sd[:, h % 2, c, :], rv[:, n, h * RDV:(h + 1) * RDV],
                                     start=True, stop=False)
                    last = nc.tensor.matmul(ps_y[:, h // 4, hv], qx[:, c, toks[n]], state[:, c, h % 2, :],
                                            start=False, stop=True)
                last.then_inc(y_mm.sem, 1)

        @block.vector
        def _(dve):
            link = linked(dve, chain)
            link(nc.vector.memset(state[:], 0.0))
            for c in range(4):
                ins = nc.vector.tensor_tensor(qx[:, c, :].rearrange("p (t m) -> p t m", t=T),
                                              rqT[:, c, :].rearrange("p (t m) -> p t m", t=T),
                                              xi[:, c, :].unsqueeze(1).to_broadcast([P, T, P]), ALU.mult)
                if c < 3:
                    link(ins)
            ins.then_inc(decayed.sem, 1)
            for n in range(T):
                dve.wait_ge(kv_mm.sem, n + 1)
                if n >= 1:
                    dve.wait_ge(y_mm.sem, n)
                for half in range(2):
                    pp = slice(half * RDK, (half + 1) * RDK)
                    if n == 0:
                        link(nc.vector.tensor_copy(state[pp, :, half, :], ps_kv[pp]))
                    else:
                        link(nc.vector.tensor_tensor(prod[pp], state[pp, :, half, :],
                                                     gamma[pp, :].unsqueeze(2).to_broadcast([RDK, 4, P]), ALU.mult))
                        link(nc.vector.tensor_tensor(state[pp, :, half, :], prod[pp], ps_kv[pp], ALU.add))
                dve.sem_inc(state_done.sem, 1)
                dve.wait_ge(scored.sem, n + 1)
                link(nc.vector.tensor_tensor(sd[:, 0], ps_s[:, 0], decay[:, 0], ALU.mult))
                nc.vector.tensor_tensor(sd[:, 1], ps_s[:, 1], decay[:, 1], ALU.mult).then_inc(decayed.sem, 1)

        @block.scalar
        def _(act):
            for n in range(T):
                act.wait_ge(y_mm.sem, n + 1)
                nc.scalar.activation(ry[:, n, :], ps_y[:].rearrange("p a b -> p (a b)"), ACT.Copy) \
                    .then_inc(y_out.sem, 1)
    core.drop(kz, rqT, rkT, rv, qx, decay, xi, gamma, state, prod, sd)

    rg = core.sb("ret_gate", [P, T, RH * RDV])
    at += 2 * RW + RH * RDV
    project(core, [(dram_rows(w, at + b * 512, at + (b + 1) * 512),
                    [tokens_unit(hT, KD, toks[t], 512, "act",
                                 lambda ps, link, t=t, b=b: nc.scalar.activation(rg[:, t, b * 512:(b + 1) * 512], ps,
                                                                                 ACT.Silu)) for t in range(T)])
                   for b in range(2)])
    g_gn = core.sb("g_ret", [P, RH * RDV])
    st = core.sb("gn_stats", [P, T * RH, 6])
    ag = core.sb("gn_mean_var", [P, T * RH, 4])
    load(core, [(g_gn[:], a["g_ret_gn"].partition_broadcast(P))])
    b_root = root.base
    gn_var = core.sig("gn_var")
    with nc.Block() as block:
        @block.vector
        def _(dve):
            link = linked(dve, chain)
            for i in range(T * RH):
                t, hv = i // RH, slice(i % RH * RDV, (i % RH + 1) * RDV)
                link(nc.vector.bn_stats(st[:, i, :], ry[:, t, hv]))
                link(nc.vector.bn_aggr(ag[:, i, 0:2], st[:, i, :]))
            nc.vector.tensor_scalar(ag[:, :, 1:2], ag[:, :, 1:2], EPS, None, ALU.add).then_inc(gn_var.sem, 1)
            for t in range(T):
                link(nc.vector.tensor_tensor(rg[:, t, :], rg[:, t, :], g_gn[:], ALU.mult))
            dve.wait_ge(root.sem, b_root + 1)
            link(nc.vector.reciprocal(ag[:, :, 3:4], ag[:, :, 2:3]))
            for i in range(T * RH):
                t, hv = i // RH, slice(i % RH * RDV, (i % RH + 1) * RDV)
                link(nc.vector.tensor_scalar(ry[:, t, hv], ry[:, t, hv], ag[:, i, 0:1], ag[:, i, 3:4], ALU.subtract,
                                             ALU.mult))
            for t in range(T):
                link(nc.vector.tensor_tensor(ry[:, t, :], ry[:, t, :], rg[:, t, :], ALU.mult))

        @block.scalar
        def _(act):
            act.wait_ge(gn_var.sem, 1)
            nc.scalar.activation(ag[:, :, 2:3], ag[:, :, 1:2], ACT.Sqrt).then_inc(root.sem, 1)
    root.base += 1
    core.drop(rg, g_gn, st, ag)
    yT = core.sb("ret_yT", [P, KD, S])
    turn(core, [([(ry[:, t, c * P:(c + 1) * P], t * P) for t in range(T)], copied(nc, yT[:, c, :], P, S))
                for c in range(KD)])
    core.drop(ry)

    za, zr = core.sb("gate_za", [P, KD, S]), core.sb("gate_zr", [P, KD, S])
    at += RH * RDV
    blocks = []
    for dst, c0 in ((za, at), (zr, at + D)):
        for b in range(2):
            blocks.append((dram_rows(w, c0 + b * 512, c0 + (b + 1) * 512),
                           [features_unit(hT, KD, m, all_tok, "act",
                                          lambda ps, link, d=dst[:, 4 * b + m, :]: nc.scalar.activation(d, ps, ACT.Sigmoid))
                            for m in range(4)]))
    project(core, blocks)
    core.drop(hT)
    merge(core, za, zr, (omT, 4, a["w_mla_out"]), (yT, KD, a["w_ret_out"]))
    core.drop(omT, yT, zr)
    project(core, [(dram_rows(a["w_mix_out"], b * 512, (b + 1) * 512),
                    [tokens_unit(za, KD, toks[t], 512, "dve",
                                 lambda ps, link, d=x[:, t, b * 512:(b + 1) * 512]:
                                 nc.vector.tensor_tensor(d, d, ps, ALU.add)) for t in range(T)]) for b in range(2)])
    core.drop(za)


def merge(core, ga, gb, first, second):
    nc = core.nc

    def gated(m):
        return lambda ps, link: nc.vector.tensor_tensor(ga[:, m, :], ps, ga[:, m, :], ALU.mult)

    def gated_sum(m):
        def evacuate(ps, link):
            link(nc.vector.tensor_tensor(gb[:, m, :], ps, gb[:, m, :], ALU.mult))
            return nc.vector.tensor_tensor(ga[:, m, :], ga[:, m, :], gb[:, m, :], ALU.add)
        return evacuate

    blocks = []
    for (src, k_chunks, w), evacuate in ((first, gated), (second, gated_sum)):
        for b in range(2):
            blocks.append((dram_rows(w, b * 512, (b + 1) * 512),
                           [features_unit(src, k_chunks, m, slice(0, S), "dve", evacuate(4 * b + m))
                            for m in range(4)]))
    project(core, blocks)



GE = 2
NG = PNK // GE


def peer(core, a, keep, scratch):
    nc = core.nc
    x, cols, ident = keep["x"], keep["cols"], core.ident
    hT = core.sb("peer_xT", [P, KD, S])
    x_hi = core.sb("peer_xT_hi", [P, KD, S], F32R)
    chT = core.sb("chosenT", [P, 3, S])
    g0 = COLS["g_ffn_2"][0]
    norm_turned(core, [(P, x[:, t, :]) for t in range(T)], D, hT, [(0, T, 0, lambda k: cols[:, g0 + k:g0 + k + 1], None)])
    qT = core.sb("peer_qT", [P, PH, S])
    project(core, [(dram_rows(a["w_peer_q"], b * 512, (b + 1) * 512),
                    [features_unit(hT, KD, m, slice(0, S), ("act", "dve")[m % 2],
                                   (lambda ps, link, d=qT[:, 4 * b + m, :]: nc.scalar.activation(d, ps, ACT.Copy))
                                   if m % 2 == 0 else
                                   (lambda ps, link, d=qT[:, 4 * b + m, :]: nc.vector.tensor_copy(d, ps)))
                     for m in range(4)]) for b in range(2)])
    x_hi, x_lo = split(core, hT, "peer_xT", x_hi)

    keys = core.sb("keys", [P, 2 * PNK])
    s = core.sb("key_scores", [P, 2, 2 * PNK])
    less = core.sb("less", [P, 2 * PNK])
    val = core.sb("top_val", [P, 2, PK])
    index = core.sb("top_index", [P, T, 2, PH, PK], U32)
    cand = core.sb("cand", [P, PK, PK])
    best = core.sb("best", [P, T, PH, PK])
    best_at = core.sb("best_at", [P, T, PH, PK], U32)
    keys_in, clear = core.sig("keys_in"), core.sig("keys_clear")
    key_mm, key_out, taken, chain = core.sig("key_mm"), core.sig("key_out"), core.sig("key_taken"), core.sig("dve_chain")
    NT = PH * T
    with core.psum("ps_key", [P, 2, S], F32) as ps, nc.Block() as block:
        @block.sync
        def _(sp):
            sp.wait_ge(clear.sem, 1)
            for j in range(2):
                sp.dma_start(keys[j * 64:(j + 1) * 64, j * PNK:(j + 1) * PNK], a["keys"][j]).then_inc(keys_in.sem, 16)

        @block.tensor
        def _(pe):
            pe.wait_ge(keys_in.sem, 32)
            for n in range(NT):
                if n >= 2:
                    pe.wait_ge(key_out.sem, n - 1)
                t, h = n // PH, n % PH
                nc.tensor.matmul(ps[:, n % 2, 0:2 * PNK], qT[:, h, t * P:(t + 1) * P], keys[:], start=True,
                                 stop=True).then_inc(key_mm.sem, 1)

        @block.scalar
        def _(act):
            for n in range(NT):
                act.wait_ge(key_mm.sem, n + 1)
                if n >= 2:
                    act.wait_ge(taken.sem, n - 1)
                nc.scalar.activation(s[:, n % 2, :], ps[:, n % 2, 0:2 * PNK], ACT.Copy).then_inc(key_out.sem, 1)

        @block.vector
        def _(dve):
            link = linked(dve, chain)

            def top16(src, spare, values, places):
                link(nc.vector.max(values[:, 0:8], src))
                link(nc.vector.max_index(places[:, 0:8], values[:, 0:8], src))
                link(nc.vector.match_replace(spare, values[:, 0:8], src, NEG))
                link(nc.vector.max(values[:, 8:16], spare))
                link(nc.vector.max_index(places[:, 8:16], values[:, 8:16], spare))

            nc.vector.memset(keys[:], 0.0).then_inc(clear.sem, 1)
            for n in range(NT):
                t, h = n // PH, n % PH
                dve.wait_ge(key_out.sem, n + 1)
                for j in range(2):
                    top16(s[:, n % 2, j * PNK:(j + 1) * PNK], less[:, 0:PNK], val[:, j, :], index[:, t, j, h, :])
                ins = nc.vector.tensor_tensor(cand[:], val[:, 0, :].unsqueeze(2).to_broadcast([P, PK, PK]),
                                              val[:, 1, :].unsqueeze(1).to_broadcast([P, PK, PK]), ALU.add)
                ins.then_inc(taken.sem, 1)
                dve.wait_ge(taken.sem, n + 1)
                top16(cand[:].rearrange("p a b -> p (a b)"), less[:], best[:, t, h, :], best_at[:, t, h, :])
    core.drop(keys, s, less, val, cand, qT)

    at = core.sb("at", [P, 2, PH, PK], U32)
    atf = core.sb("at_f", [P, 2, PH, PK])
    indexf = core.sb("index_f", [P, 2, PH, PK])
    iota = core.sb("iota16", [P, PK])
    hot = core.sb("hot", [P, PH, PK, PK])
    chosen = core.sb("chosen", [P, 3, T, PH, PK])
    gsum = core.sb("gate_sum", [P, 2, PH])
    load(core, [(iota[:], a["k_iota"][:, 0:PK])])
    shifted, exped = core.sig("gate_shifted"), core.sig("gate_exped")
    with nc.Block() as block:
        @block.vector
        def _(dve):
            link = linked(dve, chain)
            for t in range(T):
                ins = nc.vector.tensor_tensor(chosen[:, 2, t], best[:, t],
                                              best[:, t, :, 0:1].to_broadcast([P, PH, PK]), ALU.subtract)
                ins.then_inc(shifted.sem, 1)
            for t in range(T):
                link(nc.vector.tensor_single_scalar(at[:, 0], best_at[:, t], 4, ALU.logical_shift_right))
                link(nc.vector.tensor_single_scalar(at[:, 1], best_at[:, t], PK - 1, ALU.bitwise_and))
                link(nc.vector.tensor_copy(atf[:], at[:]))
                link(nc.vector.tensor_copy(indexf[:], index[:, t]))
                for j in range(2):
                    for h in range(PH):
                        link(nc.vector.tensor_tensor(hot[:, h], atf[:, j, h, :].unsqueeze(2).to_broadcast([P, PK, PK]),
                                                     iota[:].unsqueeze(1).to_broadcast([P, PK, PK]), ALU.is_equal))
                    for h in range(PH):
                        link(nc.vector.tensor_tensor(hot[:, h], hot[:, h],
                                                     indexf[:, j, h, :].unsqueeze(1).to_broadcast([P, PK, PK]),
                                                     ALU.mult))
                    link(nc.vector.tensor_reduce(chosen[:, j, t], hot[:], AX, ALU.add))
                dve.wait_ge(exped.sem, t + 1)
                link(nc.vector.tensor_reduce(gsum[:, 0], chosen[:, 2, t], AX, ALU.add))
                link(nc.vector.reciprocal(gsum[:, 1], gsum[:, 0]))
                link(nc.vector.tensor_tensor(chosen[:, 2, t], chosen[:, 2, t],
                                             gsum[:, 1].unsqueeze(2).to_broadcast([P, PH, PK]), ALU.mult))

        @block.scalar
        def _(act):
            for t in range(T):
                act.wait_ge(shifted.sem, t + 1)
                nc.scalar.activation(chosen[:, 2, t], chosen[:, 2, t], ACT.Exp).then_inc(exped.sem, 1)
    turn(core, [([(chosen[:, j, t].rearrange("p h k -> p (h k)"), t * P) for t in range(T)],
                 copied(nc, chT[:, j, :], P, S)) for j in range(3)])
    core.drop(at, atf, indexf, iota, hot, chosen, gsum, index, best, best_at)

    place_gates(core, a, chT, scratch["gates"])
    core.drop(chT)
    peer_products(core, a, x, x_hi, x_lo, scratch["gates"])
    core.drop(hT, x_hi)


def place_gates(core, a, chT, gates):
    nc = core.nc
    B = 4
    NB = P // B
    iota = core.sb("iota", [P, PNK])
    hot1, hot2 = core.sb("hot_e1", [P, 2, B, PNK]), core.sb("hot_e2", [P, 2, B, PNK])
    tile = core.sb("gate_tile", [P, 2, PNK, P])
    iota_in, hot1_done, hot2_done, gate_mm, gate_out = (core.sig(n) for n in (
        "iota_in", "hot1_done", "hot2_done", "gate_mm", "gate_out"))
    gates_out = [core.sig("gates_stored_even"), core.sig("gates_stored_odd")]
    with core.psum("ps_gates", [P, 2, B, PNK], F32) as ps, nc.Block() as block:
        @block.sync
        def _(sp):
            sp.dma_start(iota[:], a["k_iota"]).then_inc(iota_in.sem, 16)
            for t in range(T):
                sp.wait_ge(gate_out.sem, NB * (t + 1))
                sp.dma_start(gates[:, :, t * P:(t + 1) * P], tile[:, t % 2]).then_inc(gates_out[t % 2].sem, 16)
            for s in range(2):
                sp.wait_ge(gates_out[s].sem, 16 * T // 2)

        def steps(eng, step, loop_from=1):
            for b in range(2 * loop_from):
                step(b, b % 2, True)
            with eng.Fori(loop_from, S // B // 2) as i:
                for s in range(2):
                    step(2 * i + s, s, False)

        @block.vector
        def _(dve):
            dve.wait_ge(iota_in.sem, 16)

            def step(b, s, first):
                if not first:
                    dve.wait_ge(gate_mm.sem, b - 1)
                nc.vector.tensor_tensor(hot1[:, s], iota[:].unsqueeze(1).to_broadcast([P, B, PNK]),
                                        chT[:, 0, bass.ds(b * B, B)].unsqueeze(2).to_broadcast([P, B, PNK]),
                                        ALU.is_equal).then_inc(hot1_done.sem, 1)
                for i in range(B):
                    last = nc.vector.tensor_scalar(hot2[:, s, i], iota[:], chT[:, 1, bass.ds(b * B + i, 1)],
                                                   chT[:, 2, bass.ds(b * B + i, 1)], ALU.is_equal, ALU.mult)
                last.then_inc(hot2_done.sem, 1)

            steps(dve, step)

        @block.tensor
        def _(pe):
            def step(b, s, first):
                pe.wait_ge(hot1_done.sem, b + 1)
                pe.wait_ge(hot2_done.sem, b + 1)
                if not first:
                    pe.wait_ge(gate_out.sem, b - 1)
                for i in range(B):
                    last = nc.tensor.matmul(ps[:, s, i], hot1[:, s, i], hot2[:, s, i], start=True, stop=True)
                last.then_inc(gate_mm.sem, 1)

            steps(pe, step)

        @block.scalar
        def _(act):
            for t in range(T):
                if t >= 2:
                    act.wait_ge(gates_out[t % 2].sem, 16 * (t // 2))
                with act.Fori(0, NB // 2) as i:
                    for s in range(2):
                        act.wait_ge(gate_mm.sem, 2 * i + (NB * t + s + 1))
                        nc.scalar.activation(tile[:, t % 2, :, bass.ds((2 * i + s) * B, B)],
                                             ps[:, s].rearrange("p b e -> p e b"), ACT.Copy).then_inc(gate_out.sem, 1)
    core.drop(iota, hot1, hot2, tile)


def peer_products(core, a, x, x_hi, x_lo, gates):
    nc = core.nc
    W = GE * D
    u = core.sb("u", [P, 2, W])
    u_hi, u_lo = core.sb("u_hi", [P, 2, W], F32R), core.alias(u, "u_lo", [P, 2, W], F32R)
    v = core.sb("v", [P, 2, W])
    v_hi, v_lo = core.sb("v_hi", [P, 2, W], F32R), core.alias(v, "v_lo", [P, 2, W], F32R)
    g = core.sb("g", [P, 2, GE, S])
    act_out = core.sb("act_out", [P, GE, S])
    c_hi, c_lo = core.sb("coef_hi", [P, 2, GE, S], F32R), core.sb("coef_lo", [P, 2, GE, S], F32R)
    u_in, v_in, g_in = ([core.sig(f"peer_{n}_even"), core.sig(f"peer_{n}_odd")] for n in "uvg")
    (u_hi_done, u_lo_done, v_hi_done, v_lo_done, u_mm, v_mm, gelu_done, coef_done, coef_hi_done, coef_lo_done,
     added) = (core.sig("peer_" + n) for n in ("u_hi_done", "u_lo_done", "v_hi_done", "v_lo_done", "u_mm", "v_mm",
                                              "gelu_done", "coef_done", "coef_hi_done", "coef_lo_done", "added"))
    with (core.psum("ps_act", [P, 4, S], F32) as ps_a, core.psum("ps_y", [P, 4, S], F32) as ps_y,
          nc.Block() as block):
        @block.sync
        def _(sp):
            def loads(n, s, first):
                def part(src):
                    return src[bass.ds(n, 1)].rearrange("g p n -> (g p) n")
                if not first:
                    sp.wait_ge(u_mm.sem, GE * n - GE)
                sp.dma_start(u[:, s, :], part(a["peer_u"])).then_inc(u_in[s].sem, 16)
                if not first:
                    sp.wait_ge(coef_done.sem, GE * n - GE)
                sp.dma_start(g[:, s].rearrange("p j t -> p (j t)"),
                             part(gates.rearrange("p (g j) t -> g p (j t)", j=GE))).then_inc(g_in[s].sem, 16)
                if not first:
                    sp.wait_ge(v_mm.sem, 8 * n - 8)
                sp.dma_start(v[:, s, :], part(a["peer_v"])).then_inc(v_in[s].sem, 16)

            for n in range(2):
                loads(n, n, True)
            with sp.Fori(1, NG // 2) as i:
                for s in range(2):
                    loads(2 * i + s, s, False)

        @block.scalar
        def _(act):
            def high(dst, src, arrived, value, s, done):
                act.wait_ge(arrived[s].sem, value)
                nc.scalar.activation(dst[:, s, :], src[:, s, :], ACT.Copy).then_inc(done.sem, 1)

            def coefficients(n, s, first):
                for j in range(GE):
                    act.wait_ge(u_mm.sem, GE * n + (j + 1))
                    if not (first and n == 0):
                        act.wait_ge(coef_lo_done.sem, GE * n + (j + 1 - GE))
                    nc.scalar.activation(act_out[:, j, :], ps_a[:, 2 * s + j, :], ACT.Gelu).then_inc(gelu_done.sem, 1)
                for j in range(GE):
                    act.wait_ge(coef_done.sem, GE * n + (j + 1))
                    if not first:
                        act.wait_ge(v_mm.sem, 8 * n - 8)
                    nc.scalar.activation(c_hi[:, s, j, :], act_out[:, j, :], ACT.Copy).then_inc(coef_hi_done.sem, 1)

            high(u_hi, u, u_in, 16, 0, u_hi_done)
            high(u_hi, u, u_in, 16, 1, u_hi_done)
            high(v_hi, v, v_in, 16, 0, v_hi_done)
            for n in range(2):
                coefficients(n, n, True)
                high(u_hi, u, u_in, 32, n, u_hi_done)
                high(v_hi, v, v_in, 16 if n == 0 else 32, 1 - n, v_hi_done)
            with act.Fori(1, NG // 2 - 1) as i:
                for s in range(2):
                    coefficients(2 * i + s, s, False)
                    high(u_hi, u, u_in, 16 * i + 32, s, u_hi_done)
                    high(v_hi, v, v_in, 16 * i + 16 * (s + 1), 1 - s, v_hi_done)
            coefficients(NG - 2, 0, False)
            high(v_hi, v, v_in, 16 * (NG // 2), 1, v_hi_done)
            coefficients(NG - 1, 1, False)

        @block.vector
        def _(dve):
            def low(n, s, lo, raw, hi, hi_done, done):
                dve.wait_ge(hi_done.sem, n + 1)
                nc.vector.tensor_tensor(lo[:, s, :], raw[:, s, :], hi[:, s, :].bitcast(F32), ALU.subtract) \
                    .then_inc(done.sem, 1)

            def coefficients(n, s, arrived):
                dve.wait_ge(g_in[s].sem, arrived)
                for j in range(GE):
                    dve.wait_ge(gelu_done.sem, GE * n + (j + 1))
                    nc.vector.tensor_tensor(act_out[:, j, :], act_out[:, j, :], g[:, s, j, :], ALU.mult) \
                        .then_inc(coef_done.sem, 1)
                for j in range(GE):
                    dve.wait_ge(coef_hi_done.sem, GE * n + (j + 1))
                    nc.vector.tensor_tensor(c_lo[:, s, j, :], act_out[:, j, :], c_hi[:, s, j, :].bitcast(F32),
                                            ALU.subtract).then_inc(coef_lo_done.sem, 1)

            def add(n, first):
                for i in range(2 * T):
                    t, sl = i // 2, slice(i % 2 * S, (i % 2 + 1) * S)
                    dve.wait_ge(v_mm.sem, 8 * n + (i + 1))
                    if not (first and n == 0):
                        dve.wait_ge(added.sem, 8 * n + (i - 7))
                    nc.vector.tensor_tensor(x[:, t, sl], x[:, t, sl], ps_y[:, i % 4, :], ALU.add) \
                        .then_inc(added.sem, 1)

            def u_low(n, s):
                low(n, s, u_lo, u, u_hi, u_hi_done, u_lo_done)

            def v_low(n, s):
                low(n, s, v_lo, v, v_hi, v_hi_done, v_lo_done)

            u_low(0, 0)
            u_low(1, 1)
            v_low(0, 0)
            for n in range(2):
                coefficients(n, n, 16)
                u_low(n + 2, n)
                v_low(n + 1, 1 - n)
                add(n, True)
            with dve.Fori(1, NG // 2 - 1) as i:
                for s in range(2):
                    n = 2 * i + s
                    coefficients(n, s, 16 * i + 16)
                    u_low(n + 2, s)
                    v_low(n + 1, 1 - s)
                    add(n, False)
            coefficients(NG - 2, 0, 16 * (NG // 2))
            v_low(NG - 1, 1)
            add(NG - 2, False)
            coefficients(NG - 1, 1, 16 * (NG // 2))
            add(NG - 1, False)

        @block.tensor
        def _(pe):
            def activations(n, s, first=False):
                pe.wait_ge(u_lo_done.sem, n + 1)
                for j in range(GE):
                    if not first:
                        pe.wait_ge(gelu_done.sem, GE * n + (j + 1 - 2 * GE))
                    for k in range(KD):
                        at = (j * KD + k) * P
                        last = three_pass(nc, ps_a[:, 2 * s + j, :], u_hi[:, s, at:at + P], u_lo[:, s, at:at + P],
                                          x_hi[:, k, :], x_lo[:, k, :], k == 0, k == KD - 1)
                    last.then_inc(u_mm.sem, 1)

            def values(n, s, first=False):
                pe.wait_ge(coef_lo_done.sem, GE * n + GE)
                pe.wait_ge(v_lo_done.sem, n + 1)
                for i in range(2 * T):
                    t, h = i // 2, i % 2
                    if not first or i >= 4:
                        pe.wait_ge(added.sem, 8 * n + (i - 3))
                    for j in range(GE):
                        at = j * D + h * S
                        last = three_pass(nc, ps_y[:, i % 4, :], c_hi[:, s, j, t * P:(t + 1) * P],
                                          c_lo[:, s, j, t * P:(t + 1) * P], v_hi[:, s, at:at + S],
                                          v_lo[:, s, at:at + S], j == 0, j == GE - 1)
                    last.then_inc(v_mm.sem, 1)

            activations(0, 0, True)
            activations(1, 1, True)
            values(0, 0, True)
            activations(2, 0)
            values(1, 1)
            with pe.Fori(1, NG // 2 - 1) as i:
                for s in range(2):
                    activations(2 * i + (s + 1), 1 - s)
                    values(2 * i + s, s)
            activations(NG - 1, 1)
            values(NG - 2, 0)
            values(NG - 1, 1)
    core.drop(u, u_hi, v, v_hi, g, act_out, c_hi, c_lo)



def build(nc, a, out, scratch):
    with ExitStack() as stack:
        core = Core(nc, stack)
        keep = {}
        for name, shape in (("ident", [P, P]), ("ones", [P, P]), ("cols", [P, N_COLS]), ("x", [P, T, D]),
                            ("gain_mix", [P, 2, KD]), ("shift_mix", [P, 2, KD]), ("gain_ffn", [P, KD]),
                            ("shift_ffn", [P, KD]), ("gate_mix_row", [P, D]), ("gate_ffn_row", [P, D])):
            keep[name] = core.sb(name, shape)
        core.ident = keep["ident"]
        load_constants(core, a, keep)
        modulation(core, a, keep)
        first_mixer(core, a, keep)
        experts(core, a, keep)
        second_mixer(core, a, keep)
        core.drop(*(keep[n] for n in ("ones", "gate_mix_row", "gate_ffn_row")))
        peer(core, a, keep, scratch)
        store(core, out, keep["x"])


def store(core, out, x):
    done = core.sig("stored")
    with core.nc.Block() as block:
        @block.sync
        def _(sp):
            sp.dma_start(out.rearrange("(t p) d -> p t d", p=P), x[:]).then_inc(done.sem, 16)
            sp.wait_ge(done.sem, 16)


def kernel(**inputs):
    import numpy as np
    import concourse.bacc as bacc
    from concourse.bass_utils import run_bass_kernel_spmd as run

    one = {n: np.asarray(v)[0] if n not in ("c_ctx", "final_norm_g", "meta_tokens_2") else np.asarray(v)
           for n, v in inputs.items()}

    def cols(v):
        return v.reshape(-1, P).T

    b_in = one["b_in"]
    parts = {"c": one["c"], "c_ctx": one["c_ctx"], "b_ada": one["b_ada"], "g_mix": one["norm_mix_g"],
             "g_ffn": one["norm_ffn_g"], "b_u": b_in[0:1024], "b_nq": b_in[2240:2752], "b_nk": b_in[2752:3264],
             "b_ga": b_in[3776:4800], "b_gb": b_in[4800:5824], "g_mix_2": one["g_mix_2"],
             "g_ffn_2": one["g_ffn_2"], "g_q_lora": one["g_q_lora_2"], "g_kv_lora": one["g_kv_lora_2"]}
    arrays = {
        "x": one["x"], "ctx": one["ctx"], "cols": np.concatenate([cols(parts[n]) for n in COLS], 1),
        "b_rows": np.concatenate([b_in[1024:2240], b_in[3264:3776]]),
        "ln_rows": np.stack([one["sgu_ln_g"], one["sgu_ln_b"]]),
        "sgu_w": one["sgu_w_s"].transpose(2, 0, 1), "sgu_b": one["sgu_b_s"],
        "rpb": np.pad(one["na_rpb"][:, :, ::-1], ((0, 0), (0, 0), (48, 48))),
    }
    for n in ("w_ada", "w_in", "tiny_w_o", "w_up_a", "w_up_b", "w_out"):
        arrays[n] = one[n]
    arrays.update(tables(np))
    more_arrays(np, one, arrays)

    nc = bacc.Bacc("TRN2", target_bir_lowering=False, num_devices=1)
    sent, a = {}, {}
    for n, v in arrays.items():
        sent["in_" + n] = np.ascontiguousarray(v)
        a[n] = nc.dram_tensor("in_" + n, v.shape, mybir.dt.from_np(v.dtype), kind="ExternalInput").ap()
    out = nc.dram_tensor("out", (S, D), F32, kind="ExternalOutput").ap()
    build(nc, a, out, scratch_tensors(nc))
    r = run(nc, [sent], core_ids=[0])
    return r.results[0]["out"].reshape(1, S, D)


def scratch_tensors(nc):
    return {"gates": nc.dram_tensor("gates", (P, PNK, S), F32).ap()}


def more_arrays(np, one, arrays):
    def chunked(w):
        e, k, n = w.shape
        return w.reshape(e, k // P, P, n).transpose(0, 2, 1, 3).reshape(e, P, -1)

    with_shared = {w: np.concatenate([one["w_sh_" + w][None], one["w_e_" + w]]) for w in ("gate", "up", "down")}
    arrays["e_gu"] = np.concatenate([chunked(with_shared["gate"]), chunked(with_shared["up"])], 2)
    arrays["e_dn"] = chunked(with_shared["down"])
    arrays["peer_u"] = one["peer_u_2"].reshape(PNK, NG, GE, KD, P).transpose(1, 4, 2, 3, 0).reshape(NG, P, GE * D)
    arrays["peer_v"] = one["peer_v_2"].reshape(PNK, NG, GE * D).transpose(1, 0, 2)
    arrays["keys"] = np.stack([one["peer_keys_1_2"].T, one["peer_keys_2_2"].T])
    arrays["w_peer_q"] = one["w_peer_q_2"]
    arrays["meta"] = one["meta_tokens_2"]
    arrays["g_qk"] = np.stack([one["g_qk_q_2"], one["g_qk_k_2"]])
    for n in ("w_in_2", "w_uq_2", "w_ukv_2", "w_mla_out_2", "w_ret_out_2", "w_mix_out_2", "g_ret_gn_2"):
        arrays[n if n == "w_in_2" else n[:-2]] = one[n]
    for n in ("w_router", "b_router", "final_norm_g"):
        arrays[n] = one[n]


def tables(np):
    f = np.float32
    t = np.arange(S)
    pos = np.stack([t // GRID, t % GRID], -1).astype(f)
    inv = (10000.0 ** (-np.arange(16, dtype=f) / 16)).astype(f)
    ang = (pos[:, :, None] * inv).reshape(T, P, 2, 16).transpose(1, 0, 2, 3)
    cq = np.arange(GRID)
    start = np.clip(cq - 8, 0, GRID - 16)
    inside = (cq[None, :] >= start[:, None]) & (cq[None, :] < start[:, None] + 16)
    near = np.where(inside, 0.0, NEG).astype(f)
    pos = np.zeros((P, T + 1), f)
    pos[:, :T] = META + np.arange(T)[None] * P + np.arange(P)[:, None]
    pos[:, T] = np.arange(P)

    def rope_table(half):
        inv = (10000.0 ** (-np.arange(half, dtype=f) / half)).astype(f)
        ang = pos[:, :, None] * inv
        return np.stack([np.cos(ang), np.sin(ang)], 1).astype(f)

    log_gamma = np.log(1.0 - 2.0 ** (-5.0 - np.arange(RH, dtype=f)))
    idx = np.arange(P, dtype=f)
    diff = idx[:, None] - idx[None, :]
    decay = np.where(diff[None] >= 0, np.exp(np.maximum(diff, 0.0)[None] * log_gamma[:, None, None]), 0.0)
    decay_t = decay.transpose(2, 0, 1).reshape(P, 4, 2, P).transpose(0, 2, 1, 3)
    zeta = np.exp((P - 1 - idx)[:, None] * log_gamma[None])
    xi = np.exp((idx + 1)[None] * log_gamma[:, None])
    by_half = np.arange(P) // RDK
    heads = 2 * np.arange(4)[None] + by_half[:, None]
    zeta_meta = np.concatenate([zeta[P - META:], np.zeros((P - META, RH))])
    causal = np.zeros((P, S), f)
    causal[:, S - P:] = np.where(idx[None] <= idx[:, None], 0.0, NEG)
    return {"k_rope_mla": rope_table(MROPE // 2), "k_rope_ret": rope_table(RDK // 2),
            "k_zeta": np.stack([zeta, zeta_meta], 1).astype(f), "k_decay": decay_t.astype(f),
            "k_xi": xi[heads].astype(f), "k_gamma": np.exp(P * log_gamma)[heads].astype(f), "k_causal": causal,
            "k_iota": np.broadcast_to(idx, (P, P)),
            "k_ident": np.eye(P, dtype=f), "k_ones": np.ones((P, P), f),
            "k_rope_tiny": np.stack([np.cos(ang), np.sin(ang)], 1).astype(f),
            "k_near_mask": np.concatenate([near, near])}
```

```python
from contextlib import ExitStack

import concourse.bass as bass
from concourse import mybir

ALU = mybir.AluOpType
ACT = mybir.ActivationFunctionType
F32 = mybir.dt.float32
F32R = mybir.dt.float32r
U32 = mybir.dt.uint32
AX = mybir.AxisListType.X

P = 128
S, D = 512, 1024
T = S // P
KD = D // P
CTX, META = 256, 16
EPS = 1e-6
TINY, NAH, NAD = 64, 16, 32
GRID, ROWS = 64, 8
SGU_G = 8
E, FF, TOPK = 64, 256, 8
MH, MNOPE, MROPE, MV = 8, 64, 32, 64
MQK = MNOPE + MROPE
QL, KVL = 384, 256
RH, RDK, RDV = 8, 64, 128
PH, PK, PNK = 8, 16, 128
NEG = -1e30
DR = 2 * ROWS - 2
W_BLOCK = 512

COLS = {}


def _place_cols():
    at = 0
    for name, n in (("c", 8), ("c_ctx", 8), ("b_ada", 48), ("g_mix", 8), ("g_ffn", 8), ("b_u", 8), ("b_nq", 4),
                    ("b_nk", 4), ("b_ga", 8), ("b_gb", 8), ("g_mix_2", 8), ("g_ffn_2", 8), ("g_q_lora", 3),
                    ("g_kv_lora", 2)):
        COLS[name] = (at, n)
        at += n
    return at


N_COLS = _place_cols()


class Signal:

    def __init__(self, sem):
        self.sem, self.base = sem, 0

    def at(self, n):
        return self.base + n


class Core:

    def __init__(self, nc, stack):
        self.nc, self.stack = nc, stack
        self.held = []
        self.top = nc.sbuf_usable_end // 64 * 64
        self.low = (nc.sbuf_base + 63) // 64 * 64
        self.signals = {}
        self.uid = 0
        self.spans = {}

    def sb(self, name, shape, dt=F32, high=False):
        size = 1
        for n in shape[1:]:
            size *= n
        size = (size * 4 + 63) // 64 * 64
        at = self.low
        for a, b in sorted(self.held):
            if not high and a - at >= size:
                break
            at = max(at, b)
        if high:
            at, free_to = self.top - size, self.top
            for a, b in sorted(self.held, reverse=True):
                if free_to - b >= size:
                    break
                free_to = min(free_to, a)
                at = free_to - size
            assert at >= self.low, (name, at, size)
        assert at + size <= self.top, (name, at, size)
        self.uid += 1
        t = self.nc.alloc_sbuf_tensor_at(f"{name}_{self.uid}", shape, dt, offset=at)
        self.held.append((at, at + size))
        self.spans[t.name] = (at, at + size)
        return t

    def alias(self, t, name, shape, dt):
        self.uid += 1
        return self.nc.alloc_sbuf_tensor_at(f"{name}_{self.uid}", shape, dt, offset=self.at(t))

    def psum(self, name, shape, dt):
        self.uid += 1
        return self.nc.psum_tensor(f"{name}_{self.uid}", shape, dt)

    def at(self, t):
        return self.spans[t.name][0]

    def drop(self, *tensors):
        for t in tensors:
            self.held.remove(self.spans[t.name])

    def sig(self, name):
        if name not in self.signals:
            self.signals[name] = Signal(self.stack.enter_context(self.nc.semaphore(name)))
        return self.signals[name]


def linked(eng, signal):
    def link(ins):
        signal.base += 1
        ins.then_inc(signal.sem, 1)
        eng.wait_ge(signal.sem, signal.base)
    return link


def dram_rows(ap, lo, hi):
    return ap[:, lo:hi].rearrange("(k p) n -> p k n", p=P)



def load_constants(core, a, keep):
    nc = core.nc
    loads = [(keep["ident"][:], a["k_ident"]), (keep["cols"][:], a["cols"]),
             (keep["gate_mix_row"][:], a["b_gates"][0:D].partition_broadcast(P)),
             (keep["gate_ffn_row"][:], a["b_gates"][D:2 * D].partition_broadcast(P)),
             (keep["x"][:], a["x"].rearrange("(t p) d -> p t d", p=P))]
    done = core.sig("constants_in")
    with nc.Block() as block:
        @block.sync
        def _(sp):
            for dst, src in loads:
                sp.dma_start(dst, src).then_inc(done.sem, 16)
            sp.wait_ge(done.sem, 16 * len(loads))


def modulation(core, a, keep):
    nc = core.nc
    NB, W = 6 * D // W_BLOCK, W_BLOCK
    w = core.sb("w_ada", [P, 3, KD, W])
    silu_c = core.sb("silu_c", [P, KD, 2])
    rows = core.sb("mod_rows", [2, 6 * D])
    first = core.sb("first_row", [2, P])
    mod = core.sb("mod", [P, 6 * KD, 2])
    w_in = [core.sig(f"ada_w_{i}") for i in range(3)]
    first_in, c_ready, mm, row_ready = (core.sig(n) for n in ("first_row_in", "silu_c_ready", "ada_mm", "mod_row_ready"))
    turned, row_mm, chain, row_out = (core.sig(n) for n in ("mod_turned", "gain_row_mm", "dve_chain", "gain_row_out"))
    c0 = COLS["c"][0]
    col = keep["cols"]
    with (core.psum("ps_mod_rows", [2, 2, W], F32) as ps, core.psum("ps_mod", [P, 6 * KD, 2], F32) as ps_mod,
          core.psum("ps_row", [P, 2, 2 * W], F32) as ps_row, nc.Block() as block):
        @block.sync
        def _(sp):
            for b in range(NB):
                if b >= 3:
                    sp.wait_ge(mm.sem, b - 2)
                sp.dma_start(w[:, b % 3], dram_rows(a["w_ada"], b * W, (b + 1) * W)).then_inc(w_in[b % 3].sem, 16)
                if b == 0:
                    sp.dma_start(first[:], a["k_first"]).then_inc(first_in.sem, 16)

        @block.scalar
        def _(act):
            for j in range(2):
                nc.scalar.activation(silu_c[:, :, j], col[:, c0 + j * KD:c0 + (j + 1) * KD], ACT.Silu) \
                    .then_inc(c_ready.sem, 1)
            for b in range(NB):
                act.wait_ge(mm.sem, b + 1)
                nc.scalar.activation(rows[:, b * W:(b + 1) * W], ps[:, b % 2, :], ACT.Copy).then_inc(row_ready.sem, 1)

        @block.tensor
        def _(pe):
            pe.wait_ge(c_ready.sem, 2)
            for b in range(NB):
                pe.wait_ge(w_in[b % 3].sem, 16 * (b // 3 + 1))
                if b >= 2:
                    pe.wait_ge(row_ready.sem, b - 1)
                for k in range(KD):
                    last = nc.tensor.matmul(ps[:, b % 2, :], silu_c[:, k, :], w[:, b % 3, k, :], start=k == 0,
                                            stop=k == KD - 1)
                last.then_inc(mm.sem, 1)
            pe.wait_ge(row_ready.sem, NB)
            for n in range(6 * KD):
                last = nc.tensor.transpose(ps_mod[:, n, :], rows[:, n * P:(n + 1) * P], keep["ident"][0:2, 0:2])
            last.then_inc(turned.sem, 1)
            pe.wait_ge(first_in.sem, 16)
            for g, at in enumerate((2 * D, 5 * D)):
                for h in range(2):
                    last = nc.tensor.matmul(ps_row[:, g, h * W:(h + 1) * W], first[:],
                                            rows[:, at + h * W:at + (h + 1) * W], start=True, stop=True)
            last.then_inc(row_mm.sem, 1)

        @block.vector
        def _(dve):
            link = linked(dve, chain)
            dve.wait_ge(turned.sem, 1)
            b0 = COLS["b_ada"][0]
            for j in range(2):
                link(nc.vector.tensor_tensor(mod[:, :, j], ps_mod[:, :, j], col[:, b0:b0 + 6 * KD], ALU.add))
            for j in range(2):
                g0 = COLS["g_mix"][0]
                link(nc.vector.scalar_tensor_tensor(keep["gain_mix"][:, j, :], mod[:, KD:2 * KD, j], 1.0,
                                                    col[:, g0:g0 + KD], ALU.add, ALU.mult))
                link(nc.vector.tensor_copy(keep["shift_mix"][:, j, :], mod[:, 0:KD, j]))
            g0 = COLS["g_ffn"][0]
            link(nc.vector.scalar_tensor_tensor(keep["gain_ffn"][:], mod[:, 4 * KD:5 * KD, 0], 1.0,
                                                col[:, g0:g0 + KD], ALU.add, ALU.mult))
            link(nc.vector.tensor_copy(keep["shift_ffn"][:], mod[:, 3 * KD:4 * KD, 0]))
            dve.wait_ge(row_mm.sem, 1)
            for g, name in enumerate(("gate_mix_row", "gate_ffn_row")):
                for h in range(2):
                    sl = slice(h * W, (h + 1) * W)
                    nc.vector.tensor_tensor(keep[name][:, sl], ps_row[:, g, sl], keep[name][:, sl], ALU.add) \
                        .then_inc(row_out.sem, 1)
    core.drop(w, silu_c, rows, first, mod)



def normalise(core, sources, width, out):
    nc = core.nc
    n = len(sources)
    stat = core.sb("stat", [P, 3, n])
    junk = core.sb("junk", [P, width], high=True)
    squares, root, chain, done = core.sig("squares"), core.sig("root"), core.sig("dve_chain"), core.sig("normalised")
    act_chain = core.sig("act_chain")
    b_sq, b_root, b_done = squares.base, root.base, done.base
    with nc.Block() as block:
        @block.scalar
        def _(act):
            link = linked(act, act_chain)
            act.wait_ge(squares.sem, b_sq + 1)
            for i, (rows, src) in enumerate(sources):
                link(nc.scalar.activation(junk[0:rows, :], src, ACT.Square, accum_out=stat[0:rows, 0, i:i + 1]))
            nc.scalar.activation(junk[0:1, 0:1], junk[0:1, 0:1], ACT.Copy).then_inc(root.sem, 1)
            act.wait_ge(squares.sem, b_sq + 2)
            nc.scalar.activation(stat[:, 2, :], stat[:, 1, :], ACT.Sqrt).then_inc(root.sem, 1)

        @block.vector
        def _(dve):
            link = linked(dve, chain)
            nc.vector.memset(stat[:], 1.0).then_inc(squares.sem, 1)
            dve.wait_ge(root.sem, b_root + 1)
            nc.vector.tensor_scalar(stat[:, 1, :], stat[:, 0, :], 1.0 / width, EPS, ALU.mult, ALU.add) \
                .then_inc(squares.sem, 1)
            dve.wait_ge(root.sem, b_root + 2)
            link(nc.vector.reciprocal(stat[:, 0, :], stat[:, 2, :]))
            for i, (rows, src) in enumerate(sources):
                nc.vector.tensor_scalar(out[i], src, stat[0:rows, 0, i:i + 1], None, ALU.mult) \
                    .then_inc(done.sem, 1)
    squares.base += 2
    root.base += 2
    done.base += n
    core.drop(stat, junk)


def turn(core, jobs):
    nc = core.nc
    turned, out = core.sig("turned"), [core.sig("turn_out_dve"), core.sig("turn_out_act")]
    ident = core.ident
    b_t, b_o = turned.base, [o.base for o in out]
    with core.psum("ps_turn", [P, 4, W_BLOCK], F32) as ps, nc.Block() as block:
        @block.tensor
        def _(pe):
            for n, (pieces, _) in enumerate(jobs):
                if n >= 4:
                    pe.wait_ge(out[n % 2].sem, b_o[n % 2] + (n - 4) // 2 + 1)
                for src, c0 in pieces:
                    rows, cols = src.shape[0], src.shape[-1]
                    last = nc.tensor.transpose(ps[0:cols, n % 4, c0:c0 + rows], src, ident[0:rows, 0:rows])
                last.then_inc(turned.sem, 1)

        @block.vector
        def _(dve):
            for n in range(0, len(jobs), 2):
                dve.wait_ge(turned.sem, b_t + n + 1)
                jobs[n][1](nc.vector, ps[:, n % 4, :]).then_inc(out[0].sem, 1)

        @block.scalar
        def _(act):
            for n in range(1, len(jobs), 2):
                act.wait_ge(turned.sem, b_t + n + 1)
                jobs[n][1](nc.scalar, ps[:, n % 4, :]).then_inc(out[1].sem, 1)
    turned.base += len(jobs)
    out[0].base += (len(jobs) + 1) // 2
    out[1].base += len(jobs) // 2


def copied(nc, dst, rows, cols):
    def evacuate(eng, bank):
        if eng is nc.scalar:
            return nc.scalar.activation(dst, bank[0:rows, 0:cols], ACT.Copy)
        return nc.vector.tensor_copy(dst, bank[0:rows, 0:cols])
    return evacuate


def scaled(nc, dst, rows, cols, gain, shift=None):
    def evacuate(eng, bank):
        src = bank[0:rows, 0:cols]
        if eng is nc.scalar:
            if shift is None:
                return nc.scalar.activation(dst, src, ACT.Copy, scale=gain)
            return nc.scalar.activation(dst, src, ACT.Identity, scale=gain, bias=shift)
        if shift is None:
            return nc.vector.tensor_scalar(dst, src, gain, None, ALU.mult)
        return nc.vector.tensor_scalar(dst, src, gain, shift, ALU.mult, ALU.add)
    return evacuate


def norm_turned(core, sources, width, dst, spans):
    nc = core.nc
    xn = core.sb("xn", [P, len(sources), width], high=True)
    normalise(core, sources, width, [xn[0:r, i, :] for i, (r, _) in enumerate(sources)])
    jobs = []
    for k in range(width // P):
        for first, count, c0, gain, shift in spans:
            rows = [sources[first + i][0] for i in range(count)]
            pieces = [(xn[0:rows[i], first + i, k * P:(k + 1) * P], i * P) for i in range(count)]
            total = sum(rows)
            jobs.append((pieces, scaled(nc, dst[:, k, c0:c0 + total], P, total, gain(k), shift(k) if shift else None)))
    turn(core, jobs)
    core.drop(xn)


class Halves:

    def __init__(self, core, raw, name, hi=None):
        shape = [P, raw.shape[1], raw.shape[2]]
        self.raw = raw
        self.hi = core.sb(name + "_hi", shape, F32R) if hi is None else hi
        self.lo = core.alias(raw, name + "_lo", shape, F32R)


def project(core, blocks, halve=()):
    nc = core.nc
    NW, NP = 2, 4
    kmax = max(b[0].shape[1] for b in blocks)
    nmax = max(b[0].shape[2] for b in blocks)
    w = core.sb("w", [P, NW, kmax, nmax], high=True)
    w_hi, w_lo = core.sb("w_hi", [P, NW, kmax, nmax], F32R, high=True), core.alias(w, "w_lo", [P, NW, kmax, nmax], F32R)
    w_in = [core.sig(f"w_in_{i}") for i in range(NW)]
    mm, w_hi_done, w_lo_done = core.sig("unit_mm"), core.sig("w_hi_done"), core.sig("w_lo_done")
    x_hi_done, x_lo_done = core.sig("x_hi_done"), core.sig("x_lo_done")
    out = {"act": core.sig("unit_out_act"), "dve": core.sig("unit_out_dve")}
    chain = {"act": core.sig("act_chain"), "dve": core.sig("dve_chain")}
    b_w, b_mm, b_wh, b_wl = [s.base for s in w_in], mm.base, w_hi_done.base, w_lo_done.base
    b_xh, b_xl = x_hi_done.base, x_lo_done.base
    b_out = {e: s.base for e, s in out.items()}
    units = [(b, u) for b, (_, us) in enumerate(blocks) for u in us]

    def part(t, b):
        src = blocks[b][0]
        return t[:, b % NW, 0:src.shape[1], 0:src.shape[2]]

    def outs_before(n, e):
        return sum(1 for _, u in units[:n] if u[3] == e)

    chunks = [(x, k) for x in halve for k in range(x.raw.shape[1])]
    with core.psum("ps_unit", [P, NP, W_BLOCK], F32) as ps, nc.Block() as block:
        @block.sync
        def _(sp):
            for b, (src, _) in enumerate(blocks):
                if b >= NW:
                    sp.wait_ge(mm.sem, b_mm + sum(len(us) for _, us in blocks[:b - NW + 1]))
                sp.dma_start(part(w, b), src).then_inc(w_in[b % NW].sem, 16)

        @block.tensor
        def _(pe):
            if halve:
                pe.wait_ge(x_lo_done.sem, b_xl + len(chunks))
            for n, (b, (pairs, rows, cols, _, _)) in enumerate(units):
                if n == 0 or units[n - 1][0] != b:
                    pe.wait_ge(w_lo_done.sem, b_wl + b + 1)
                if n >= NP:
                    e = units[n - NP][1][3]
                    pe.wait_ge(out[e].sem, b_out[e] + outs_before(n - NP + 1, e))
                both = pairs(part(w_hi, b), part(w_lo, b))
                for i, (lhs, rhs) in enumerate(both):
                    last = nc.tensor.matmul(ps[0:rows, n % NP, 0:cols], lhs, rhs, start=i == 0, stop=i == len(both) - 1)
                last.then_inc(mm.sem, 1)

        def write_out(eng, name, halve_block):
            link = linked(eng, chain[name])
            halve_block(0)
            for b in range(len(blocks)):
                if b + 1 < len(blocks):
                    halve_block(b + 1)
                for n, (ub, (_, rows, cols, e, evacuate)) in enumerate(units):
                    if ub == b and e == name:
                        eng.wait_ge(mm.sem, b_mm + n + 1)
                        evacuate(ps[0:rows, n % NP, 0:cols], link).then_inc(out[name].sem, 1)

        @block.scalar
        def _(act):
            for x, k in chunks:
                nc.scalar.activation(x.hi[:, k, :], x.raw[:, k, :], ACT.Copy).then_inc(x_hi_done.sem, 1)

            def high(b):
                act.wait_ge(w_in[b % NW].sem, b_w[b % NW] + 16 * (b // NW + 1))
                nc.scalar.activation(part(w_hi, b), part(w, b), ACT.Copy).then_inc(w_hi_done.sem, 1)

            write_out(act, "act", high)

        @block.vector
        def _(dve):
            for i, (x, k) in enumerate(chunks):
                dve.wait_ge(x_hi_done.sem, b_xh + i + 1)
                nc.vector.tensor_tensor(x.lo[:, k, :], x.raw[:, k, :], x.hi[:, k, :].bitcast(F32), ALU.subtract) \
                    .then_inc(x_lo_done.sem, 1)

            def low(b):
                dve.wait_ge(w_hi_done.sem, b_wh + b + 1)
                nc.vector.tensor_tensor(part(w_lo, b), part(w, b), part(w_hi, b).bitcast(F32), ALU.subtract) \
                    .then_inc(w_lo_done.sem, 1)

            write_out(dve, "dve", low)
    for b in range(len(blocks)):
        w_in[b % NW].base += 16
    mm.base += len(units)
    w_hi_done.base += len(blocks)
    w_lo_done.base += len(blocks)
    x_hi_done.base += len(chunks)
    x_lo_done.base += len(chunks)
    for e in out:
        out[e].base += outs_before(len(units), e)
    core.drop(w, w_hi)


def features_unit(x, k_chunks, m, n, engine, evacuate):
    def pairs(w_hi, w_lo):
        both = []
        for k in range(k_chunks):
            hi, lo = w_hi[:, k, m * P:(m + 1) * P], w_lo[:, k, m * P:(m + 1) * P]
            both += [(hi, x.hi[:, k, n]), (hi, x.lo[:, k, n]), (lo, x.hi[:, k, n])]
        return both
    return pairs, P, n.stop - n.start, engine, evacuate


def tokens_unit(x, k_chunks, tok, cols, engine, evacuate, c0=0):
    def pairs(w_hi, w_lo):
        both = []
        for k in range(k_chunks):
            hi, lo = w_hi[:, k, c0:c0 + cols], w_lo[:, k, c0:c0 + cols]
            both += [(x.hi[:, k, tok], hi), (x.hi[:, k, tok], lo), (x.lo[:, k, tok], hi)]
        return both
    return pairs, tok.stop - tok.start, cols, engine, evacuate


def joined(core, x):
    nc = core.nc
    with nc.Block() as block:
        @block.vector
        def _(dve):
            nc.vector.tensor_tensor(x.raw[:], x.hi[:].bitcast(F32), x.lo[:].bitcast(F32), ALU.add)
    core.drop(x.hi)


def rope(nc, link, x1, x2, cos, sin, o1, o2, t1, t2):
    link(nc.vector.tensor_tensor(t1, x1, cos, ALU.mult))
    link(nc.vector.tensor_tensor(t2, x2, sin, ALU.mult))
    link(nc.vector.tensor_tensor(o1, t1, t2, ALU.subtract))
    link(nc.vector.tensor_tensor(t1, x2, cos, ALU.mult))
    link(nc.vector.tensor_tensor(t2, x1, sin, ALU.mult))
    link(nc.vector.tensor_tensor(o2, t1, t2, ALU.add))


def attend(core, tiles, dv, outs):
    nc = core.nc
    units = [(j, h, u) for j, heads in enumerate(tiles) for h, u in enumerate(heads)]
    U, H = len(units), len(tiles[0])
    G = min(H, P // dv)
    R = G * dv
    FAR = max(u[4] for _, _, u in units)
    s = core.sb("scores", [P, 2, S], high=True)
    pr = core.sb("probs", [P, 2, S + FAR], high=True)
    prT = core.sb("probsT", [P, 2, S + 2 * P], high=True)
    mx = core.sb("maxima", [P, 3, 2])
    sums = core.sb("sums", [P, 3, U])
    inv_rows, inv = core.sb("inv_rows", [G, P]), core.sb("inv_spread", [R, P])
    spread = core.sb("spread", [G, R])
    load(core, [(spread[:], core.spread[dv][0:G, 0:R])])
    scored, maxed, exped = core.sig("scored"), core.sig("maxed"), core.sig("exped")
    turned, near_out, far_out = core.sig("probs_turned"), core.sig("near_out"), core.sig("far_out")
    near_taken, valued, tile_out = core.sig("near_taken"), core.sig("valued"), core.sig("group_out")
    inv_done, inv_turned, inv_copied, inv_mm = (core.sig(n) for n in ("inv_done", "inv_turned", "inv_copied", "inv_mm"))
    b_id, b_it, b_ic, b_im = (x.base for x in (inv_done, inv_turned, inv_copied, inv_mm))
    chain = core.sig("dve_chain")
    sigs = (scored, maxed, exped, turned, near_out, far_out, near_taken, valued, tile_out)
    bs, bm, be, bt, bn, bf, bk, bv, bo = (x.base for x in sigs)
    ident = core.ident
    with (core.psum("ps_near", [P, 2, S], F32) as ps_near, core.psum("ps_far", [P, 2, S], F32) as ps_far,
          core.psum("ps_ptn", [P, S], F32) as ps_ptn, core.psum("ps_ptf", [P, S], F32) as ps_ptf,
          core.psum("ps_o", [P, 2, S], F32) as ps_o, nc.Block() as block):
        @block.tensor
        def _(pe):
            def score(n):
                _, _, (q, kn, near, kf, far, _, _, _) = units[n]
                b = n % 2
                if n >= 2:
                    pe.wait_ge(near_taken.sem, bk + n - 1)
                    pe.wait_ge(exped.sem, be + n - 1)
                nc.tensor.matmul(ps_near[:, b, 0:near], q, kn, start=True, stop=True)
                nc.tensor.matmul(ps_far[:, b, 0:far], q, kf, start=True, stop=True).then_inc(scored.sem, 1)

            def turn_probs(n):
                _, _, (_, _, near, _, far, _, vn, vf) = units[n]
                b = n % 2
                pe.wait_ge(exped.sem, be + n + 1)
                if n >= 1:
                    pe.wait_ge(near_out.sem, bn + n)
                    pe.wait_ge(far_out.sem, bf + n)
                for i in range(near // P):
                    nc.tensor.transpose(ps_ptn[:, i * P:(i + 1) * P], pr[:, b, i * P:(i + 1) * P], ident[:])
                for i, v in enumerate(vf):
                    rows = v.shape[0]
                    last = nc.tensor.transpose(ps_ptf[0:rows, i * P:(i + 1) * P],
                                               pr[:, b, S + i * P:S + i * P + rows], ident[:])
                last.then_inc(turned.sem, 1)

            def value(n):
                _, _, (_, _, _, _, _, _, vn, vf) = units[n]
                b, g, i0 = n % 2, n // G, n % G * dv
                pe.wait_ge(near_out.sem, bn + n + 1)
                pe.wait_ge(far_out.sem, bf + n + 1)
                if n % G == 0 and g >= 2:
                    pe.wait_ge(tile_out.sem, bo + g - 1)
                total = len(vn) + len(vf)
                for i, v in enumerate(vn + vf):
                    rows = v.shape[0]
                    at = i * P if i < len(vn) else S + (i - len(vn)) * P
                    last = nc.tensor.matmul(ps_o[i0:i0 + dv, g % 2, 0:P], v, prT[0:rows, b, at:at + P],
                                            start=i == 0, stop=i == total - 1)
                last.then_inc(valued.sem, 1)

            def turn_inverse(g):
                pe.wait_ge(inv_done.sem, b_id + g + 1)
                nc.tensor.transpose(ps_o[0:G, g % 2, P:2 * P], sums[:, 0, g * G:(g + 1) * G], ident[:]) \
                    .then_inc(inv_turned.sem, 1)

            def spread_inverse(g):
                pe.wait_ge(inv_copied.sem, b_ic + g + 1)
                nc.tensor.matmul(ps_o[0:R, g % 2, 2 * P:3 * P], spread[:], inv_rows[:], start=True, stop=True) \
                    .then_inc(inv_mm.sem, 1)

            score(0)
            for n in range(U + 2):
                if n + 1 < U:
                    score(n + 1)
                if n < U:
                    turn_probs(n)
                if 1 <= n <= U:
                    value(n - 1)
                if n >= 2 and (n - 1) % G == 0:
                    spread_inverse((n - 1) // G - 1)
                if 1 <= n <= U and n % G == 0:
                    turn_inverse(n // G - 1)

        @block.vector
        def _(dve):
            link = linked(dve, chain)

            def maxima(n):
                _, _, (_, _, near, _, far, bias, _, _) = units[n]
                b = n % 2
                dve.wait_ge(scored.sem, bs + n + 1)
                if n >= 2:
                    dve.wait_ge(exped.sem, be + n - 1)
                nc.vector.tensor_tensor_reduce(s[:, b, 0:near], ps_near[:, b, 0:near], bias, 1.0, NEG, ALU.add,
                                               ALU.max, mx[:, 0, b:b + 1]).then_inc(near_taken.sem, 1)
                link(nc.vector.tensor_reduce(mx[:, 1, b:b + 1], ps_far[:, b, 0:far], AX, ALU.max))
                dve.wait_ge(near_taken.sem, bk + n + 1)
                nc.vector.tensor_scalar(mx[:, 2, b:b + 1], mx[:, 0, b:b + 1], mx[:, 1, b:b + 1], -1.0, ALU.max,
                                        ALU.mult).then_inc(maxed.sem, 1)

            def inverse(g):
                cols = slice(g * G, (g + 1) * G)
                link(nc.vector.tensor_tensor(sums[:, 2, cols], sums[:, 0, cols], sums[:, 1, cols], ALU.add))
                nc.vector.reciprocal(sums[:, 0, cols], sums[:, 2, cols]).then_inc(inv_done.sem, 1)

            def copy_inverse(g):
                dve.wait_ge(inv_turned.sem, b_it + g + 1)
                if g >= 1:
                    dve.wait_ge(inv_mm.sem, b_im + g)
                nc.vector.tensor_copy(inv_rows[:], ps_o[0:G, g % 2, P:2 * P]).then_inc(inv_copied.sem, 1)

            def group_out(g):
                dve.wait_ge(inv_mm.sem, b_im + g + 1)
                if g >= 1:
                    dve.wait_ge(tile_out.sem, bo + g)
                link(nc.vector.tensor_copy(inv[:], ps_o[0:R, g % 2, 2 * P:3 * P]))
                nc.vector.tensor_tensor(outs[g], ps_o[0:R, g % 2, 0:P], inv[:], ALU.mult).then_inc(tile_out.sem, 1)

            maxima(0)
            for n in range(U + 2):
                if n + 1 < U:
                    maxima(n + 1)
                if n < U:
                    near = units[n][2][2]
                    dve.wait_ge(turned.sem, bt + n + 1)
                    if n >= 2:
                        dve.wait_ge(valued.sem, bv + n - 1)
                    nc.vector.tensor_copy(prT[:, n % 2, 0:near], ps_ptn[:, 0:near]).then_inc(near_out.sem, 1)
                    if n % G == G - 1:
                        inverse(n // G)
                if n >= 2 and (n - 1) % G == 0:
                    group_out((n - 1) // G - 1)
                if 1 <= n <= U and n % G == 0:
                    copy_inverse(n // G - 1)

        @block.scalar
        def _(act):
            def exponentials(n):
                _, _, (_, _, near, _, far, _, _, _) = units[n]
                b = n % 2
                act.wait_ge(maxed.sem, bm + n + 1)
                if n >= 2:
                    act.wait_ge(turned.sem, bt + n - 1)
                nc.scalar.activation(pr[:, b, 0:near], s[:, b, 0:near], ACT.Exp, bias=mx[:, 2, b:b + 1],
                                     accum_out=sums[:, 0, n:n + 1])
                nc.scalar.activation(pr[:, b, S:S + far], ps_far[:, b, 0:far], ACT.Exp, bias=mx[:, 2, b:b + 1],
                                     accum_out=sums[:, 1, n:n + 1]).then_inc(exped.sem, 1)

            exponentials(0)
            for n in range(U):
                vf = units[n][2][7]
                rows = vf[0].shape[0]
                act.wait_ge(turned.sem, bt + n + 1)
                if n >= 2:
                    act.wait_ge(valued.sem, bv + n - 1)
                nc.scalar.activation(prT[0:rows, n % 2, S:S + len(vf) * P], ps_ptf[0:rows, 0:len(vf) * P],
                                     ACT.Copy).then_inc(far_out.sem, 1)
                if n + 1 < U:
                    exponentials(n + 1)
    for x in sigs[:8]:
        x.base += U
    for x in (tile_out, inv_done, inv_turned, inv_copied, inv_mm):
        x.base += U // G
    core.drop(s, pr, prT, mx, sums, inv_rows, inv, spread)



def first_mixer(core, a, keep):
    nc = core.nc
    x, cols = keep["x"], keep["cols"]
    TC = T + CTX // P

    def col(name, i):
        at = COLS[name][0]
        return cols[:, at + i:at + i + 1]

    hT = core.sb("hT", [P, KD, S + CTX])
    ctx = core.sb("ctx", [P, CTX // P, D], high=True)
    load(core, [(ctx[:], a["ctx"].rearrange("(t p) d -> p t d", p=P))])
    norm_turned(core, [(P, x[:, t, :]) for t in range(T)] + [(P, ctx[:, t, :]) for t in range(CTX // P)], D, hT,
                [(0, T, 0, lambda k: keep["gain_mix"][:, 0, k:k + 1], lambda k: keep["shift_mix"][:, 0, k:k + 1]),
                 (T, CTX // P, S, lambda k: keep["gain_mix"][:, 1, k:k + 1],
                  lambda k: keep["shift_mix"][:, 1, k:k + 1])])
    core.drop(ctx)

    h = Halves(core, hT, "hT")
    v = core.sb("v", [P, T, D], high=True)
    tiny = core.sb("tiny_qkv", [P, TC, 3 * TINY])
    nq = core.sb("nq", [P, 4, S])
    nk = core.sb("nk", [P, 4, S + CTX])
    nv = core.sb("nv", [P, TC, NAH * NAD])
    brow = core.sb("b_rows", [P, D + 3 * TINY + 512], high=True)
    load(core, [(brow[:], a["b_rows"].partition_broadcast(P))])
    all_tok = slice(0, S)
    blocks = []

    def toks(t):
        return slice(t * P, (t + 1) * P)

    def plus_row(dst, at, n):
        return lambda ps, link: nc.vector.tensor_tensor(dst, ps, brow[:, at:at + n], ALU.add)

    def through(func, dst, bias):
        return lambda ps, link: nc.scalar.activation(dst, ps, func, bias=bias)

    for b in range(2):
        at = 1024 + b * 512
        blocks.append((dram_rows(a["w_in"], at, at + 512),
                       [tokens_unit(h, KD, toks(t), 512, "dve", plus_row(v[:, t, b * 512:(b + 1) * 512], b * 512, 512))
                        for t in range(T)]))
    blocks.append((dram_rows(a["w_in"], 2048, 2240),
                   [tokens_unit(h, KD, toks(t), 192, "dve", plus_row(tiny[:, t, :], D, 192)) for t in range(TC)]))
    scale = NAD ** -0.5
    blocks.append((dram_rows(a["w_in"], 2240, 2752),
                   [features_unit(h, KD, m, all_tok, "dve",
                                  lambda ps, link, m=m: nc.vector.tensor_scalar(nq[:, m, :], ps, col("b_nq", m), scale,
                                                                                ALU.add, ALU.mult))
                    for m in range(4)]))
    blocks.append((dram_rows(a["w_in"], 2752, 3264),
                   [features_unit(h, KD, m, sl, "act", through(ACT.Identity, nk[:, m, sl], col("b_nk", m)))
                    for m in range(4) for sl in (all_tok, slice(S, S + CTX))]))
    blocks.append((dram_rows(a["w_in"], 3264, 3776),
                   [tokens_unit(h, KD, toks(t), 512, "dve", plus_row(nv[:, t, :], D + 192, 512)) for t in range(TC)]))
    project(core, blocks, [h])
    core.drop(brow)
    joined(core, h)

    rows = core.sb("ln_rows", [P, 2, D], high=True)
    tab = core.sb("rope_tab", [P, 2, T, 2, 16])
    tq = core.sb("tq", [P, T, TINY])
    tk = core.sb("tk", [P, TC, TINY])
    t1, t2 = core.sb("t1", [P, T, 2, 16]), core.sb("t2", [P, T, 2, 16])
    zero = core.sb("zero", [P, S])
    near_bias = core.sb("near_bias", [P, NAH, DR, GRID])
    raw = core.sb("raw_bias", [P, 2, DR, GRID], high=True)
    mask = core.sb("near_mask", [P, GRID])
    stats = core.sb("ln_stats", [P, T, 16])
    in_, gelu, chain = core.sig("prepare_in"), core.sig("v_gelu"), core.sig("dve_chain")
    raw_in = [core.sig("raw_bias_even"), core.sig("raw_bias_odd")]
    pool_done, root, var_done, ln_done = (core.sig("near_bias_done"), core.sig("root"), core.sig("ln_var"),
                                          core.sig("ln_done"))
    b_root = root.base
    with nc.Block() as block:
        @block.sync
        def _(sp):
            sp.dma_start(rows[:], a["ln_rows"].partition_broadcast(P)).then_inc(in_.sem, 16)
            sp.dma_start(tab[:], a["k_rope_tiny"]).then_inc(in_.sem, 16)
            sp.dma_start(mask[:], a["k_near_mask"]).then_inc(in_.sem, 16)
            rpb = a["rpb"]
            for h in range(NAH):
                if h >= 2:
                    sp.wait_ge(pool_done.sem, h - 1)
                for half in range(2):
                    src = bass.AP(tensor=rpb.tensor, offset=(h * 15 + 1 - half) * 127,
                                  ap=[[1, GRID], [127, DR], [1, GRID]])
                    sp.dma_start(raw[half * GRID:(half + 1) * GRID, h % 2, :, :], src).then_inc(raw_in[h % 2].sem, 16)

        @block.gpsimd
        def _(pool):
            pool.wait_ge(in_.sem, 48)
            for h in range(NAH):
                pool.wait_ge(raw_in[h % 2].sem, 32 * (h // 2 + 1))
                r = raw[:, h % 2, :, :]
                back = bass.AP(tensor=r.tensor, offset=r.offset + GRID - 1,
                               ap=[list(r.ap[0]), [GRID, DR], [-1, GRID]])
                nc.gpsimd.tensor_tensor(near_bias[:, h], back, mask[:].unsqueeze(1).to_broadcast([P, DR, GRID]),
                                        ALU.add).then_inc(pool_done.sem, 1)

        @block.scalar
        def _(act):
            for t in range(T):
                nc.scalar.activation(v[:, t, :], v[:, t, :], ACT.Gelu).then_inc(gelu.sem, 1)
            act.wait_ge(var_done.sem, 1)
            nc.scalar.activation(stats[:, :, 14:15], stats[:, :, 13:14], ACT.Sqrt, bias=0.0).then_inc(root.sem, 1)

        @block.vector
        def _(dve):
            link = linked(dve, chain)
            link(nc.vector.memset(zero[:], 0.0))
            dve.wait_ge(in_.sem, 48)
            for dst, at in ((tq, 0), (tk, TINY)):
                src = tiny[:, 0:T, at:at + TINY].rearrange("p t (a h d) -> p t a h d", a=2, h=2)
                o = dst[:, 0:T, :].rearrange("p t (a h d) -> p t a h d", a=2, h=2)
                for t in range(T):
                    rope(nc, link, src[:, t, :, 0, :], src[:, t, :, 1, :], tab[:, 0, t], tab[:, 1, t],
                         o[:, t, :, 0, :], o[:, t, :, 1, :], t1[:, t], t2[:, t])
            link(nc.vector.tensor_copy(tk[:, T:TC, :], tiny[:, T:TC, TINY:2 * TINY]))
            link(nc.vector.tensor_scalar(tq[:], tq[:], TINY ** -0.5, None, ALU.mult))
            for t in range(T):
                dve.wait_ge(gelu.sem, t + 1)
                for h in range(2):
                    link(nc.vector.bn_stats(stats[:, t, 6 * h:6 * h + 6], v[:, t, h * 512:(h + 1) * 512]))
                link(nc.vector.bn_aggr(stats[:, t, 12:14], stats[:, t, 0:12]))
            nc.vector.tensor_scalar(stats[:, :, 13:14], stats[:, :, 13:14], EPS, None, ALU.add) \
                .then_inc(var_done.sem, 1)
            dve.wait_ge(root.sem, b_root + 1)
            link(nc.vector.reciprocal(stats[:, :, 13:14], stats[:, :, 14:15]))
            for t in range(T):
                link(nc.vector.tensor_scalar(v[:, t, :], v[:, t, :], stats[:, t, 12:13], stats[:, t, 13:14],
                                             ALU.subtract, ALU.mult))
                link(nc.vector.tensor_tensor(v[:, t, :], v[:, t, :], rows[:, 0, :], ALU.mult))
                link(nc.vector.tensor_tensor(v[:, t, :], v[:, t, :], rows[:, 1, :], ALU.add))
    root.base += 1
    core.drop(rows, tab, t1, t2, raw, mask, stats)

    tqT = core.sb("tqT", [TINY, S])
    tkT = core.sb("tkT", [TINY, S + CTX])
    turn(core, [([(tq[:, t, :], t * P) for t in range(T)], copied(nc, tqT[:], TINY, S)),
                ([(tk[:, t, :], t * P) for t in range(T)], copied(nc, tkT[:, 0:S], TINY, S)),
                ([(tk[:, T + t, :], t * P) for t in range(2)], copied(nc, tkT[:, S:S + CTX], TINY, CTX))])
    core.drop(tq, tk)
    otT = core.sb("tiny_outT", [TINY, S])
    vt = [tiny[:, t, 2 * TINY:3 * TINY] for t in range(TC)]
    attend(core, [[(tqT[:, toks(j)], tkT[:, 0:S], S, tkT[:, S:S + CTX], CTX, zero[:], vt[:T], vt[T:])]
                  for j in range(T)], TINY, [otT[:, toks(j)] for j in range(T)])
    core.drop(tiny, tqT, tkT, zero)

    onT = core.sb("near_outT", [P, 4, S])
    tiles = []
    for j in range(T):
        heads = []
        for h in range(NAH):
            p0, c = (h % 4) * NAD, h // 4
            pp = slice(p0, p0 + NAD)
            vh = [nv[:, t, h * NAD:(h + 1) * NAD] for t in range(TC)]
            bias = near_bias[:, h, 6 - 2 * j:14 - 2 * j, :].rearrange("p a b -> p (a b)")
            heads.append((nq[pp, c, toks(j)], nk[pp, c, 0:S], S, nk[pp, c, S:S + CTX], CTX, bias, vh[:T], vh[T:]))
        tiles.append(heads)
    attend(core, tiles, NAD, [onT[:, c, toks(j)] for j in range(T) for c in range(4)])
    core.drop(nq, nk, nv, near_bias)
    u = core.sb("u", [P, KD, S], high=True)
    h = Halves(core, hT, "hT")
    project(core, [(dram_rows(a["w_in"], b * 512, (b + 1) * 512),
                    [features_unit(h, KD, m, all_tok, "act", through(ACT.Gelu, u[:, 4 * b + m, :], col("b_u", 4 * b + m)))
                     for m in range(4)]) for b in range(2)], [h])
    ws = core.sb("sgu_w", [P, SGU_G, P])
    wo = core.sb("tiny_w_o", [TINY, D])
    bs = core.sb("sgu_b", [P, SGU_G, P])
    in_, mixed, out, link_sig = core.sig("sgu_in"), core.sig("sgu_mm"), core.sig("sgu_out"), core.sig("dve_chain")
    with core.psum("ps_sgu", [P, 2, S], F32) as ps, nc.Block() as block:
        @block.sync
        def _(sp):
            sp.dma_start(ws[:], a["sgu_w"]).then_inc(in_.sem, 16)
            sp.dma_start(wo[:], a["tiny_w_o"]).then_inc(in_.sem, 16)
            sp.dma_start(bs[:], a["sgu_b"].partition_broadcast(P)).then_inc(in_.sem, 16)

        @block.tensor
        def _(pe):
            pe.wait_ge(in_.sem, 48)
            for g in range(SGU_G):
                if g >= 2:
                    pe.wait_ge(out.sem, g - 1)
                for n in range(T):
                    nc.tensor.matmul(ps[:, g % 2, n * P:(n + 1) * P], v[:, n, g * P:(g + 1) * P], ws[:, g, :],
                                     start=n == 0, stop=False, skip_group_check=True)
                last = nc.tensor.matmul(ps[:, g % 2, :], wo[:, g * P:(g + 1) * P], otT[:], start=False, stop=True,
                                        skip_group_check=True)
                last.then_inc(mixed.sem, 1)

        @block.vector
        def _(dve):
            link = linked(dve, link_sig)
            dve.wait_ge(in_.sem, 48)
            for g in range(SGU_G):
                dve.wait_ge(mixed.sem, g + 1)
                p3 = ps[:, g % 2, :].rearrange("p (n q) -> p n q", n=T)
                link(nc.vector.tensor_tensor(p3, p3, bs[:, g, :].unsqueeze(1).to_broadcast([P, T, P]), ALU.add))
                nc.vector.tensor_tensor(u[:, g, :], ps[:, g % 2, :], u[:, g, :], ALU.mult).then_inc(out.sem, 1)
    core.drop(ws, wo, bs, otT, v)

    ga = core.sb("gate_a", [P, KD, S])
    gb = core.sb("gate_b", [P, KD, S])
    blocks = []
    for name, dst, at in (("b_ga", ga, 3776), ("b_gb", gb, 4800)):
        for b in range(4):
            blocks.append((dram_rows(a["w_in"], at + b * 256, at + (b + 1) * 256),
                           [features_unit(h, KD, m, all_tok, "act",
                                          through(ACT.Sigmoid, dst[:, 2 * b + m, :], col(name, 2 * b + m)))
                            for m in range(2)]))
    project(core, blocks)
    core.drop(hT, h.hi)

    merge(core, ga, gb, (u, KD, a["w_up_a"]), (onT, 4, a["w_up_b"]))
    core.drop(u, onT, gb)

    merged = Halves(core, ga, "merged")

    def residual(t, sl):
        def evacuate(ps, link):
            link(nc.vector.tensor_tensor(ps, ps, keep["gate_mix_row"][:, sl], ALU.mult))
            return nc.vector.tensor_tensor(x[:, t, sl], x[:, t, sl], ps, ALU.add)
        return evacuate

    project(core, [(dram_rows(a["w_out"], b * 512, (b + 1) * 512),
                    [tokens_unit(merged, KD, toks(t), 512, "dve", residual(t, slice(b * 512, (b + 1) * 512)))
                     for t in range(T)]) for b in range(2)], [merged])
    core.drop(ga, merged.hi)


def load(core, pairs):
    done = core.sig("loaded")
    base = done.base
    with core.nc.Block() as block:
        @block.sync
        def _(sp):
            for dst, src in pairs:
                sp.dma_start(dst, src).then_inc(done.sem, 16)
            sp.wait_ge(done.sem, base + 16 * len(pairs))
    done.base += 16 * len(pairs)



def three_pass(nc, out, w_hi, w_lo, x_hi, x_lo, first, last):
    nc.tensor.matmul(out, w_hi, x_hi, start=first, stop=False)
    nc.tensor.matmul(out, w_hi, x_lo, start=False, stop=False)
    return nc.tensor.matmul(out, w_lo, x_hi, start=False, stop=last)


def experts(core, a, keep):
    nc = core.nc
    x = keep["x"]
    N = E + 1
    h2 = core.sb("h2T", [P, KD, S])
    norm_turned(core, [(P, x[:, t, :]) for t in range(T)], D, h2,
                [(0, T, 0, lambda k: keep["gain_ffn"][:, k:k + 1], lambda k: keep["shift_ffn"][:, k:k + 1])])

    sc = core.sb("router_scores", [P, T, E])
    sel = core.sb("router_sel", [P, 2, T, E])
    best = core.sb("router_best", [P, T, 8])
    total = core.sb("router_total", [P, 2, T])
    wt = core.sb("expert_weights", [P, T, N])
    brow = core.sb("router_bias", [P, E])
    load(core, [(brow[:], a["b_router"].partition_broadcast(P))])
    h = Halves(core, h2, "h2T")
    x_hi, x_lo = h.hi, h.lo
    project(core, [(dram_rows(a["w_router"], 0, E),
                    [tokens_unit(h, KD, slice(t * P, (t + 1) * P), E, "act",
                                 lambda ps, link, t=t: nc.scalar.activation(sc[:, t, :], ps, ACT.Sigmoid))
                     for t in range(T)])], [h])
    with nc.Block() as block:
        @block.vector
        def _(dve):
            link = linked(dve, core.sig("dve_chain"))
            link(nc.vector.memset(wt[:], 1.0))
            link(nc.vector.tensor_tensor(sel[:, 0], sc[:], brow[:].unsqueeze(1).to_broadcast([P, T, E]), ALU.add))
            for t in range(T):
                link(nc.vector.max(best[:, t, :], sel[:, 0, t, :]))
                link(nc.vector.match_replace(sel[:, 1, t, :], best[:, t, :], sel[:, 0, t, :], NEG))
            link(nc.vector.tensor_tensor(sel[:, 0], sel[:, 0], sel[:, 1], ALU.not_equal))
            link(nc.vector.tensor_tensor(sc[:], sc[:], sel[:, 0], ALU.mult))
            link(nc.vector.tensor_reduce(total[:, 0, :], sc[:], AX, ALU.add))
            link(nc.vector.reciprocal(total[:, 1, :], total[:, 0, :]))
            for t in range(T):
                link(nc.vector.tensor_scalar(wt[:, t, 1:N], sc[:, t, :], total[:, 1, t:t + 1], 2.5, ALU.mult, ALU.mult))
    core.drop(sc, sel, best, total, brow)
    y = core.sb("y", [P, T, D])
    GU, DN = 2 * KD * FF, 2 * D
    gu = core.sb("gu", [P, 2, GU])
    gu_hi, gu_lo = core.sb("gu_hi", [P, 2, GU], F32R), core.alias(gu, "gu_lo", [P, 2, GU], F32R)
    dn = core.sb("dn", [P, 2, DN])
    dn_hi, dn_lo = core.sb("dn_hi", [P, 2, DN], F32R), core.alias(dn, "dn_lo", [P, 2, DN], F32R)
    sg, hg = core.sb("silu_gate", [P, 2, S]), core.sb("hidden", [P, 2, S])
    hg_hi, hg_lo = core.sb("hidden_hi", [P, 2, 2, S], F32R), core.sb("hidden_lo", [P, 2, 2, S], F32R)
    gu_in = [core.sig("gu_in_even"), core.sig("gu_in_odd")]
    dn_in = [core.sig("dn_in_even"), core.sig("dn_in_odd")]
    (gu_hi_done, gu_lo_done, dn_hi_done, dn_lo_done, gu_mm, dn_mm, silu_done, hidden_done, hidden_hi_done,
     hidden_lo_done, y_added) = (core.sig(n) for n in (
         "gu_hi_done", "gu_lo_done", "dn_hi_done", "dn_lo_done", "gu_mm", "dn_mm", "silu_done", "hidden_done",
         "hidden_hi_done", "hidden_lo_done", "y_added"))

    def weight(side, s, which, k, m):
        at = (which * KD + k) * FF + m * P
        return side[:, s, at:at + P]

    with (core.psum("ps_gate", [P, 2, S], F32) as ps_g, core.psum("ps_up", [P, 2, S], F32) as ps_u,
          core.psum("ps_down", [P, 4, S], F32) as ps_d, nc.Block() as block):
        def pairs(eng, lo, hi, step):
            n = lo
            with eng.Fori(0, (hi - lo) // 2) as i:
                for j in range(2):
                    step(2 * i + (n + j), (n + j) % 2)
            if (hi - lo) % 2:
                step(hi - 1, (hi - 1) % 2)

        @block.sync
        def _(sp):
            def load_gu(n, s, first=False):
                if not first:
                    sp.wait_ge(gu_mm.sem, 2 * n - 2)
                sp.dma_start(gu[:, s, :], a["e_gu"][bass.ds(n, 1)].rearrange("e p n -> (e p) n")) \
                    .then_inc(gu_in[s].sem, 16)

            def load_dn(n, s, first=False):
                if not first:
                    sp.wait_ge(dn_mm.sem, 8 * n - 8)
                sp.dma_start(dn[:, s, :], a["e_dn"][bass.ds(n, 1)].rearrange("e p n -> (e p) n")) \
                    .then_inc(dn_in[s].sem, 16)

            for n in range(2):
                load_gu(n, n, True)
                load_dn(n, n, True)

            def both(n, s):
                load_gu(n, s)
                load_dn(n, s)

            pairs(sp, 2, N, both)

        @block.scalar
        def _(act):
            def gu_high(n, s, half):
                act.wait_ge(gu_in[s].sem, half)
                nc.scalar.activation(gu_hi[:, s, :], gu[:, s, :], ACT.Copy).then_inc(gu_hi_done.sem, 1)

            def dn_high(n, s, half):
                act.wait_ge(dn_in[s].sem, half)
                nc.scalar.activation(dn_hi[:, s, :], dn[:, s, :], ACT.Copy).then_inc(dn_hi_done.sem, 1)

            def hidden(n, s, free):
                for m in range(2):
                    act.wait_ge(gu_mm.sem, 2 * n + (m + 1))
                    nc.scalar.activation(sg[:, m, :], ps_g[:, m, :], ACT.Silu).then_inc(silu_done.sem, 1)
                for m in range(2):
                    act.wait_ge(hidden_done.sem, 2 * n + (m + 1))
                    if free:
                        act.wait_ge(dn_mm.sem, 8 * n - 8)
                    nc.scalar.activation(hg_hi[:, s, m, :], hg[:, m, :], ACT.Copy).then_inc(hidden_hi_done.sem, 1)

            gu_high(0, 0, 16)
            gu_high(1, 1, 16)
            dn_high(0, 0, 16)
            hidden(0, 0, False)
            gu_high(2, 0, 32)
            dn_high(1, 1, 16)
            hidden(1, 1, False)
            gu_high(3, 1, 32)
            dn_high(2, 0, 32)
            with act.Fori(1, 31) as i:
                for s in range(2):
                    n = 2 * i + s
                    hidden(n, s, True)
                    gu_high(n, s, 16 * i + 32)
                    dn_high(n, 1 - s, 16 * i + 16 * (s + 1))
            hidden(62, 0, True)
            gu_high(64, 0, 16 * 33)
            dn_high(63, 1, 16 * 32)
            hidden(63, 1, True)
            dn_high(64, 0, 16 * 33)
            hidden(64, 0, True)

        @block.vector
        def _(dve):
            def gu_low(n, s):
                dve.wait_ge(gu_hi_done.sem, n + 1)
                nc.vector.tensor_tensor(gu_lo[:, s, :], gu[:, s, :], gu_hi[:, s, :].bitcast(F32), ALU.subtract) \
                    .then_inc(gu_lo_done.sem, 1)

            def dn_low(n, s):
                dve.wait_ge(dn_hi_done.sem, n + 1)
                nc.vector.tensor_tensor(dn_lo[:, s, :], dn[:, s, :], dn_hi[:, s, :].bitcast(F32), ALU.subtract) \
                    .then_inc(dn_lo_done.sem, 1)

            def hidden(n, s, before):
                for m in range(2):
                    dve.wait_ge(silu_done.sem, 2 * n + (m + 1))
                    if before:
                        dve.wait_ge(hidden_lo_done.sem, 2 * n + (m - 1))
                    nc.vector.tensor_tensor(hg[:, m, :], sg[:, m, :], ps_u[:, m, :], ALU.mult) \
                        .then_inc(hidden_done.sem, 1)
                for m in range(2):
                    dve.wait_ge(hidden_hi_done.sem, 2 * n + (m + 1))
                    nc.vector.tensor_tensor(hg_lo[:, s, m, :], hg[:, m, :], hg_hi[:, s, m, :].bitcast(F32),
                                            ALU.subtract).then_inc(hidden_lo_done.sem, 1)

            def add(n, first=False):
                for i in range(2 * T):
                    t, sl = i // 2, slice(i % 2 * S, (i % 2 + 1) * S)
                    dve.wait_ge(dn_mm.sem, 8 * n + (i + 1))
                    if first:
                        nc.vector.tensor_scalar(y[:, t, sl], ps_d[:, i % 4, :], wt[:, t, 0:1], None, ALU.mult) \
                            .then_inc(y_added.sem, 1)
                        continue
                    dve.wait_ge(y_added.sem, 8 * n + (i - 7))
                    nc.vector.scalar_tensor_tensor(y[:, t, sl], ps_d[:, i % 4, :], wt[:, t, bass.ds(n, 1)], y[:, t, sl],
                                                   ALU.mult, ALU.add).then_inc(y_added.sem, 1)

            gu_low(0, 0)
            gu_low(1, 1)
            dn_low(0, 0)
            hidden(0, 0, False)
            gu_low(2, 0)
            dn_low(1, 1)
            add(0, True)
            with dve.Fori(0, 31) as i:
                for j in range(1, 3):
                    n, s = 2 * i + j, j % 2
                    hidden(n, s, True)
                    gu_low(n + 2, s)
                    dn_low(n + 1, 1 - s)
                    add(n)
            hidden(63, 1, True)
            dn_low(64, 0)
            add(63)
            hidden(64, 0, True)
            add(64)

        @block.tensor
        def _(pe):
            def gate_up(n, s, before=True):
                pe.wait_ge(gu_lo_done.sem, n + 1)
                for m in range(2):
                    if before:
                        pe.wait_ge(hidden_done.sem, 2 * n + (m - 1))
                    for which, ps in ((0, ps_g), (1, ps_u)):
                        for k in range(KD):
                            last = three_pass(nc, ps[:, m, :], weight(gu_hi, s, which, k, m),
                                              weight(gu_lo, s, which, k, m), x_hi[:, k, :], x_lo[:, k, :],
                                              k == 0, k == KD - 1)
                    last.then_inc(gu_mm.sem, 1)

            def down(n, s, before=True):
                pe.wait_ge(hidden_lo_done.sem, 2 * n + 2)
                pe.wait_ge(dn_lo_done.sem, n + 1)
                for i in range(2 * T):
                    t, h = i // 2, i % 2
                    if before or i >= 4:
                        pe.wait_ge(y_added.sem, 8 * n + (i - 3))
                    for k in range(2):
                        at = k * D + h * S
                        last = three_pass(nc, ps_d[:, i % 4, :], hg_hi[:, s, k, t * P:(t + 1) * P],
                                          hg_lo[:, s, k, t * P:(t + 1) * P], dn_hi[:, s, at:at + S],
                                          dn_lo[:, s, at:at + S], k == 0, k == 1)
                    last.then_inc(dn_mm.sem, 1)

            gate_up(0, 0, False)
            gate_up(1, 1)
            down(0, 0, False)

            def both(n, s):
                gate_up(n + 1, 1 - s)
                down(n, s)

            pairs(pe, 1, N - 1, both)
            down(N - 1, (N - 1) % 2)
    core.drop(h2, x_hi, gu, gu_hi, dn, dn_hi, sg, hg, hg_hi, hg_lo, wt)

    row = core.sb("final_g", [P, D])
    load(core, [(row[:], a["final_norm_g"].partition_broadcast(P))])
    with nc.Block() as block:
        @block.vector
        def _(dve):
            link = linked(dve, core.sig("dve_chain"))
            for t in range(T):
                link(nc.vector.tensor_tensor(y[:, t, :], y[:, t, :], keep["gate_ffn_row"][:], ALU.mult))
                link(nc.vector.tensor_tensor(x[:, t, :], x[:, t, :], y[:, t, :], ALU.add))
    core.drop(y)
    normalise(core, [(P, x[:, t, :]) for t in range(T)], D, [x[:, t, :] for t in range(T)])
    with nc.Block() as block:
        @block.vector
        def _(dve):
            for t in range(T):
                nc.vector.tensor_tensor(x[:, t, :], x[:, t, :], row[:], ALU.mult)
    core.drop(row)



def second_mixer(core, a, keep):
    nc = core.nc
    x, cols = keep["x"], keep["cols"]
    TM = T + 1
    L = S + META
    rows = [P] * T + [META]
    toks = [slice(t * P, (t + 1) * P) for t in range(T)] + [slice(S, L)]
    all_tok = slice(0, S)

    def gains(name):
        at = COLS[name][0]
        return lambda k: cols[:, at + k:at + k + 1]

    meta = core.sb("meta", [META, D])
    load(core, [(meta[:], a["meta"])])
    hT = core.sb("hT_2", [P, KD, L])
    norm_turned(core, [(P, x[:, t, :]) for t in range(T)] + [(META, meta[:])], D, hT,
                [(0, T, 0, gains("g_mix_2"), None), (T, 1, S, gains("g_mix_2"), None)])
    core.drop(meta)
    hidden = Halves(core, hT, "hT_2")

    def plain(dst, engine):
        if engine == "act":
            return lambda ps, link: nc.scalar.activation(dst, ps, ACT.Copy)
        return lambda ps, link: nc.vector.tensor_copy(dst, ps)

    def token_block(w, at, n, dst, d0, n_tiles, engine="dve", k_chunks=KD, src=None):
        src = hidden if src is None else src
        return (dram_rows(w, at, at + n),
                [tokens_unit(src, k_chunks, toks[t], n, engine, plain(dst[0:rows[t], t, d0:d0 + n], engine))
                 for t in range(n_tiles)])

    cq, ckv = core.sb("c_q", [P, T, QL]), core.sb("c_kv", [P, TM, KVL + MROPE])
    w = a["w_in_2"]
    project(core, [token_block(w, 0, QL, cq, 0, T), token_block(w, QL, KVL + MROPE, ckv, 0, TM, "act")], [hidden])
    cqT, ckvT = core.sb("c_qT", [P, QL // P, S]), core.sb("c_kvT", [P, KVL // P, L])
    norm_turned(core, [(P, cq[:, t, :]) for t in range(T)], QL, cqT, [(0, T, 0, gains("g_q_lora"), None)])
    norm_turned(core, [(rows[t], ckv[0:rows[t], t, 0:KVL]) for t in range(TM)], KVL, ckvT,
                [(0, T, 0, gains("g_kv_lora"), None), (T, 1, S, gains("g_kv_lora"), None)])
    q, kv = core.sb("mla_q", [P, T, MH, MQK]), core.sb("mla_kv", [P, TM, MH, P])
    kv_flat, q_flat = kv[:].rearrange("p t h d -> p t (h d)"), q[:].rearrange("p t h d -> p t (h d)")
    hq, hkv = Halves(core, cqT, "c_qT"), Halves(core, ckvT, "c_kvT")
    project(core, [token_block(a["w_uq"], b * QL, QL, q_flat, b * QL, T, k_chunks=3, src=hq) for b in range(2)]
            + [token_block(a["w_ukv"], b * 512, 512, kv_flat, b * 512, TM, "act", k_chunks=2, src=hkv)
               for b in range(2)], [hq, hkv])
    core.drop(cq, cqT, ckvT, hq.hi, hkv.hi)

    kk = core.sb("mla_k", [P, TM, MH, MQK])
    g_rows = core.sb("g_qk", [P, 2, MQK])
    tab = core.sb("mla_rope", [P, 2, TM, MROPE // 2])
    sq = core.sb("mla_sq", [P, MH, MQK])
    t1, t2 = core.sb("t1", [P, MH, 16]), core.sb("t2", [P, MH, 16])
    rot = core.sb("rot", [P, MH, MROPE])
    st = core.sb("mla_stat", [P, 3, 2 * TM, MH])
    load(core, [(g_rows[:], a["g_qk"].partition_broadcast(P)), (tab[:], a["k_rope_mla"])])
    items = [(q, t, 0, t) for t in range(T)] + [(kk, t, 1, TM + t) for t in range(TM)]
    chain, var_done, root = core.sig("dve_chain"), core.sig("mla_var"), core.sig("root")
    b_root = root.base
    with nc.Block() as block:
        @block.vector
        def _(dve):
            link = linked(dve, chain)
            link(nc.vector.memset(st[:], 1.0))
            link(nc.vector.tensor_scalar(g_rows[:, 0, :], g_rows[:, 0, :], MQK ** -0.5, None, ALU.mult))
            for t in range(TM):
                r = slice(0, rows[t])
                link(nc.vector.tensor_copy(kk[r, t, :, 0:MNOPE], kv[r, t, :, 0:MNOPE]))
                link(nc.vector.tensor_copy(kk[r, t, :, MNOPE:MQK],
                                           ckv[r, t, KVL:].unsqueeze(1).to_broadcast([rows[t], MH, MROPE])))
            for src, t, _, i in items:
                r = slice(0, rows[t])
                link(nc.vector.tensor_tensor(sq[r], src[r, t], src[r, t], ALU.mult))
                link(nc.vector.tensor_reduce(st[r, 0, i, :], sq[r], AX, ALU.add))
            nc.vector.tensor_scalar(st[:, 1], st[:, 0], 1.0 / MQK, EPS, ALU.mult, ALU.add).then_inc(var_done.sem, 1)
            dve.wait_ge(root.sem, b_root + 1)
            link(nc.vector.reciprocal(st[:, 1], st[:, 2]))
            for src, t, which, i in items:
                r, n = slice(0, rows[t]), rows[t]
                link(nc.vector.tensor_tensor(src[r, t], src[r, t], st[r, 1, i, :].unsqueeze(2).to_broadcast([n, MH, MQK]),
                                             ALU.mult))
                link(nc.vector.tensor_tensor(src[r, t], src[r, t],
                                             g_rows[r, which, :].unsqueeze(1).to_broadcast([n, MH, MQK]), ALU.mult))
                cos, sin = (tab[r, j, t, :].unsqueeze(1).to_broadcast([n, MH, 16]) for j in range(2))
                rope(nc, link, src[r, t, :, MNOPE:MNOPE + 16], src[r, t, :, MNOPE + 16:MQK], cos, sin,
                     rot[r, :, 0:16], rot[r, :, 16:32], t1[r], t2[r])
                link(nc.vector.tensor_copy(src[r, t, :, MNOPE:MQK], rot[r]))

        @block.scalar
        def _(act):
            act.wait_ge(var_done.sem, 1)
            nc.scalar.activation(st[:, 2], st[:, 1], ACT.Sqrt).then_inc(root.sem, 1)
    root.base += 1
    core.drop(g_rows, tab, sq, t1, t2, rot, st, ckv)

    qT, kT, kmT = core.sb("mla_qT", [MQK, MH, S]), core.sb("mla_kT", [MQK, MH, S]), core.sb("mla_kmT", [MQK, MH, META])
    jobs = []
    for h in range(MH):
        jobs.append(([(q[:, t, h, :], t * P) for t in range(T)], copied(nc, qT[:, h, :], MQK, S)))
        jobs.append(([(kk[:, t, h, :], t * P) for t in range(T)], copied(nc, kT[:, h, :], MQK, S)))
    jobs.append(([(kk[0:META, T, h, :], h * META) for h in range(MH)],
                 copied(nc, kmT[:].rearrange("p h m -> p (h m)"), MQK, MH * META)))
    turn(core, jobs)
    core.drop(q, kk)
    causal = core.sb("causal", [P, S])
    load(core, [(causal[:], a["k_causal"])])
    omT = core.sb("mla_outT", [P, 4, S])
    tiles = []
    for j in range(T):
        near = (j + 1) * P
        tiles.append([(qT[:, h, toks[j]], kT[:, h, 0:near], near, kmT[:, h, :], META, causal[:, S - near:S],
                       [kv[:, t, h, MNOPE:P] for t in range(j + 1)], [kv[0:META, T, h, MNOPE:P]]) for h in range(MH)])
    attend(core, tiles, MV, [omT[:, c, toks[j]] for j in range(T) for c in range(4)])
    core.drop(qT, kT, kmT, kv, causal)
    at = QL + KVL + MROPE
    RW = RH * RDK
    rq, rk = core.sb("ret_q", [P, T, RH, RDK]), core.sb("ret_k", [P, TM, RH, RDK])
    rv = core.sb("ret_v", [P, TM, RH * RDV])
    rq_flat, rk_flat = (r[:].rearrange("p t h d -> p t (h d)") for r in (rq, rk))
    project(core, [token_block(w, at, RW, rq_flat, 0, T), token_block(w, at + RW, RW, rk_flat, 0, TM, "act")]
            + [token_block(w, at + 2 * RW + b * 512, 512, rv, b * 512, TM, ("dve", "act")[b]) for b in range(2)])
    rqr, rkr = core.sb("ret_q_rope", [P, T, RH, RDK]), core.sb("ret_k_rope", [P, TM, RH, RDK])
    kz = core.sb("ret_kz", [P, TM, RH, RDK])
    tab = core.sb("ret_rope", [P, 2, TM, 32])
    zeta = core.sb("zeta", [P, 2, RH])
    t1, t2 = core.sb("t1", [P, RH, 32]), core.sb("t2", [P, RH, 32])
    load(core, [(tab[:], a["k_rope_ret"]), (zeta[:], a["k_zeta"])])
    with nc.Block() as block:
        @block.vector
        def _(dve):
            link = linked(dve, chain)
            for src, dst, n_tiles in ((rq, rqr, T), (rk, rkr, TM)):
                for t in range(n_tiles):
                    r, n = slice(0, rows[t]), rows[t]
                    cos, sin = (tab[r, j, t, :].unsqueeze(1).to_broadcast([n, RH, 32]) for j in range(2))
                    rope(nc, link, src[r, t, :, 0:32], src[r, t, :, 32:64], cos, sin, dst[r, t, :, 0:32],
                         dst[r, t, :, 32:64], t1[r], t2[r])
            for t in range(TM):
                r, n = slice(0, rows[t]), rows[t]
                link(nc.vector.tensor_scalar(rkr[r, t], rkr[r, t], RDK ** -0.5, None, ALU.mult))
                link(nc.vector.tensor_tensor(kz[r, t], rkr[r, t],
                                             zeta[r, t // T, :].unsqueeze(2).to_broadcast([n, RH, RDK]), ALU.mult))
    core.drop(rq, rk, tab, zeta, t1, t2)
    rqT, rkT = core.sb("ret_qT", [P, 4, S]), core.sb("ret_kT", [P, 4, S])
    jobs = []
    for c in range(4):
        for src, dst in ((rqr, rqT), (rkr, rkT)):
            jobs.append(([(src[:, t, 2 * c:2 * c + 2, :].rearrange("p h d -> p (h d)"), t * P) for t in range(T)],
                         copied(nc, dst[:, c, :], P, S)))
    turn(core, jobs)
    core.drop(rqr, rkr)
    qx = core.sb("ret_qx", [P, 4, S])
    decay = core.sb("decay", [P, 2, 4, P])
    xi = core.sb("xi", [P, 4, P])
    gamma = core.sb("gamma", [P, 4])
    state = core.sb("state", [P, 4, 2, P])
    prod = core.sb("state_decayed", [P, 4, P])
    sd = core.sb("ret_scores", [P, 2, 4, P])
    ry = core.sb("ret_y", [P, T, RH * RDV])
    load(core, [(decay[:], a["k_decay"]), (xi[:], a["k_xi"]), (gamma[:], a["k_gamma"])])
    scored, kv_mm, y_mm, decayed, state_done, y_out = (core.sig(n) for n in (
        "ret_scored", "ret_kv_mm", "ret_y_mm", "ret_decayed", "ret_state", "ret_y_out"))
    with (core.psum("ps_rs", [P, 2, 4, P], F32) as ps_s, core.psum("ps_kv", [P, 4, P], F32) as ps_kv,
          core.psum("ps_ry", [P, 2, 512], F32) as ps_y, nc.Block() as block):
        @block.tensor
        def _(pe):
            pe.wait_ge(decayed.sem, 1)
            for n in range(T):
                src, r = (T, slice(0, META)) if n == 0 else (n - 1, slice(0, P))
                if n >= 1:
                    pe.wait_ge(state_done.sem, n)
                    pe.wait_ge(decayed.sem, n + 1)
                for h in range(RH):
                    c, p0 = h // 2, h % 2 * RDK
                    last = nc.tensor.matmul(ps_kv[p0:p0 + RDK, c, :], kz[r, src, h, :],
                                            rv[r, src, h * RDV:(h + 1) * RDV], start=True, stop=True)
                last.then_inc(kv_mm.sem, 1)
                for h in range(RH):
                    c, p0 = h // 2, h % 2 * RDK
                    last = nc.tensor.matmul(ps_s[:, h % 2, c, :], rkT[p0:p0 + RDK, c, toks[n]],
                                            rqT[p0:p0 + RDK, c, toks[n]], start=True, stop=True)
                last.then_inc(scored.sem, 1)
                pe.wait_ge(state_done.sem, n + 1)
                pe.wait_ge(decayed.sem, n + 2)
                if n >= 1:
                    pe.wait_ge(y_out.sem, n)
                for h in range(RH):
                    c, hv = h // 2, slice(h % 4 * RDV, (h % 4 + 1) * RDV)
                    nc.tensor.matmul(ps_y[:, h // 4, hv], sd[:, h % 2, c, :], rv[:, n, h * RDV:(h + 1) * RDV],
                                     start=True, stop=False)
                    last = nc.tensor.matmul(ps_y[:, h // 4, hv], qx[:, c, toks[n]], state[:, c, h % 2, :],
                                            start=False, stop=True)
                last.then_inc(y_mm.sem, 1)

        @block.vector
        def _(dve):
            link = linked(dve, chain)
            link(nc.vector.memset(state[:], 0.0))
            for c in range(4):
                ins = nc.vector.tensor_tensor(qx[:, c, :].rearrange("p (t m) -> p t m", t=T),
                                              rqT[:, c, :].rearrange("p (t m) -> p t m", t=T),
                                              xi[:, c, :].unsqueeze(1).to_broadcast([P, T, P]), ALU.mult)
                if c < 3:
                    link(ins)
            ins.then_inc(decayed.sem, 1)
            for n in range(T):
                dve.wait_ge(kv_mm.sem, n + 1)
                if n >= 1:
                    dve.wait_ge(y_mm.sem, n)
                for half in range(2):
                    pp = slice(half * RDK, (half + 1) * RDK)
                    if n == 0:
                        link(nc.vector.tensor_copy(state[pp, :, half, :], ps_kv[pp]))
                    else:
                        link(nc.vector.tensor_tensor(prod[pp], state[pp, :, half, :],
                                                     gamma[pp, :].unsqueeze(2).to_broadcast([RDK, 4, P]), ALU.mult))
                        link(nc.vector.tensor_tensor(state[pp, :, half, :], prod[pp], ps_kv[pp], ALU.add))
                dve.sem_inc(state_done.sem, 1)
                dve.wait_ge(scored.sem, n + 1)
                link(nc.vector.tensor_tensor(sd[:, 0], ps_s[:, 0], decay[:, 0], ALU.mult))
                nc.vector.tensor_tensor(sd[:, 1], ps_s[:, 1], decay[:, 1], ALU.mult).then_inc(decayed.sem, 1)

        @block.scalar
        def _(act):
            for n in range(T):
                act.wait_ge(y_mm.sem, n + 1)
                nc.scalar.activation(ry[:, n, :], ps_y[:].rearrange("p a b -> p (a b)"), ACT.Copy) \
                    .then_inc(y_out.sem, 1)
    core.drop(kz, rqT, rkT, rv, qx, decay, xi, gamma, state, prod, sd)

    rg = core.sb("ret_gate", [P, T, RH * RDV])
    at += 2 * RW + RH * RDV
    project(core, [(dram_rows(w, at + b * 512, at + (b + 1) * 512),
                    [tokens_unit(hidden, KD, toks[t], 512, "act",
                                 lambda ps, link, t=t, b=b: nc.scalar.activation(rg[:, t, b * 512:(b + 1) * 512], ps,
                                                                                 ACT.Silu)) for t in range(T)])
                   for b in range(2)])
    g_gn = core.sb("g_ret", [P, RH * RDV])
    st = core.sb("gn_stats", [P, T * RH, 6])
    ag = core.sb("gn_mean_var", [P, T * RH, 4])
    load(core, [(g_gn[:], a["g_ret_gn"].partition_broadcast(P))])
    b_root = root.base
    gn_var = core.sig("gn_var")
    with nc.Block() as block:
        @block.vector
        def _(dve):
            link = linked(dve, chain)
            for i in range(T * RH):
                t, hv = i // RH, slice(i % RH * RDV, (i % RH + 1) * RDV)
                link(nc.vector.bn_stats(st[:, i, :], ry[:, t, hv]))
                link(nc.vector.bn_aggr(ag[:, i, 0:2], st[:, i, :]))
            nc.vector.tensor_scalar(ag[:, :, 1:2], ag[:, :, 1:2], EPS, None, ALU.add).then_inc(gn_var.sem, 1)
            for t in range(T):
                link(nc.vector.tensor_tensor(rg[:, t, :], rg[:, t, :], g_gn[:], ALU.mult))
            dve.wait_ge(root.sem, b_root + 1)
            link(nc.vector.reciprocal(ag[:, :, 3:4], ag[:, :, 2:3]))
            for i in range(T * RH):
                t, hv = i // RH, slice(i % RH * RDV, (i % RH + 1) * RDV)
                link(nc.vector.tensor_scalar(ry[:, t, hv], ry[:, t, hv], ag[:, i, 0:1], ag[:, i, 3:4], ALU.subtract,
                                             ALU.mult))
            for t in range(T):
                link(nc.vector.tensor_tensor(ry[:, t, :], ry[:, t, :], rg[:, t, :], ALU.mult))

        @block.scalar
        def _(act):
            act.wait_ge(gn_var.sem, 1)
            nc.scalar.activation(ag[:, :, 2:3], ag[:, :, 1:2], ACT.Sqrt).then_inc(root.sem, 1)
    root.base += 1
    core.drop(rg, g_gn, st, ag)
    yT = core.sb("ret_yT", [P, KD, S])
    turn(core, [([(ry[:, t, c * P:(c + 1) * P], t * P) for t in range(T)], copied(nc, yT[:, c, :], P, S))
                for c in range(KD)])
    core.drop(ry)

    za, zr = core.sb("gate_za", [P, KD, S]), core.sb("gate_zr", [P, KD, S])
    at += RH * RDV
    blocks = []
    for dst, c0 in ((za, at), (zr, at + D)):
        for b in range(4):
            blocks.append((dram_rows(w, c0 + b * 256, c0 + (b + 1) * 256),
                           [features_unit(hidden, KD, m, all_tok, "act",
                                          lambda ps, link, d=dst[:, 2 * b + m, :]: nc.scalar.activation(d, ps, ACT.Sigmoid))
                            for m in range(2)]))
    project(core, blocks)
    core.drop(hT, hidden.hi)
    merge(core, za, zr, (omT, 4, a["w_mla_out"]), (yT, KD, a["w_ret_out"]))
    core.drop(omT, yT, zr)
    merged = Halves(core, za, "merged_2")
    project(core, [(dram_rows(a["w_mix_out"], b * 512, (b + 1) * 512),
                    [tokens_unit(merged, KD, toks[t], 512, "dve",
                                 lambda ps, link, d=x[:, t, b * 512:(b + 1) * 512]:
                                 nc.vector.tensor_tensor(d, d, ps, ALU.add)) for t in range(T)]) for b in range(2)], [merged])
    core.drop(za, merged.hi)


def merge(core, ga, gb, first, second):
    nc = core.nc

    def gated(m):
        return lambda ps, link: nc.vector.tensor_tensor(ga[:, m, :], ps, ga[:, m, :], ALU.mult)

    def gated_sum(m):
        def evacuate(ps, link):
            link(nc.vector.tensor_tensor(gb[:, m, :], ps, gb[:, m, :], ALU.mult))
            return nc.vector.tensor_tensor(ga[:, m, :], ga[:, m, :], gb[:, m, :], ALU.add)
        return evacuate

    h1, h2 = Halves(core, first[0], "x1"), Halves(core, second[0], "x2")
    blocks = []
    for (src, k_chunks, w), evacuate in (((h1, *first[1:]), gated), ((h2, *second[1:]), gated_sum)):
        for b in range(4):
            blocks.append((dram_rows(w, b * 256, (b + 1) * 256),
                           [features_unit(src, k_chunks, m, slice(0, S), "dve", evacuate(2 * b + m))
                            for m in range(2)]))
    project(core, blocks, [h1, h2])
    core.drop(h1.hi, h2.hi)



GE = 2
NG = PNK // GE


def peer(core, a, keep, scratch):
    nc = core.nc
    x, cols, ident = keep["x"], keep["cols"], core.ident
    hT = core.sb("peer_xT", [P, KD, S])
    x_hi = core.sb("peer_xT_hi", [P, KD, S], F32R)
    chT = core.sb("chosenT", [P, 3, S])
    g0 = COLS["g_ffn_2"][0]
    norm_turned(core, [(P, x[:, t, :]) for t in range(T)], D, hT, [(0, T, 0, lambda k: cols[:, g0 + k:g0 + k + 1], None)])
    halves = Halves(core, hT, "peer_xT", x_hi)
    qT = core.sb("peer_qT", [P, PH, S])
    project(core, [(dram_rows(a["w_peer_q"], b * 512, (b + 1) * 512),
                    [features_unit(halves, KD, m, slice(0, S), ("act", "dve")[m % 2],
                                   (lambda ps, link, d=qT[:, 4 * b + m, :]: nc.scalar.activation(d, ps, ACT.Copy))
                                   if m % 2 == 0 else
                                   (lambda ps, link, d=qT[:, 4 * b + m, :]: nc.vector.tensor_copy(d, ps)))
                     for m in range(4)]) for b in range(2)], [halves])
    x_lo = halves.lo

    keys = core.sb("keys", [P, 2 * PNK])
    s = core.sb("key_scores", [P, 2, 2 * PNK])
    less = core.sb("less", [P, 2 * PNK])
    val = core.sb("top_val", [P, 2, PK])
    index = core.sb("top_index", [P, T, 2, PH, PK], U32)
    cand = core.sb("cand", [P, PK, PK])
    best = core.sb("best", [P, T, PH, PK])
    best_at = core.sb("best_at", [P, T, PH, PK], U32)
    keys_in, clear = core.sig("keys_in"), core.sig("keys_clear")
    key_mm, key_out, taken, chain = core.sig("key_mm"), core.sig("key_out"), core.sig("key_taken"), core.sig("dve_chain")
    NT = PH * T
    with core.psum("ps_key", [P, 2, S], F32) as ps, nc.Block() as block:
        @block.sync
        def _(sp):
            sp.wait_ge(clear.sem, 1)
            for j in range(2):
                sp.dma_start(keys[j * 64:(j + 1) * 64, j * PNK:(j + 1) * PNK], a["keys"][j]).then_inc(keys_in.sem, 16)

        @block.tensor
        def _(pe):
            pe.wait_ge(keys_in.sem, 32)
            for n in range(NT):
                if n >= 2:
                    pe.wait_ge(key_out.sem, n - 1)
                t, h = n // PH, n % PH
                nc.tensor.matmul(ps[:, n % 2, 0:2 * PNK], qT[:, h, t * P:(t + 1) * P], keys[:], start=True,
                                 stop=True).then_inc(key_mm.sem, 1)

        @block.scalar
        def _(act):
            for n in range(NT):
                act.wait_ge(key_mm.sem, n + 1)
                if n >= 2:
                    act.wait_ge(taken.sem, n - 1)
                nc.scalar.activation(s[:, n % 2, :], ps[:, n % 2, 0:2 * PNK], ACT.Copy).then_inc(key_out.sem, 1)

        @block.vector
        def _(dve):
            link = linked(dve, chain)

            def top16(src, spare, values, places):
                link(nc.vector.max(values[:, 0:8], src))
                link(nc.vector.max_index(places[:, 0:8], values[:, 0:8], src))
                link(nc.vector.match_replace(spare, values[:, 0:8], src, NEG))
                link(nc.vector.max(values[:, 8:16], spare))
                link(nc.vector.max_index(places[:, 8:16], values[:, 8:16], spare))

            nc.vector.memset(keys[:], 0.0).then_inc(clear.sem, 1)
            for n in range(NT):
                t, h = n // PH, n % PH
                dve.wait_ge(key_out.sem, n + 1)
                for j in range(2):
                    top16(s[:, n % 2, j * PNK:(j + 1) * PNK], less[:, 0:PNK], val[:, j, :], index[:, t, j, h, :])
                ins = nc.vector.tensor_tensor(cand[:], val[:, 0, :].unsqueeze(2).to_broadcast([P, PK, PK]),
                                              val[:, 1, :].unsqueeze(1).to_broadcast([P, PK, PK]), ALU.add)
                ins.then_inc(taken.sem, 1)
                dve.wait_ge(taken.sem, n + 1)
                top16(cand[:].rearrange("p a b -> p (a b)"), less[:], best[:, t, h, :], best_at[:, t, h, :])
    core.drop(keys, s, less, val, cand, qT)

    at = core.sb("at", [P, 2, PH, PK], U32)
    atf = core.sb("at_f", [P, 2, PH, PK])
    indexf = core.sb("index_f", [P, 2, PH, PK])
    iota = core.sb("iota16", [P, PK])
    hot = core.sb("hot", [P, PH, PK, PK])
    chosen = core.sb("chosen", [P, 3, T, PH, PK])
    gsum = core.sb("gate_sum", [P, 2, PH])
    load(core, [(iota[:], a["k_iota"][:, 0:PK])])
    shifted, exped = core.sig("gate_shifted"), core.sig("gate_exped")
    with nc.Block() as block:
        @block.vector
        def _(dve):
            link = linked(dve, chain)
            for t in range(T):
                ins = nc.vector.tensor_tensor(chosen[:, 2, t], best[:, t],
                                              best[:, t, :, 0:1].to_broadcast([P, PH, PK]), ALU.subtract)
                ins.then_inc(shifted.sem, 1)
            for t in range(T):
                link(nc.vector.tensor_single_scalar(at[:, 0], best_at[:, t], 4, ALU.logical_shift_right))
                link(nc.vector.tensor_single_scalar(at[:, 1], best_at[:, t], PK - 1, ALU.bitwise_and))
                link(nc.vector.tensor_copy(atf[:], at[:]))
                link(nc.vector.tensor_copy(indexf[:], index[:, t]))
                for j in range(2):
                    for h in range(PH):
                        link(nc.vector.tensor_tensor(hot[:, h], atf[:, j, h, :].unsqueeze(2).to_broadcast([P, PK, PK]),
                                                     iota[:].unsqueeze(1).to_broadcast([P, PK, PK]), ALU.is_equal))
                    for h in range(PH):
                        link(nc.vector.tensor_tensor(hot[:, h], hot[:, h],
                                                     indexf[:, j, h, :].unsqueeze(1).to_broadcast([P, PK, PK]),
                                                     ALU.mult))
                    link(nc.vector.tensor_reduce(chosen[:, j, t], hot[:], AX, ALU.add))
                dve.wait_ge(exped.sem, t + 1)
                link(nc.vector.tensor_reduce(gsum[:, 0], chosen[:, 2, t], AX, ALU.add))
                link(nc.vector.reciprocal(gsum[:, 1], gsum[:, 0]))
                link(nc.vector.tensor_tensor(chosen[:, 2, t], chosen[:, 2, t],
                                             gsum[:, 1].unsqueeze(2).to_broadcast([P, PH, PK]), ALU.mult))

        @block.scalar
        def _(act):
            for t in range(T):
                act.wait_ge(shifted.sem, t + 1)
                nc.scalar.activation(chosen[:, 2, t], chosen[:, 2, t], ACT.Exp).then_inc(exped.sem, 1)
    turn(core, [([(chosen[:, j, t].rearrange("p h k -> p (h k)"), t * P) for t in range(T)],
                 copied(nc, chT[:, j, :], P, S)) for j in range(3)])
    core.drop(at, atf, indexf, iota, hot, chosen, gsum, index, best, best_at)

    place_gates(core, a, chT, scratch["gates"])
    core.drop(chT)
    peer_products(core, a, x, x_hi, x_lo, scratch["gates"])
    core.drop(hT, x_hi)


def place_gates(core, a, chT, gates):
    nc = core.nc
    B = 4
    NB = P // B
    iota = core.sb("iota", [P, PNK])
    hot1, hot2 = core.sb("hot_e1", [P, 2, B, PNK]), core.sb("hot_e2", [P, 2, B, PNK])
    tile = core.sb("gate_tile", [P, 2, PNK, P])
    iota_in, hot1_done, hot2_done, gate_mm, gate_out = (core.sig(n) for n in (
        "iota_in", "hot1_done", "hot2_done", "gate_mm", "gate_out"))
    gates_out = [core.sig("gates_stored_even"), core.sig("gates_stored_odd")]
    with core.psum("ps_gates", [P, 2, B, PNK], F32) as ps, nc.Block() as block:
        @block.sync
        def _(sp):
            sp.dma_start(iota[:], a["k_iota"]).then_inc(iota_in.sem, 16)
            for t in range(T):
                sp.wait_ge(gate_out.sem, NB * (t + 1))
                sp.dma_start(gates[:, :, t * P:(t + 1) * P], tile[:, t % 2]).then_inc(gates_out[t % 2].sem, 16)
            for s in range(2):
                sp.wait_ge(gates_out[s].sem, 16 * T // 2)

        def steps(eng, step, loop_from=1):
            for b in range(2 * loop_from):
                step(b, b % 2, True)
            with eng.Fori(loop_from, S // B // 2) as i:
                for s in range(2):
                    step(2 * i + s, s, False)

        @block.vector
        def _(dve):
            dve.wait_ge(iota_in.sem, 16)

            def step(b, s, first):
                if not first:
                    dve.wait_ge(gate_mm.sem, b - 1)
                nc.vector.tensor_tensor(hot1[:, s], iota[:].unsqueeze(1).to_broadcast([P, B, PNK]),
                                        chT[:, 0, bass.ds(b * B, B)].unsqueeze(2).to_broadcast([P, B, PNK]),
                                        ALU.is_equal).then_inc(hot1_done.sem, 1)
                for i in range(B):
                    last = nc.vector.tensor_scalar(hot2[:, s, i], iota[:], chT[:, 1, bass.ds(b * B + i, 1)],
                                                   chT[:, 2, bass.ds(b * B + i, 1)], ALU.is_equal, ALU.mult)
                last.then_inc(hot2_done.sem, 1)

            steps(dve, step)

        @block.tensor
        def _(pe):
            def step(b, s, first):
                pe.wait_ge(hot1_done.sem, b + 1)
                pe.wait_ge(hot2_done.sem, b + 1)
                if not first:
                    pe.wait_ge(gate_out.sem, b - 1)
                for i in range(B):
                    last = nc.tensor.matmul(ps[:, s, i], hot1[:, s, i], hot2[:, s, i], start=True, stop=True)
                last.then_inc(gate_mm.sem, 1)

            steps(pe, step)

        @block.scalar
        def _(act):
            for t in range(T):
                if t >= 2:
                    act.wait_ge(gates_out[t % 2].sem, 16 * (t // 2))
                with act.Fori(0, NB // 2) as i:
                    for s in range(2):
                        act.wait_ge(gate_mm.sem, 2 * i + (NB * t + s + 1))
                        nc.scalar.activation(tile[:, t % 2, :, bass.ds((2 * i + s) * B, B)],
                                             ps[:, s].rearrange("p b e -> p e b"), ACT.Copy).then_inc(gate_out.sem, 1)
    core.drop(iota, hot1, hot2, tile)


def peer_products(core, a, x, x_hi, x_lo, gates):
    nc = core.nc
    W = GE * D
    u = core.sb("u", [P, 2, W])
    u_hi, u_lo = core.sb("u_hi", [P, 2, W], F32R), core.alias(u, "u_lo", [P, 2, W], F32R)
    v = core.sb("v", [P, 2, W])
    v_hi, v_lo = core.sb("v_hi", [P, 2, W], F32R), core.alias(v, "v_lo", [P, 2, W], F32R)
    g = core.sb("g", [P, 2, GE, S])
    act_out = core.sb("act_out", [P, GE, S])
    c_hi, c_lo = core.sb("coef_hi", [P, 2, GE, S], F32R), core.sb("coef_lo", [P, 2, GE, S], F32R)
    u_in, v_in, g_in = ([core.sig(f"peer_{n}_even"), core.sig(f"peer_{n}_odd")] for n in "uvg")
    (u_hi_done, u_lo_done, v_hi_done, v_lo_done, u_mm, v_mm, gelu_done, coef_done, coef_hi_done, coef_lo_done,
     added) = (core.sig("peer_" + n) for n in ("u_hi_done", "u_lo_done", "v_hi_done", "v_lo_done", "u_mm", "v_mm",
                                              "gelu_done", "coef_done", "coef_hi_done", "coef_lo_done", "added"))
    with (core.psum("ps_act", [P, 4, S], F32) as ps_a, core.psum("ps_y", [P, 4, S], F32) as ps_y,
          nc.Block() as block):
        @block.sync
        def _(sp):
            def loads(n, s, first):
                def part(src):
                    return src[bass.ds(n, 1)].rearrange("g p n -> (g p) n")
                if not first:
                    sp.wait_ge(u_mm.sem, GE * n - GE)
                sp.dma_start(u[:, s, :], part(a["peer_u"])).then_inc(u_in[s].sem, 16)
                if not first:
                    sp.wait_ge(coef_done.sem, GE * n - GE)
                sp.dma_start(g[:, s].rearrange("p j t -> p (j t)"),
                             part(gates.rearrange("p (g j) t -> g p (j t)", j=GE))).then_inc(g_in[s].sem, 16)
                if not first:
                    sp.wait_ge(v_mm.sem, 8 * n - 8)
                sp.dma_start(v[:, s, :], part(a["peer_v"])).then_inc(v_in[s].sem, 16)

            for n in range(2):
                loads(n, n, True)
            with sp.Fori(1, NG // 2) as i:
                for s in range(2):
                    loads(2 * i + s, s, False)

        @block.scalar
        def _(act):
            def high(dst, src, arrived, value, s, done):
                act.wait_ge(arrived[s].sem, value)
                nc.scalar.activation(dst[:, s, :], src[:, s, :], ACT.Copy).then_inc(done.sem, 1)

            def coefficients(n, s, first):
                for j in range(GE):
                    act.wait_ge(u_mm.sem, GE * n + (j + 1))
                    if not (first and n == 0):
                        act.wait_ge(coef_lo_done.sem, GE * n + (j + 1 - GE))
                    nc.scalar.activation(act_out[:, j, :], ps_a[:, 2 * s + j, :], ACT.Gelu).then_inc(gelu_done.sem, 1)
                for j in range(GE):
                    act.wait_ge(coef_done.sem, GE * n + (j + 1))
                    if not first:
                        act.wait_ge(v_mm.sem, 8 * n - 8)
                    nc.scalar.activation(c_hi[:, s, j, :], act_out[:, j, :], ACT.Copy).then_inc(coef_hi_done.sem, 1)

            high(u_hi, u, u_in, 16, 0, u_hi_done)
            high(u_hi, u, u_in, 16, 1, u_hi_done)
            high(v_hi, v, v_in, 16, 0, v_hi_done)
            for n in range(2):
                coefficients(n, n, True)
                high(u_hi, u, u_in, 32, n, u_hi_done)
                high(v_hi, v, v_in, 16 if n == 0 else 32, 1 - n, v_hi_done)
            with act.Fori(1, NG // 2 - 1) as i:
                for s in range(2):
                    coefficients(2 * i + s, s, False)
                    high(u_hi, u, u_in, 16 * i + 32, s, u_hi_done)
                    high(v_hi, v, v_in, 16 * i + 16 * (s + 1), 1 - s, v_hi_done)
            coefficients(NG - 2, 0, False)
            high(v_hi, v, v_in, 16 * (NG // 2), 1, v_hi_done)
            coefficients(NG - 1, 1, False)

        @block.vector
        def _(dve):
            def low(n, s, lo, raw, hi, hi_done, done):
                dve.wait_ge(hi_done.sem, n + 1)
                nc.vector.tensor_tensor(lo[:, s, :], raw[:, s, :], hi[:, s, :].bitcast(F32), ALU.subtract) \
                    .then_inc(done.sem, 1)

            def coefficients(n, s, arrived):
                dve.wait_ge(g_in[s].sem, arrived)
                for j in range(GE):
                    dve.wait_ge(gelu_done.sem, GE * n + (j + 1))
                    nc.vector.tensor_tensor(act_out[:, j, :], act_out[:, j, :], g[:, s, j, :], ALU.mult) \
                        .then_inc(coef_done.sem, 1)
                for j in range(GE):
                    dve.wait_ge(coef_hi_done.sem, GE * n + (j + 1))
                    nc.vector.tensor_tensor(c_lo[:, s, j, :], act_out[:, j, :], c_hi[:, s, j, :].bitcast(F32),
                                            ALU.subtract).then_inc(coef_lo_done.sem, 1)

            def add(n, first):
                for i in range(2 * T):
                    t, sl = i // 2, slice(i % 2 * S, (i % 2 + 1) * S)
                    dve.wait_ge(v_mm.sem, 8 * n + (i + 1))
                    if not (first and n == 0):
                        dve.wait_ge(added.sem, 8 * n + (i - 7))
                    nc.vector.tensor_tensor(x[:, t, sl], x[:, t, sl], ps_y[:, i % 4, :], ALU.add) \
                        .then_inc(added.sem, 1)

            def u_low(n, s):
                low(n, s, u_lo, u, u_hi, u_hi_done, u_lo_done)

            def v_low(n, s):
                low(n, s, v_lo, v, v_hi, v_hi_done, v_lo_done)

            u_low(0, 0)
            u_low(1, 1)
            v_low(0, 0)
            for n in range(2):
                coefficients(n, n, 16)
                u_low(n + 2, n)
                v_low(n + 1, 1 - n)
                add(n, True)
            with dve.Fori(1, NG // 2 - 1) as i:
                for s in range(2):
                    n = 2 * i + s
                    coefficients(n, s, 16 * i + 16)
                    u_low(n + 2, s)
                    v_low(n + 1, 1 - s)
                    add(n, False)
            coefficients(NG - 2, 0, 16 * (NG // 2))
            v_low(NG - 1, 1)
            add(NG - 2, False)
            coefficients(NG - 1, 1, 16 * (NG // 2))
            add(NG - 1, False)

        @block.tensor
        def _(pe):
            def activations(n, s, first=False):
                pe.wait_ge(u_lo_done.sem, n + 1)
                for j in range(GE):
                    if not first:
                        pe.wait_ge(gelu_done.sem, GE * n + (j + 1 - 2 * GE))
                    for k in range(KD):
                        at = (j * KD + k) * P
                        last = three_pass(nc, ps_a[:, 2 * s + j, :], u_hi[:, s, at:at + P], u_lo[:, s, at:at + P],
                                          x_hi[:, k, :], x_lo[:, k, :], k == 0, k == KD - 1)
                    last.then_inc(u_mm.sem, 1)

            def values(n, s, first=False):
                pe.wait_ge(coef_lo_done.sem, GE * n + GE)
                pe.wait_ge(v_lo_done.sem, n + 1)
                for i in range(2 * T):
                    t, h = i // 2, i % 2
                    if not first or i >= 4:
                        pe.wait_ge(added.sem, 8 * n + (i - 3))
                    for j in range(GE):
                        at = j * D + h * S
                        last = three_pass(nc, ps_y[:, i % 4, :], c_hi[:, s, j, t * P:(t + 1) * P],
                                          c_lo[:, s, j, t * P:(t + 1) * P], v_hi[:, s, at:at + S],
                                          v_lo[:, s, at:at + S], j == 0, j == GE - 1)
                    last.then_inc(v_mm.sem, 1)

            activations(0, 0, True)
            activations(1, 1, True)
            values(0, 0, True)
            activations(2, 0)
            values(1, 1)
            with pe.Fori(1, NG // 2 - 1) as i:
                for s in range(2):
                    activations(2 * i + (s + 1), 1 - s)
                    values(2 * i + s, s)
            activations(NG - 1, 1)
            values(NG - 2, 0)
            values(NG - 1, 1)
    core.drop(u, u_hi, v, v_hi, g, act_out, c_hi, c_lo)



def build(nc, a, out, scratch):
    with ExitStack() as stack:
        core = Core(nc, stack)
        keep = {}
        for name, shape in (("ident", [P, P]), ("cols", [P, N_COLS]), ("x", [P, T, D]),
                            ("gain_mix", [P, 2, KD]), ("shift_mix", [P, 2, KD]), ("gain_ffn", [P, KD]),
                            ("shift_ffn", [P, KD]), ("gate_mix_row", [P, D]), ("gate_ffn_row", [P, D])):
            keep[name] = core.sb(name, shape)
        core.ident = keep["ident"]
        core.spread = {NAD: a["k_spread_4"], TINY: a["k_spread_2"]}
        load_constants(core, a, keep)
        modulation(core, a, keep)
        first_mixer(core, a, keep)
        experts(core, a, keep)
        second_mixer(core, a, keep)
        core.drop(*(keep[n] for n in ("gate_mix_row", "gate_ffn_row")))
        peer(core, a, keep, scratch)
        store(core, out, keep["x"])


def store(core, out, x):
    done = core.sig("stored")
    with core.nc.Block() as block:
        @block.sync
        def _(sp):
            sp.dma_start(out.rearrange("(t p) d -> p t d", p=P), x[:]).then_inc(done.sem, 16)
            sp.wait_ge(done.sem, 16)


def kernel(**inputs):
    import numpy as np
    import concourse.bacc as bacc
    from concourse.bass_utils import run_bass_kernel_spmd as run

    one = {n: np.asarray(v)[0] if n not in ("c_ctx", "final_norm_g", "meta_tokens_2") else np.asarray(v)
           for n, v in inputs.items()}

    def cols(v):
        return v.reshape(-1, P).T

    b_in = one["b_in"]
    parts = {"c": one["c"], "c_ctx": one["c_ctx"], "b_ada": one["b_ada"], "g_mix": one["norm_mix_g"],
             "g_ffn": one["norm_ffn_g"], "b_u": b_in[0:1024], "b_nq": b_in[2240:2752], "b_nk": b_in[2752:3264],
             "b_ga": b_in[3776:4800], "b_gb": b_in[4800:5824], "g_mix_2": one["g_mix_2"],
             "g_ffn_2": one["g_ffn_2"], "g_q_lora": one["g_q_lora_2"], "g_kv_lora": one["g_kv_lora_2"]}
    arrays = {
        "x": one["x"], "ctx": one["ctx"], "cols": np.concatenate([cols(parts[n]) for n in COLS], 1),
        "b_rows": np.concatenate([b_in[1024:2240], b_in[3264:3776]]),
        "b_gates": np.concatenate([one["b_ada"][2 * D:3 * D], one["b_ada"][5 * D:6 * D]]),
        "ln_rows": np.stack([one["sgu_ln_g"], one["sgu_ln_b"]]),
        "sgu_w": one["sgu_w_s"].transpose(2, 0, 1), "sgu_b": one["sgu_b_s"],
        "rpb": np.pad(one["na_rpb"][:, :, ::-1], ((0, 0), (0, 0), (48, 48))),
    }
    for n in ("w_ada", "w_in", "tiny_w_o", "w_up_a", "w_up_b", "w_out"):
        arrays[n] = one[n]
    arrays.update(tables(np))
    more_arrays(np, one, arrays)

    nc = bacc.Bacc("TRN2", target_bir_lowering=False, num_devices=1)
    sent, a = {}, {}
    for n, v in arrays.items():
        sent["in_" + n] = np.ascontiguousarray(v)
        a[n] = nc.dram_tensor("in_" + n, v.shape, mybir.dt.from_np(v.dtype), kind="ExternalInput").ap()
    out = nc.dram_tensor("out", (S, D), F32, kind="ExternalOutput").ap()
    build(nc, a, out, scratch_tensors(nc))
    r = run(nc, [sent], core_ids=[0])
    return r.results[0]["out"].reshape(1, S, D)


def scratch_tensors(nc):
    return {"gates": nc.dram_tensor("gates", (P, PNK, S), F32).ap()}


def more_arrays(np, one, arrays):
    def chunked(w):
        e, k, n = w.shape
        return w.reshape(e, k // P, P, n).transpose(0, 2, 1, 3).reshape(e, P, -1)

    with_shared = {w: np.concatenate([one["w_sh_" + w][None], one["w_e_" + w]]) for w in ("gate", "up", "down")}
    arrays["e_gu"] = np.concatenate([chunked(with_shared["gate"]), chunked(with_shared["up"])], 2)
    arrays["e_dn"] = chunked(with_shared["down"])
    arrays["peer_u"] = one["peer_u_2"].reshape(PNK, NG, GE, KD, P).transpose(1, 4, 2, 3, 0).reshape(NG, P, GE * D)
    arrays["peer_v"] = one["peer_v_2"].reshape(PNK, NG, GE * D).transpose(1, 0, 2)
    arrays["keys"] = np.stack([one["peer_keys_1_2"].T, one["peer_keys_2_2"].T])
    arrays["w_peer_q"] = one["w_peer_q_2"]
    arrays["meta"] = one["meta_tokens_2"]
    arrays["g_qk"] = np.stack([one["g_qk_q_2"], one["g_qk_k_2"]])
    for n in ("w_in_2", "w_uq_2", "w_ukv_2", "w_mla_out_2", "w_ret_out_2", "w_mix_out_2", "g_ret_gn_2"):
        arrays[n if n == "w_in_2" else n[:-2]] = one[n]
    for n in ("w_router", "b_router", "final_norm_g"):
        arrays[n] = one[n]


def tables(np):
    f = np.float32
    t = np.arange(S)
    pos = np.stack([t // GRID, t % GRID], -1).astype(f)
    inv = (10000.0 ** (-np.arange(16, dtype=f) / 16)).astype(f)
    ang = (pos[:, :, None] * inv).reshape(T, P, 2, 16).transpose(1, 0, 2, 3)
    cq = np.arange(GRID)
    start = np.clip(cq - 8, 0, GRID - 16)
    inside = (cq[None, :] >= start[:, None]) & (cq[None, :] < start[:, None] + 16)
    near = np.where(inside, 0.0, NEG).astype(f)
    pos = np.zeros((P, T + 1), f)
    pos[:, :T] = META + np.arange(T)[None] * P + np.arange(P)[:, None]
    pos[:, T] = np.arange(P)

    def rope_table(half):
        inv = (10000.0 ** (-np.arange(half, dtype=f) / half)).astype(f)
        ang = pos[:, :, None] * inv
        return np.stack([np.cos(ang), np.sin(ang)], 1).astype(f)

    log_gamma = np.log(1.0 - 2.0 ** (-5.0 - np.arange(RH, dtype=f)))
    idx = np.arange(P, dtype=f)
    diff = idx[:, None] - idx[None, :]
    decay = np.where(diff[None] >= 0, np.exp(np.maximum(diff, 0.0)[None] * log_gamma[:, None, None]), 0.0)
    decay_t = decay.transpose(2, 0, 1).reshape(P, 4, 2, P).transpose(0, 2, 1, 3)
    zeta = np.exp((P - 1 - idx)[:, None] * log_gamma[None])
    xi = np.exp((idx + 1)[None] * log_gamma[:, None])
    by_half = np.arange(P) // RDK
    heads = 2 * np.arange(4)[None] + by_half[:, None]
    zeta_meta = np.concatenate([zeta[P - META:], np.zeros((P - META, RH))])
    causal = np.zeros((P, S), f)
    causal[:, S - P:] = np.where(idx[None] <= idx[:, None], 0.0, NEG)
    return {"k_rope_mla": rope_table(MROPE // 2), "k_rope_ret": rope_table(RDK // 2),
            "k_zeta": np.stack([zeta, zeta_meta], 1).astype(f), "k_decay": decay_t.astype(f),
            "k_xi": xi[heads].astype(f), "k_gamma": np.exp(P * log_gamma)[heads].astype(f), "k_causal": causal,
            "k_iota": np.broadcast_to(idx, (P, P)),
            "k_ident": np.eye(P, dtype=f), "k_spread_4": np.kron(np.eye(4, dtype=f), np.ones((1, 32), f)),
            "k_spread_2": np.kron(np.eye(2, dtype=f), np.ones((1, 64), f)), "k_first": np.stack([np.ones(P, f), np.zeros(P, f)]),
            "k_rope_tiny": np.stack([np.cos(ang), np.sin(ang)], 1).astype(f),
            "k_near_mask": np.concatenate([near, near])}
```
